# Optimizing a Trainium2 kernel written in Bass

```python
import jax, jax.numpy as jnp
from jax import lax
import numpy as np

D_MODEL = 1024
BATCH = 1
SEQ = 2048
DEPTH = 1

CTX_LEN = 256
GRID_W = 64
F32 = jnp.float32
EPS = 1e-6
N_MOD = 6
D_MIX = D_MODEL
D_LRU = D_MIX // 2
LRU_BLOCKS = 8
LRU_BLOCK_DIM = D_LRU // LRU_BLOCKS
CONV_W = 4
LRU_C = 8.0
D_RET = D_MIX - D_LRU
RET_HEADS = 4
RET_HEAD_DIM = D_RET // RET_HEADS
RET_CHUNK = 128
ROPE_BASE = 10000.0
N_EXPERTS = 64
TOP_K = 6
N_GROUPS = 8
TOP_GROUPS = 4
D_EXPERT = D_MODEL // 4
D_SHARED = D_EXPERT
ROUTE_SCALE = 2.5
MOE_BLOCK = 128

kernel_name = "hybrid_lru_retention_moe_dit_block"

def rmsnorm(x, g):
    x32 = x.astype(F32)
    y = x32 * lax.rsqrt(jnp.mean(x32 * x32, axis=-1, keepdims=True) + EPS)
    return (y * g.astype(F32)).astype(x.dtype)

def modulate(h, shift, scale):
    return h * (1.0 + scale) + shift

def swiglu(x, w_gate, w_up, w_down):
    return (jax.nn.silu(x @ w_gate) * (x @ w_up)) @ w_down

def dwconv(u, w, b):
    T = u.shape[1]
    left = CONV_W // 2
    up = jnp.pad(u, ((0, 0), (left, CONV_W - 1 - left), (0, 0)))
    return b + sum(w[j] * up[:, j:j + T] for j in range(CONV_W))

def _lin_combine(e1, e2):
    a1, b1 = e1
    a2, b2 = e2
    return a1 * a2, a2 * b1 + b2

def linear_scan(a, b, h0, reverse):
    if reverse:
        a, b = a[:, ::-1], b[:, ::-1]
    b = b.at[:, 0].add(a[:, 0] * h0)
    _, h = lax.associative_scan(_lin_combine, (a, b), axis=1)
    return h[:, ::-1] if reverse else h

def lru_gates(u, w_rec, b_rec, w_inp, b_inp, lam):
    B, T, _ = u.shape
    ub = u.reshape(B, T, LRU_BLOCKS, LRU_BLOCK_DIM)
    r = jax.nn.sigmoid(jnp.einsum('bthi,hij->bthj', ub, w_rec).reshape(B, T, D_LRU) + b_rec)
    i = jax.nn.sigmoid(jnp.einsum('bthi,hij->bthj', ub, w_inp).reshape(B, T, D_LRU) + b_inp)
    log_a = -LRU_C * r * jax.nn.softplus(-lam)
    return jnp.exp(log_a), jnp.sqrt(-jnp.expm1(2.0 * log_a)) * (i * u)

def lru_direction(u_lat, u_ctx, w_rec, b_rec, w_inp, b_inp, lam, reverse):
    w_rec, b_rec, w_inp, b_inp, lam = (p.astype(F32) for p in (w_rec, b_rec, w_inp, b_inp, lam))
    a_c, b_c = lru_gates(u_ctx, w_rec, b_rec, w_inp, b_inp, lam)
    h_ctx = linear_scan(a_c, b_c, jnp.zeros_like(b_c[:, 0]), reverse)
    h_end = h_ctx[:, 0] if reverse else h_ctx[:, -1]
    a_x, b_x = lru_gates(u_lat, w_rec, b_rec, w_inp, b_inp, lam)
    return linear_scan(a_x, b_x, h_end, reverse), h_ctx

def rope_1d(x, pos):
    half = x.shape[-1] // 2
    freqs = ROPE_BASE ** (-jnp.arange(half, dtype=F32) / half)
    ang = pos[:, None] * freqs[None, :]
    cos = jnp.cos(ang)[None, :, None, :]
    sin = jnp.sin(ang)[None, :, None, :]
    x1, x2 = x[..., :half], x[..., half:]
    return jnp.concatenate([x1 * cos - x2 * sin, x1 * sin + x2 * cos], axis=-1)

def rope_2d(x, row, col):
    h = x.shape[-1] // 2
    return jnp.concatenate([rope_1d(x[..., :h], row), rope_1d(x[..., h:], col)], axis=-1)

def head_rms(o):
    return o * lax.rsqrt(jnp.mean(o * o, axis=-1, keepdims=True) + EPS)

def retention_chunkwise(q, k, v, log_g, s0, inclusive):
    B, T, H, dk = q.shape
    dv = v.shape[-1]
    C = RET_CHUNK
    n = T // C
    qc = q.reshape(B, n, C, H, dk)
    kc = k.reshape(B, n, C, H, dk)
    vc = v.reshape(B, n, C, H, dv)
    idx = jnp.arange(C, dtype=F32)
    diff = idx[:, None] - idx[None, :]
    mask = (diff >= 0) if inclusive else (diff > 0)
    dmat = jnp.where(mask[None], jnp.exp(jnp.where(mask, diff, 0.0)[None] * log_g[:, None, None]), 0.0)
    scores = jnp.einsum('bnihd,bnjhd->bnhij', qc, kc) * dmat
    intra = jnp.einsum('bnhij,bnjhe->bnihe', scores, vc)
    zeta = jnp.exp((C - 1 - idx)[:, None] * log_g[None, :])
    xi = jnp.exp((idx + 1.0)[:, None] * log_g[None, :])
    chunk_kv = jnp.einsum('bnjhd,jh,bnjhe->nbhde', kc, zeta, vc)
    decay_chunk = jnp.exp(C * log_g)[None, :, None, None]

    def step(state, kv):
        return decay_chunk * state + kv, state

    _, s_prev = lax.scan(step, s0, chunk_kv)
    cross = jnp.einsum('bnihd,ih,nbhde->bnihe', qc, xi, s_prev)
    return (intra + cross).reshape(B, T, H, dv)

def context_states(k, v, log_g):
    L = k.shape[1]
    pos = jnp.arange(L, dtype=F32)
    wf = jnp.exp((L - 1 - pos)[:, None] * log_g[None, :])
    wb = jnp.exp(pos[:, None] * log_g[None, :])
    s_f = jnp.einsum('bmhd,mh,bmhe->bhde', k, wf, v)
    s_b = jnp.einsum('bmhd,mh,bmhe->bhde', k, wb, v)
    return s_f, s_b

def retention_context(q, k, v, log_g):
    L = q.shape[1]
    pos = jnp.arange(L, dtype=F32)
    dist = jnp.abs(pos[:, None] - pos[None, :])
    dmat = jnp.exp(dist[None] * log_g[:, None, None])
    scores = jnp.einsum('bnhd,bmhd->bhnm', q, k) * dmat
    return jnp.einsum('bhnm,bmhe->bnhe', scores, v)

def mixer(hx, hc, w_in, conv_w, conv_b, w_rec, b_rec, w_inp, b_inp, lam, w_out, row, col, log_g, need_ctx_out):
    B, T, _ = hx.shape
    L = hc.shape[1]
    xa, ga, q, k, v, g = jnp.split((hx @ w_in).astype(F32), 6, axis=-1)
    xa_c, ga_c, q_c, k_c, v_c, g_c = jnp.split((hc @ w_in).astype(F32), 6, axis=-1)
    cw, cb = conv_w.astype(F32), conv_b.astype(F32)
    u, u_c = dwconv(xa, cw, cb), dwconv(xa_c, cw, cb)
    h_f, hc_f = lru_direction(u, u_c, w_rec[0], b_rec[0], w_inp[0], b_inp[0], lam[0], False)
    h_b, hc_b = lru_direction(u, u_c, w_rec[1], b_rec[1], w_inp[1], b_inp[1], lam[1], True)
    y_lru = (h_f + h_b) * jax.nn.gelu(ga)
    scale = RET_HEAD_DIM ** -0.5
    qh = rope_2d(q.reshape(B, T, RET_HEADS, RET_HEAD_DIM), row, col)
    kh = rope_2d(k.reshape(B, T, RET_HEADS, RET_HEAD_DIM), row, col) * scale
    vh = v.reshape(B, T, RET_HEADS, RET_HEAD_DIM)
    kh_c = k_c.reshape(B, L, RET_HEADS, RET_HEAD_DIM) * scale
    vh_c = v_c.reshape(B, L, RET_HEADS, RET_HEAD_DIM)
    s_f, s_b = context_states(kh_c, vh_c, log_g)
    o = retention_chunkwise(qh, kh, vh, log_g, s_f, True) + \
        retention_chunkwise(qh[:, ::-1], kh[:, ::-1], vh[:, ::-1], log_g, s_b, False)[:, ::-1]
    y_ret = head_rms(o).reshape(B, T, D_RET) * jax.nn.silu(g)
    out = (jnp.concatenate([y_lru, y_ret], axis=-1) @ w_out.astype(F32)).astype(hx.dtype)
    if not need_ctx_out:
        return out, None
    qh_c = q_c.reshape(B, L, RET_HEADS, RET_HEAD_DIM)
    y_lru_c = (hc_f + hc_b) * jax.nn.gelu(ga_c)
    y_ret_c = head_rms(retention_context(qh_c, kh_c, vh_c, log_g)).reshape(B, L, D_RET) * jax.nn.silu(g_c)
    out_c = (jnp.concatenate([y_lru_c, y_ret_c], axis=-1) @ w_out.astype(F32)).astype(hc.dtype)
    return out, out_c

def routed_experts(x, eidx, gates, w1, w3, w2):
    N, D = x.shape
    NK = N * TOP_K
    e_flat = eidx.reshape(-1)
    tok_flat = jnp.repeat(jnp.arange(N, dtype=jnp.int32), TOP_K)
    g_flat = gates.reshape(-1)
    order = jnp.argsort(e_flat)
    e_sorted, tok_sorted, g_sorted = e_flat[order], tok_flat[order], g_flat[order]
    counts = jnp.bincount(e_flat, length=N_EXPERTS)
    starts = jnp.cumsum(counts) - counts
    padded = (counts + MOE_BLOCK - 1) // MOE_BLOCK * MOE_BLOCK
    pends = jnp.cumsum(padded)
    pstarts = pends - padded
    dest = pstarts[e_sorted] + jnp.arange(NK, dtype=jnp.int32) - starts[e_sorted]
    n_blocks = -(-NK // MOE_BLOCK) + N_EXPERTS
    P = n_blocks * MOE_BLOCK
    tok_buf = jnp.zeros((P,), jnp.int32).at[dest].set(tok_sorted)
    g_buf = jnp.zeros((P,), F32).at[dest].set(g_sorted)
    block_expert = jnp.clip(jnp.searchsorted(pends, jnp.arange(n_blocks) * MOE_BLOCK, side='right'), 0, N_EXPERTS - 1)

    def run_block(args):
        tok, gw, e = args
        return swiglu(x[tok], w1[e], w3[e], w2[e]).astype(F32) * gw[:, None]

    y = lax.map(run_block, (tok_buf.reshape(n_blocks, MOE_BLOCK), g_buf.reshape(n_blocks, MOE_BLOCK), block_expert))
    return jax.ops.segment_sum(y.reshape(P, D), tok_buf, num_segments=N)

def moe(h, w_router, b_router, w1, w3, w2, ws1, ws3, ws2):
    B, T, D = h.shape
    x = h.reshape(B * T, D)
    N = x.shape[0]
    s = jax.nn.sigmoid(x.astype(F32) @ w_router.astype(F32))
    sb = s + b_router.astype(F32)
    grp = sb.reshape(N, N_GROUPS, N_EXPERTS // N_GROUPS)
    gscore = lax.top_k(grp, 2)[0].sum(-1)
    _, gidx = lax.top_k(gscore, TOP_GROUPS)
    gmask = jnp.repeat(jax.nn.one_hot(gidx, N_GROUPS, dtype=F32).sum(1), N_EXPERTS // N_GROUPS, axis=1)
    _, eidx = lax.top_k(jnp.where(gmask > 0, sb, -jnp.inf), TOP_K)
    sel = jnp.take_along_axis(s, eidx, axis=1)
    gates = sel / jnp.sum(sel, axis=-1, keepdims=True) * ROUTE_SCALE
    routed = routed_experts(x, eidx, gates, w1, w3, w2)
    shared = swiglu(x, ws1, ws3, ws2).astype(F32)
    return (routed + shared).astype(h.dtype).reshape(B, T, D)

def setup_inputs(seed: int = 0) -> dict:
    key = jax.random.key(seed)
    ks = jax.random.split(key, 28)

    def nrm(k, shape, scale):
        return jax.random.normal(k, shape, F32) * scale

    u = jax.random.uniform(ks[15], (DEPTH, 2, D_LRU), F32, minval=0.9, maxval=0.999)
    s = u ** (1.0 / LRU_C)
    return {
        'x': nrm(ks[0], (BATCH, SEQ, D_MODEL), 1.0),
        'c': nrm(ks[1], (BATCH, D_MODEL), 1.0),
        'ctx': nrm(ks[2], (BATCH, CTX_LEN, D_MODEL), 1.0),
        'c_ctx': nrm(ks[3], (D_MODEL,), 1.0),
        'w_mod': nrm(ks[4], (DEPTH, D_MODEL, N_MOD * D_MODEL), D_MODEL ** -0.5),
        'b_mod': nrm(ks[5], (DEPTH, N_MOD * D_MODEL), 0.01),
        'norm_mix': 1.0 + nrm(ks[6], (DEPTH, D_MODEL), 0.01),
        'norm_ffn': 1.0 + nrm(ks[7], (DEPTH, D_MODEL), 0.01),
        'w_in': nrm(ks[8], (DEPTH, D_MODEL, 2 * D_LRU + 4 * D_RET), D_MODEL ** -0.5),
        'conv_w': nrm(ks[9], (DEPTH, CONV_W, D_LRU), CONV_W ** -0.5),
        'conv_b': nrm(ks[10], (DEPTH, D_LRU), 0.01),
        'lru_w_rec': nrm(ks[11], (DEPTH, 2, LRU_BLOCKS, LRU_BLOCK_DIM, LRU_BLOCK_DIM), LRU_BLOCK_DIM ** -0.5),
        'lru_b_rec': nrm(ks[12], (DEPTH, 2, D_LRU), 0.01),
        'lru_w_in': nrm(ks[13], (DEPTH, 2, LRU_BLOCKS, LRU_BLOCK_DIM, LRU_BLOCK_DIM), LRU_BLOCK_DIM ** -0.5),
        'lru_b_in': nrm(ks[14], (DEPTH, 2, D_LRU), 0.01),
        'lru_lambda': jnp.log(s) - jnp.log1p(-s),
        'w_out': nrm(ks[16], (DEPTH, D_MIX, D_MODEL), D_MIX ** -0.5),
        'w_router': nrm(ks[17], (DEPTH, D_MODEL, N_EXPERTS), D_MODEL ** -0.5),
        'b_router': nrm(ks[18], (DEPTH, N_EXPERTS), 0.01),
        'w_exp_gate': nrm(ks[19], (DEPTH, N_EXPERTS, D_MODEL, D_EXPERT), D_MODEL ** -0.5),
        'w_exp_up': nrm(ks[20], (DEPTH, N_EXPERTS, D_MODEL, D_EXPERT), D_MODEL ** -0.5),
        'w_exp_down': nrm(ks[21], (DEPTH, N_EXPERTS, D_EXPERT, D_MODEL), D_EXPERT ** -0.5),
        'w_sh_gate': nrm(ks[22], (DEPTH, D_MODEL, D_SHARED), D_MODEL ** -0.5),
        'w_sh_up': nrm(ks[23], (DEPTH, D_MODEL, D_SHARED), D_MODEL ** -0.5),
        'w_sh_down': nrm(ks[24], (DEPTH, D_SHARED, D_MODEL), D_SHARED ** -0.5),
        'norm_final': 1.0 + nrm(ks[25], (D_MODEL,), 0.01),
    }

def reference(x, c, ctx, c_ctx, w_mod, b_mod, norm_mix, norm_ffn, w_in, conv_w, conv_b, lru_w_rec, lru_b_rec, lru_w_in, lru_b_in, lru_lambda, w_out, w_router, b_router, w_exp_gate, w_exp_up, w_exp_down, w_sh_gate, w_sh_up, w_sh_down, norm_final):
    T = x.shape[1]
    rows = T // GRID_W
    row = jnp.repeat(jnp.arange(rows, dtype=F32), GRID_W)
    col = jnp.tile(jnp.arange(GRID_W, dtype=F32), rows)
    log_g = jnp.log1p(-jnp.exp2(-(5.0 + 2.0 * jnp.arange(RET_HEADS, dtype=F32))))
    for l in range(DEPTH):
        last = l == DEPTH - 1
        mod = jax.nn.silu(c) @ w_mod[l] + b_mod[l]
        sh1, sc1, g1, sh2, sc2, g2 = jnp.split(mod[:, None, :], N_MOD, axis=-1)
        mod_c = jax.nn.silu(c_ctx) @ w_mod[l] + b_mod[l]
        csh1, csc1, cg1, csh2, csc2, cg2 = jnp.split(mod_c, N_MOD, axis=-1)
        hx = modulate(rmsnorm(x, norm_mix[l]), sh1, sc1)
        hc = modulate(rmsnorm(ctx, norm_mix[l]), csh1, csc1)
        mx, mc = mixer(hx, hc, w_in[l], conv_w[l], conv_b[l], lru_w_rec[l], lru_b_rec[l], lru_w_in[l], lru_b_in[l], lru_lambda[l], w_out[l], row, col, log_g, not last)
        x = x + g1 * mx
        ffn_args = (w_router[l], b_router[l], w_exp_gate[l], w_exp_up[l], w_exp_down[l], w_sh_gate[l], w_sh_up[l], w_sh_down[l])
        x = x + g2 * moe(modulate(rmsnorm(x, norm_ffn[l]), sh2, sc2), *ffn_args)
        if not last:
            ctx = ctx + cg1 * mc
            ctx = ctx + cg2 * moe(modulate(rmsnorm(ctx, norm_ffn[l]), csh2, csc2), *ffn_args)
    return rmsnorm(x, norm_final)


_drawn_inputs = setup_inputs


def setup_inputs(seed=0):
    import zlib

    import numpy as np

    out = dict(_drawn_inputs(seed))
    spreads = {}
    factors = {'lru_b_rec': 6.16, 'lru_b_in': 4.414, 'norm_final': 5.312}
    for name, (base, spread) in spreads.items():
        noise = np.random.default_rng([zlib.crc32(name.encode()), seed]).standard_normal(out[name].shape)
        drawn = base * np.exp(spread * noise) if base else spread * noise
        out[name] = __import__('jax').numpy.asarray(drawn.astype(out[name].dtype))
    for name, factor in factors.items():
        out[name] = (out[name] * factor).astype(out[name].dtype)
    return out
```

```python
from contextlib import ExitStack

import numpy as np

import concourse.bass as bass
from concourse import mybir

F32 = mybir.dt.float32
F32R = mybir.dt.float32r
I32 = mybir.dt.int32
U32 = mybir.dt.uint32
ALU = mybir.AluOpType
ACT = mybir.ActivationFunctionType
AX = mybir.AxisListType

P = 128
D = 1024
KC = D // P
SEQ = 2048
CTX = 256
NT = SEQ // P
NC = CTX // P
GT = 4
NG = NT // GT
HEADS = 4
DH = 128
HD = HEADS * DH
D_LRU = 512
NCT = D_LRU // P
N_EXP = 64
TOP_K = 6
N_GROUPS = 8
TOP_GROUPS = 4
D_EXP = 256
EPS = 1e-6
ROUTE_SCALE = 2.5
NE = N_EXP + 1
LIST = SEQ
TAIL = 4
MAXB = NT + NT * TOP_K + N_EXP
ROWS = SEQ + P
PADX = CTX + 3
UW = PADX + SEQ


class Count:

    def __init__(self, eng, sem, base=0):
        self.eng, self.sem, self.base, self.n = eng, sem, base, 0

    def of(self, instruction, next_apart=False):
        self.n += 1
        instruction.then_inc(self.sem, 1)
        self.eng.wait_ge(self.sem, self.base + self.n)
        if next_apart:
            self.eng.nop(nofuse=True)


def wait_apart(eng, semaphore, value):
    if not isinstance(value, int) or value > 0:
        eng.wait_ge(semaphore, value)
        eng.nop(nofuse=True)


def clear(nc, semaphores):
    with nc.Block() as block:
        @block.gpsimd
        def _(pool):
            for s in semaphores:
                pool.sem_clear(s)


def modulation(nc, for_dma, io, mod_d, h2_d, sum_d, list_d):
    NB, RING = 12, 4
    with ExitStack() as ctx:
        def sb(name, shape, dt=F32):
            return ctx.enter_context(nc.sbuf_tensor(name, shape, dt))

        def sem(name):
            return ctx.enter_context(nc.semaphore(name))

        def dma_sem(name):
            return for_dma.enter_context(nc.semaphore(name))

        cond = sb("cond", [P, KC, 2])
        cond_t = sb("cond_t", [P, KC, 2])
        cond_s = sb("cond_s", [P, KC, 2])
        wm = sb("wm", [P, RING, KC, 512])
        bm = sb("bm", [2, NB * 512])
        mod = sb("mod", [2, NB * 512])
        fill = sb("fill", [P, LIST * N_EXP // P, 2], U32)
        fill_s = sb("fill_shared", [P, LIST // P, 2], U32)
        zero = sb("zero_rows", [P, D])
        ps = ctx.enter_context(nc.psum_tensor("ps_mod", [P, 2, 512], F32))
        c_loaded, b_loaded = dma_sem("c_loaded"), dma_sem("b_loaded")
        wm_loaded = [dma_sem(f"wm_loaded{s}") for s in range(RING)]
        tanh_done, silu_own, silu_done = sem("tanh_done"), sem("silu_own"), sem("silu_done")
        mm_done, mod_done, stored = sem("mm_done"), sem("mod_done"), dma_sem("mod_stored")
        fill_set, filled = sem("fill_set"), dma_sem("filled")
        block = ctx.enter_context(nc.Block())

        @block.sync
        def _(sp):
            sp.dma_start(cond[:], io["cond"]).then_inc(c_loaded, 16)
            sp.dma_start(bm[:], io["b_mod"]).then_inc(b_loaded, 16)
            for s in range(RING):
                sp.dma_start(wm[:, s].rearrange("p k n -> p (k n)"), io["w_mod"][s]).then_inc(wm_loaded[s], 16)
            with sp.Fori(1, NB // RING) as r:
                for s in range(RING):
                    sp.wait_ge(mm_done, (r - 1) * RING + s + 1)
                    src = io["w_mod"][bass.ds(r * RING + s, 1)].rearrange("a p n -> (a p) n")
                    sp.dma_start(wm[:, s].rearrange("p k n -> p (k n)"), src).then_inc(wm_loaded[s], 16)
            sp.wait_ge(mod_done, NB)
            sp.dma_start(mod_d, mod[:]).then_inc(stored, 16)
            sp.wait_ge(stored, 16)

        @block.gpsimd
        def _(pool):
            pool.memset(fill[:].rearrange("p r c -> p (r c)"), 0).then_inc(fill_set, 1)
            pool.memset(fill_s[:, :, 1].bitcast(F32), 1.0).then_inc(fill_set, 1)
            pool.memset(zero[:], 0.0).then_inc(fill_set, 1)
            pool.wait_ge(fill_set, 3)
            pool.iota(fill[:, :, 0].rearrange("p (a b) -> p a b", b=P), [[0, LIST * N_EXP // P // P], [1, P]], base=SEQ,
                      channel_multiplier=0).then_inc(fill_set, 1)
            pool.iota(fill_s[:, :, 0], [[1, LIST // P]], base=0, channel_multiplier=LIST // P).then_inc(fill_set, 1)
            pool.wait_ge(fill_set, 5)
            pool.dma_start(list_d[LIST:LIST * NE].rearrange("(p r) c -> p (r c)", p=P),
                           fill[:].rearrange("p r c -> p (r c)")).then_inc(filled, 16)
            pool.dma_start(list_d[0:LIST].rearrange("(p r) c -> p (r c)", p=P),
                           fill_s[:].rearrange("p r c -> p (r c)")).then_inc(filled, 16)
            pool.dma_start(list_d[LIST * NE:LIST * NE + TAIL * P].rearrange("(a r) c -> a (r c)", a=TAIL),
                           fill[0:TAIL, 0:P].rearrange("p r c -> p (r c)")).then_inc(filled, 16)
            pool.dma_start(h2_d[SEQ:ROWS], zero[:]).then_inc(filled, 16)
            pool.dma_start(sum_d[SEQ:ROWS], zero[:]).then_inc(filled, 16)
            pool.wait_ge(filled, 16 * 5)

        @block.scalar
        def _(act):
            act.wait_ge(c_loaded, 16)
            act.activation(cond_t[:], cond[:], ACT.Tanh, scale=0.5).then_inc(tanh_done, 1)

        @block.tensor
        def _(pe):
            pe.wait_ge(silu_done, 1)
            with pe.Fori(0, NB // RING) as r:
                for s in range(RING):
                    pe.wait_ge(wm_loaded[s], (r + 1) * 16)
                    pe.wait_ge(mod_done, r * RING + max(s - 1, 0))
                    for k in range(KC):
                        last = pe.matmul(ps[0:2, s % 2], cond_s[:, k], wm[:, s, k],
                                         start=(k == 0), stop=(k == KC - 1))
                    last.then_inc(mm_done, 1)

        @block.vector
        def _(dve):
            own = Count(dve, silu_own)
            dve.wait_ge(tanh_done, 1)
            own.of(dve.scalar_tensor_tensor(cond_s[:], cond_t[:], 1.0, cond[:], ALU.add, ALU.mult))
            dve.tensor_scalar(cond_s[:], cond_s[:], 0.5, None, ALU.mult).then_inc(silu_done, 1)
            dve.wait_ge(b_loaded, 16)
            with dve.Fori(0, NB // 2) as r:
                for s in range(2):
                    dve.wait_ge(mm_done, r * 2 + s + 1)
                    cols = bass.ds((r * 2 + s) * 512, 512)
                    dve.tensor_tensor(mod[:, cols], ps[0:2, s], bm[:, cols], ALU.add).then_inc(mod_done, 1)


def project(nc, for_dma, io, mod_d, hx_d, xa_t, ga_t, ident):
    with ExitStack() as ctx:
        def sb(name, shape, dt=F32):
            return ctx.enter_context(nc.sbuf_tensor(name, shape, dt))

        def sem(name):
            return ctx.enter_context(nc.semaphore(name))

        def dma_sem(name):
            return for_dma.enter_context(nc.semaphore(name))

        wa = sb("wa", [P, KC, 2 * D_LRU])
        xt = sb("xt", [P, 2, GT, D])
        junk = sb("sq_out", [P, 2, D])
        hx = sb("hx", [P, 2, KC, GT * P])
        ssq = sb("ssq", [P, NC + NT])
        rstd = sb("rstd", [P, NC + NT])
        mhalf = sb("mhalf", [P, 1])
        shift = sb("shift", [P, 2, KC])
        scale = sb("scale", [P, 2, KC])
        gain = sb("gain", [P, KC])
        ps_t = ctx.enter_context(nc.psum_tensor("ps_t", [P, 4, 512], F32))
        ps_p = ctx.enter_context(nc.psum_tensor("ps_p", [P, 4, 512], F32))
        w_loaded, m_loaded = dma_sem("wa_loaded"), dma_sem("m_loaded")
        x_loaded = [[dma_sem(f"x_loaded{p}{j}") for j in range(GT)] for p in range(2)]
        sq_done, half_set, rstd_own, rstd_done = sem("sq_done"), sem("half_set"), sem("rstd_own"), sem("rstd_done")
        z_done, t_done = sem("z_done"), sem("t_done")
        ev_act, ev_dve = sem("ev_act"), sem("ev_dve")
        p_done, xa_done, ga_done = sem("p_done"), sem("xa_done"), sem("ga_done")
        hx_stored = [dma_sem("hx_stored0"), dma_sem("hx_stored1")]
        scale_own, pads_set = sem("scale_own"), sem("pads_set")
        block = ctx.enter_context(nc.Block())

        first_tile = [0] + [NC + i * GT for i in range(NG)]
        tiles = [NC] + [GT] * NG
        n_groups = NG + 1
        p_before = [0] + [NCT + i * 2 * NCT for i in range(NG)]

        def loads(i, j):
            return sum(1 for h in range(i % 2, i + 1, 2) if j < tiles[h])

        def stores(i):
            return sum(tiles[h] for h in range(i % 2, i, 2))

        @block.sync
        def _(sp):
            sp.dma_start(gain[:], io["gain_mix"]).then_inc(m_loaded, 16)
            for s in range(2):
                for n, t in ((0, shift), (1, scale)):
                    src = mod_d[s, n * D:(n + 1) * D].rearrange("(k p) -> p k", p=P)
                    sp.dma_start(t[:, s], src, allow_slow_non_contiguous=True).then_inc(m_loaded, 16)
            for k in range(KC):
                sp.dma_start(wa[:, k], io["w_a"][:, k]).then_inc(w_loaded, 16)

            for i in range(n_groups):
                sp.wait_ge(ev_act, (i + 1) * (KC // 2))
                sp.wait_ge(ev_dve, (i + 1) * (KC // 2))
                for j in range(tiles[i]):
                    dst = hx_d[first_tile[i] + j].rearrange("p (k t) -> p k t", k=KC)
                    sp.dma_start(dst, hx[:, i % 2, :, j * P:(j + 1) * P]).then_inc(hx_stored[i % 2], 16)
            for b in range(2):
                sp.wait_ge(hx_stored[b], 16 * sum(tiles[b::2]))

        @block.gpsimd
        def _(pool):
            pool.memset(mhalf[:], -0.5).then_inc(half_set, 1)
            for c in range(NCT):
                for a, b in ((0, 2), (2 + CTX, 2 + PADX), (2 + UW, 3 + UW)):
                    pool.memset(xa_t[:, c, a:b], 0.0).then_inc(pads_set, 1)
            pool.wait_ge(half_set, 1)

            def load(i):
                if i >= 2:
                    pool.wait_ge(t_done, (i - 1) * KC)
                for j in range(tiles[i]):
                    pool.dma_start(xt[:, i % 2, j], io["xt"][first_tile[i] + j]).then_inc(x_loaded[i % 2][j], 16)

            load(0)
            load(1)
            for i in range(n_groups):
                for t in range(first_tile[i], first_tile[i] + tiles[i]):
                    col = slice(t, t + 1)
                    pool.wait_ge(sq_done, t + 1)
                    pool.tensor_scalar(rstd[:, col], ssq[:, col], 1.0 / D, EPS, ALU.mult, ALU.add).then_inc(rstd_own, 1)
                    pool.wait_ge(rstd_own, t + 1)
                    pool.tensor_tensor(rstd[:, col], rstd[:, col], mhalf[:], ALU.pow).then_inc(rstd_done, 1)
                if i + 2 < n_groups:
                    load(i + 2)

        @block.scalar
        def _(act):
            act.wait_ge(scale_own, 2)

            def squares(i):
                for j in range(tiles[i]):
                    t = first_tile[i] + j
                    act.wait_ge(x_loaded[i % 2][j], loads(i, j) * 16)
                    if t >= 2:
                        act.wait_ge(sq_done, t - 1)
                    act.activation(junk[:, t % 2], xt[:, i % 2, j], ACT.Square, accum_out=ssq[:, t:t + 1]).then_inc(sq_done, 1)

            squares(0)
            for i in range(n_groups):
                w = tiles[i] * P
                s = 1 if i == 0 else 0
                if i >= 2:
                    act.wait_ge(hx_stored[i % 2], stores(i) * 16)
                for k in range(0, KC, 2):
                    act.wait_ge(t_done, i * KC + k + 1)
                    act.activation(hx[:, i % 2, k, 0:w], ps_t[:, k % 4, 0:w], ACT.Identity,
                                   bias=shift[:, s, k:k + 1], scale=scale[:, s, k:k + 1]).then_inc(ev_act, 1)
                if i + 1 < n_groups:
                    squares(i + 1)
                if i >= 1:
                    for c in range(NCT):
                        act.wait_ge(p_done, p_before[i] + NCT + c + 1)
                        act.activation(ga_t[:, c, (i - 1) * GT * P:i * GT * P], ps_p[:, c],
                                       ACT.Gelu_apprx_tanh).then_inc(ga_done, 1)

        @block.vector
        def _(dve):
            dve.wait_ge(m_loaded, 5 * 16)
            for s in range(2):
                dve.scalar_tensor_tensor(scale[:, s], scale[:, s], 1.0, gain[:], ALU.add, ALU.mult).then_inc(scale_own, 1)
            dve.wait_ge(scale_own, 2)

            def normed(i):
                for j in range(tiles[i]):
                    t = first_tile[i] + j
                    dve.wait_ge(rstd_done, t + 1)
                    dve.tensor_scalar(xt[:, i % 2, j], xt[:, i % 2, j], rstd[:, t:t + 1], None, ALU.mult).then_inc(z_done, 1)

            normed(0)
            for i in range(n_groups):
                w = tiles[i] * P
                s = 1 if i == 0 else 0
                if i >= 2:
                    dve.wait_ge(hx_stored[i % 2], stores(i) * 16)
                for k in range(1, KC, 2):
                    dve.wait_ge(t_done, i * KC + k + 1)
                    dve.tensor_scalar(hx[:, i % 2, k, 0:w], ps_t[:, k % 4, 0:w], scale[:, s, k:k + 1],
                                      shift[:, s, k:k + 1], ALU.mult, ALU.add).then_inc(ev_dve, 1)
                if i + 1 < n_groups:
                    normed(i + 1)
                to = 2 if i == 0 else 2 + PADX + (i - 1) * GT * P
                for c in range(NCT):
                    dve.wait_ge(p_done, p_before[i] + c + 1)
                    dve.tensor_copy(xa_t[:, c, to:to + w], ps_p[:, c, 0:w]).then_inc(xa_done, 1)

        @block.tensor
        def _(pe):
            for i in range(n_groups):
                w = tiles[i] * P
                pe.wait_ge(z_done, first_tile[i] + tiles[i])
                for k in range(KC):
                    if i >= 1 or k >= 4:
                        pe.wait_ge(ev_act if k % 2 == 0 else ev_dve, i * (KC // 2) + (k - 4) // 2 + 1)
                    for j in range(tiles[i]):
                        last = pe.transpose(ps_t[:, k % 4, j * P:(j + 1) * P], xt[:, i % 2, j, k * P:(k + 1) * P], ident[:])
                    last.then_inc(t_done, 1)
                if i == 0:
                    pe.wait_ge(w_loaded, 16 * KC)
                pe.wait_ge(ev_act, (i + 1) * (KC // 2))
                pe.wait_ge(ev_dve, (i + 1) * (KC // 2))
                for c in range(NCT if i == 0 else 2 * NCT):
                    if c >= NCT:
                        pe.wait_ge(xa_done, i * NCT + c - NCT + 1)
                    elif i == 1:
                        pe.wait_ge(xa_done, c + 1)
                    elif i >= 2:
                        pe.wait_ge(ga_done, (i - 2) * NCT + c + 1)
                    for k in range(KC):
                        last = pe.matmul(ps_p[:, c % 4, 0:w], wa[:, k, c * P:(c + 1) * P], hx[:, i % 2, k, 0:w],
                                         start=(k == 0), stop=(k == KC - 1))
                    last.then_inc(p_done, 1)
def lru(nc, for_dma, io, xa_t, ga_t, yl_d):
    SEG = [(a, min(a + 512, UW)) for a in range(0, UW, 512)]
    NS = len(SEG)
    LOG_TERMS = 9
    with ExitStack() as ctx:
        def sb(name, shape, dt=F32):
            return ctx.enter_context(nc.sbuf_tensor(name, shape, dt))

        def sem(name):
            return ctx.enter_context(nc.semaphore(name))

        def dma_sem(name):
            return for_dma.enter_context(nc.semaphore(name))

        wg = sb("w_gates", [P, NCT, 2, 2, P])
        small = sb("lru_small", [P, NCT * 15])
        taps = small[:, 0:NCT * 4].rearrange("p (c j) -> p c j", j=4)
        cbias = small[:, NCT * 4:NCT * 5]
        gbias = small[:, NCT * 5:NCT * 9].rearrange("p (c d g) -> p c d g", d=2, g=2)
        lam = small[:, NCT * 9:NCT * 11]
        hbias = sb("half_bias", [P, NCT, 2, 2])
        lw = sb("lam_work", [P, 5, NCT * 2])
        ch = sb("decay_half", [P, NCT * 2])
        u = sb("u", [P, 2, UW])
        tr = sb("tanh_r", [P, 2, UW])
        ti = sb("tanh_i", [P, 2, UW])
        a = sb("decay", [P, 2, UW])
        tl = sb("tanh_l", [P, 2, UW])
        h = sb("states", [P, 2, UW])
        ps = ctx.enter_context(nc.psum_tensor("ps_gate", [P, 8, 512], F32))
        g_loaded, s_loaded = dma_sem("g_loaded"), dma_sem("s_loaded")
        exp_lam, ch_own, ch_done, hb_done = sem("exp_lam"), sem("ch_own"), sem("ch_done"), sem("hb_done")
        u_done, u_own, gates_done, tanh_done = sem("u_done"), sem("u_own"), sem("gates_done"), sem("gate_tanh_done")
        a_done, tl_done, sq_done, s2_done, beta_done = sem("a_done"), sem("tl_done"), sem("a2_done"), sem("s2_done"), sem("beta_done")
        ib_done, b_done, scan_own, scan_done = sem("ib_done"), sem("b_done"), sem("scan_own"), sem("scan_done")
        sum_done, y_done, y_stored = sem("sum_done"), sem("y_done"), dma_sem("y_stored")
        block = ctx.enter_context(nc.Block())

        @block.sync
        def _(sp):
            sp.dma_start(small[:, 0:NCT * 11], io["lru_small"]).then_inc(s_loaded, 16)
            sp.dma_start(wg[:].rearrange("p c d g n -> p (c d g n)"), io["lru_gates"]).then_inc(g_loaded, 16)
            for c in range(NCT):
                sp.wait_ge(y_done, c + 1)
                dst = yl_d.rearrange("m p (c t) -> c p m t", c=NCT)[c]
                sp.dma_start(dst, ga_t[:, c].rearrange("p (m t) -> p m t", t=P)).then_inc(y_stored, 16)
            sp.wait_ge(y_stored, 16 * NCT)

        @block.tensor
        def _(pe):
            pe.wait_ge(g_loaded, 16)
            for c in range(NCT):
                for d in range(2):
                    if d == 0:
                        pe.wait_ge(u_done, c + 1)
                    for s, (lo, hi) in enumerate(SEG):
                        for g in range(2):
                            n = ((c * 2 + d) * NS + s) * 2 + g
                            if n >= 8:
                                pe.wait_ge(tanh_done, n - 7)
                            pe.matmul(ps[:, n % 8, 0:hi - lo], wg[:, c, d, g], u[:, c % 2, lo:hi],
                                      start=True, stop=True).then_inc(gates_done, 1)

        @block.scalar
        def _(act):
            act.wait_ge(s_loaded, 16)
            act.activation(lw[:, 0], lam, ACT.Abs).then_inc(exp_lam, 1)
            act.wait_ge(exp_lam, 1)
            act.activation(lw[:, 1], lw[:, 0], ACT.Exp, scale=-1.0).then_inc(exp_lam, 1)
            act.wait_ge(hb_done, 1)
            act.wait_ge(ch_done, 1)
            for c in range(NCT):
                for d in range(2):
                    i = c * 2 + d
                    for s, (lo, hi) in enumerate(SEG):
                        for g, dst in enumerate((tr, ti)):
                            n = (i * NS + s) * 2 + g
                            if s == 0 and i >= 2:
                                act.wait_ge(scan_done if g else s2_done, i - 1)
                            act.wait_ge(gates_done, n + 1)
                            act.activation(dst[:, d, lo:hi], ps[:, n % 8, 0:hi - lo], ACT.Tanh,
                                           bias=hbias[:, c, d, g:g + 1], scale=0.5).then_inc(tanh_done, 1)
                    act.wait_ge(tanh_done, (i + 1) * NS * 2)
                    if i >= 2:
                        act.wait_ge(scan_done, (i - 1))
                        act.wait_ge(b_done, i - 1)
                    k = ch[:, i:i + 1]
                    act.activation(a[:, d], tr[:, d], ACT.Exp, bias=k, scale=k).then_inc(a_done, 1)
                    act.activation(tl[:, d], tr[:, d], ACT.Tanh, bias=k, scale=k).then_inc(tl_done, 1)
                    act.wait_ge(a_done, i + 1)
                    act.wait_ge(tl_done, i + 1)
                    act.activation(tr[:, d], a[:, d], ACT.Square).then_inc(sq_done, 1)
                for d in range(2):
                    i = c * 2 + d
                    act.wait_ge(s2_done, i + 1)
                    act.activation(tl[:, d], tl[:, d], ACT.Sqrt, scale=-0.25).then_inc(beta_done, 1)

        @block.gpsimd
        def _(pool):
            for c in range(NCT):
                for d in range(2):
                    i = c * 2 + d
                    pool.wait_ge(beta_done, i + 1)
                    pool.wait_ge(ib_done, i + 1)
                    pool.tensor_tensor(ti[:, d], ti[:, d], tl[:, d], ALU.mult).then_inc(b_done, 1)

        @block.vector
        def _(dve):
            dve.wait_ge(s_loaded, 16)
            dve.tensor_scalar(hbias[:].rearrange("p c d g -> p (c d g)"), gbias.rearrange("p c d g -> p (c d g)"),
                              0.5, None, ALU.mult).then_inc(hb_done, 1)
            own = Count(dve, ch_own)
            dve.wait_ge(exp_lam, 2)
            z, s, s2, t = lw[:, 1], lw[:, 2], lw[:, 3], lw[:, 4]
            own.of(dve.tensor_scalar(s, z, 2.0, None, ALU.add))
            own.of(dve.reciprocal(s, s))
            own.of(dve.tensor_tensor(s, s, z, ALU.mult))
            own.of(dve.tensor_tensor(s2, s, s, ALU.mult))
            own.of(dve.memset(t, 1.0 / (2 * LOG_TERMS - 1)))
            for k in range(LOG_TERMS - 2, -1, -1):
                own.of(dve.tensor_tensor(t, t, s2, ALU.mult))
                own.of(dve.tensor_scalar(t, t, 1.0 / (2 * k + 1), None, ALU.add))
            own.of(dve.scalar_tensor_tensor(t, t, 2.0, s, ALU.mult, ALU.mult))
            own.of(dve.tensor_scalar(s, lam, -1.0, 0.0, ALU.mult, ALU.max))
            own.of(dve.tensor_tensor(t, t, s, ALU.add))
            dve.tensor_scalar(ch[:], t, -4.0, None, ALU.mult).then_inc(ch_done, 1)
            conv = Count(dve, u_own)

            def convolve(c):
                b = c % 2
                if c >= 2:
                    dve.wait_ge(gates_done, (c - 1) * 4 * NS)
                    dve.wait_ge(ib_done, (c - 1) * 2)
                conv.of(dve.tensor_scalar(u[:, b], xa_t[:, c, 0:UW], taps[:, c, 0:1], cbias[:, c:c + 1],
                                          ALU.mult, ALU.add))
                for j in range(1, 4):
                    step = dve.scalar_tensor_tensor(u[:, b], xa_t[:, c, j:j + UW], taps[:, c, j:j + 1], u[:, b],
                                                    ALU.mult, ALU.add)
                    if j < 3:
                        conv.of(step)
                    else:
                        step.then_inc(u_done, 1)
                dve.wait_ge(u_done, c + 1)

            convolve(0)
            scans = Count(dve, scan_own)
            for c in range(NCT):
                for d in range(2):
                    i = c * 2 + d
                    dve.wait_ge(sq_done, i + 1)
                    dve.scalar_tensor_tensor(tl[:, d], tr[:, d], 1.0, tl[:, d], ALU.add, ALU.mult).then_inc(s2_done, 1)
                    dve.scalar_tensor_tensor(ti[:, d], ti[:, d], 1.0, u[:, c % 2], ALU.add, ALU.mult).then_inc(ib_done, 1)
                if c + 1 < NCT:
                    convolve(c + 1)
                lat, con = slice(PADX, UW), slice(0, CTX)
                dve.wait_ge(b_done, c * 2 + 1)
                if c >= 1:
                    dve.wait_ge(y_done, c)
                scans.of(dve.tensor_tensor_scan(h[:, 0, con], a[:, 0, con], ti[:, 0, con], 0.0, ALU.mult, ALU.add))
                dve.tensor_tensor_scan(h[:, 0, lat], a[:, 0, lat], ti[:, 0, lat], h[:, 0, CTX - 1:CTX],
                                       ALU.mult, ALU.add).then_inc(scan_done, 1)
                dve.wait_ge(b_done, c * 2 + 2)
                scans.of(dve.tensor_tensor_scan(h[:, 1, 0:CTX][:, ::-1], a[:, 1, 0:CTX][:, ::-1], ti[:, 1, 0:CTX][:, ::-1],
                                                0.0, ALU.mult, ALU.add))
                dve.tensor_tensor_scan(h[:, 1, lat][:, ::-1], a[:, 1, lat][:, ::-1], ti[:, 1, lat][:, ::-1], h[:, 1, 0:1],
                                       ALU.mult, ALU.add).then_inc(scan_done, 1)
                dve.wait_ge(scan_done, c * 2 + 2)
                dve.tensor_tensor(h[:, 0, lat], h[:, 0, lat], h[:, 1, lat], ALU.add).then_inc(sum_done, 1)
                dve.wait_ge(sum_done, c + 1)
                dve.tensor_tensor(ga_t[:, c], h[:, 0, lat], ga_t[:, c], ALU.mult).then_inc(y_done, 1)


def rotate(dve, own, out, tmp, src, table):
    heads = [P, HEADS, DH]
    src4 = src.rearrange("p (h a s i) -> p h a s i", h=HEADS, a=2, s=2)
    tmp4 = tmp.rearrange("p (h a s i) -> p h a s i", h=HEADS, a=2, s=2)
    own.of(dve.tensor_tensor(out.rearrange("p (h e) -> p h e", h=HEADS), src.rearrange("p (h e) -> p h e", h=HEADS),
                             table[:, None, 0:DH].broadcast_to(heads), ALU.mult))
    sines = table[:, DH:2 * DH].rearrange("p (a s i) -> p a s i", a=2, s=2)
    for s in range(2):
        own.of(dve.tensor_tensor(tmp4[:, :, :, s], src4[:, :, :, 1 - s],
                                 sines[:, None, :, s].broadcast_to([P, HEADS, 2, DH // 4]), ALU.mult))
    return dve.tensor_tensor(out, out, tmp, ALU.add)


def keys(nc, for_dma, io, hx_d, rec_d, sf, ident):
    NU = NC + NT
    KT, V, KVF, SB = (slice(i * HD, (i + 1) * HD) for i in range(4))
    with ExitStack() as ctx:
        def sb(name, shape, dt=F32):
            return ctx.enter_context(nc.sbuf_tensor(name, shape, dt))

        def sem(name):
            return ctx.enter_context(nc.semaphore(name))

        def dma_sem(name):
            return for_dma.enter_context(nc.semaphore(name))

        w = sb("w_kv_s", [P, KC, 2 * HD])
        hx = sb("hx_kv", [P, 2, KC, P])
        rope = sb("rope_kv", [P, 2, 2 * DH])
        kr = sb("kr", [P, 2, HD])
        tmp = sb("rot_kv", [P, HD])
        rec = sb("rec", [P, 2, 4 * HD])
        vfb = sb("vfb", [P, 2, HEADS, 2, DH])
        sbd = sb("sb_decayed", [P, HD])
        zeta = sb("zeta_s", [P, 2 * HEADS])
        gc = sb("gc_s", [P, HEADS])
        ps_k = ctx.enter_context(nc.psum_tensor("ps_k", [P, 2, 512], F32))
        ps_v = ctx.enter_context(nc.psum_tensor("ps_v", [P, 2, 512], F32))
        ps_t = ctx.enter_context(nc.psum_tensor("ps_kt", [P, 512], F32))
        ps_kv = ctx.enter_context(nc.psum_tensor("ps_kv", [P, 2, 512], F32))
        c_loaded, w_loaded = dma_sem("kv_c_loaded"), dma_sem("kv_w_loaded")
        hx_loaded = [dma_sem("hxk_loaded0"), dma_sem("hxk_loaded1")]
        rope_loaded = [dma_sem("rok_loaded0"), dma_sem("rok_loaded1")]
        k_done, v_done, rot_own, kr_done = sem("k_done"), sem("v_done"), sem("rotk_own"), sem("kr_done")
        v_copied, vfb_done, kt_done, kt_copied = sem("v_copied"), sem("vfb_done"), sem("kt_done"), sem("kt_copied")
        kv_done, kvf_done, sbd_done, state_done = sem("kv_done"), sem("kvf_done"), sem("sbd_done"), sem("state_done")
        zeroed = sem("sb_zeroed")
        rec_stored = [dma_sem("rec_stored0"), dma_sem("rec_stored1")]
        block = ctx.enter_context(nc.Block())

        def loop(eng, step):
            with eng.Fori(0, NT // 2) as r:
                step(r * 2 + 2, 0, r)
                step(r * 2 + 3, 1, r)

        @block.sync
        def _(sp):
            sp.dma_start(zeta[:], io["zeta"]).then_inc(c_loaded, 16)
            sp.dma_start(gc[:], io["gc"]).then_inc(c_loaded, 16)
            for n in range(2):
                sp.dma_start(hx[:, n].rearrange("p k t -> p (k t)"), hx_d[1 - n]).then_inc(hx_loaded[n], 16)
            for k in range(KC):
                sp.dma_start(w[:, k], io["w_kv"][:, k]).then_inc(w_loaded, 16)

            def step(n, par, r):
                sp.wait_ge(v_done, n - 1)
                tile = r * -2 + (NT - 1 - par)
                src = hx_d[bass.ds(tile + NC, 1)].rearrange("a p n -> (a p) n")
                sp.dma_start(hx[:, par].rearrange("p k t -> p (k t)"), src).then_inc(hx_loaded[par], 16)
                sp.wait_ge(kr_done, n - 1)
                src = io["rope"][bass.ds(tile, 1)].rearrange("a p n -> (a p) n")
                sp.dma_start(rope[:, par], src).then_inc(rope_loaded[par], 16)
            loop(sp, step)

        @block.gpsimd
        def _(pool):
            pool.memset(rec[:, 0, SB], 0.0).then_inc(zeroed, 1)
            pool.wait_ge(c_loaded, 32)
            pool.wait_ge(zeroed, 1)
            heads = [P, HEADS, DH]

            def scaled(n, par):
                if not isinstance(n, int):
                    pool.wait_ge(kv_done, n - 1)
                pool.wait_ge(v_copied, n + 1)
                v = rec[:, par, V].rearrange("p (h e) -> p h e", h=HEADS)
                for f in range(2):
                    z = zeta[:, f * HEADS:(f + 1) * HEADS]
                    pool.tensor_tensor(vfb[:, par, :, f], v, z[:, :, None].broadcast_to(heads), ALU.mult).then_inc(vfb_done, 1)
                if not (isinstance(n, int) and n == 0):
                    pool.wait_ge(state_done, n)
                pool.tensor_tensor(sbd[:].rearrange("p (h e) -> p h e", h=HEADS),
                                   rec[:, par, SB].rearrange("p (h e) -> p h e", h=HEADS),
                                   gc[:, :, None].broadcast_to(heads), ALU.mult).then_inc(sbd_done, 1)

            def store(n, par, r):
                pool.wait_ge(v_copied, n + 1)
                pool.wait_ge(kt_copied, n - 1)
                pool.wait_ge(kvf_done, n + 1)
                tile = r * -2 + (NT - 1 - par)
                dst = rec_d[bass.ds(tile, 1)].rearrange("a p n -> (a p) n")
                pool.dma_start(dst, rec[:, par]).then_inc(rec_stored[par], 16)
            scaled(0, 0)
            scaled(1, 1)

            def step(n, par, r):
                scaled(n, par)
                store(n, par, r)
            loop(pool, step)
            for b in range(2):
                pool.wait_ge(rec_stored[b], 16 * (NT // 2))

        @block.scalar
        def _(act):
            def step(n, par, r):
                if r is not None:
                    act.wait_ge(rec_stored[par], r * 16)
                act.wait_ge(v_done, n + 1)
                act.activation(rec[:, par, V], ps_v[:, par], ACT.Copy).then_inc(v_copied, 1)
                if r is not None:
                    act.wait_ge(kt_done, n - 1)
                    act.activation(rec[:, par, KT], ps_t[:], ACT.Copy).then_inc(kt_copied, 1)
            step(0, 0, None)
            step(1, 1, None)
            loop(act, step)

        @block.vector
        def _(dve):
            heads = [P, HEADS, DH]
            rotations = Count(dve, rot_own)

            def to_sbuf(n, par, r):
                dve.wait_ge(k_done, n + 1)
                if r is None:
                    dve.tensor_copy(kr[:, par], ps_k[:, par]).then_inc(kr_done, 1)
                else:
                    dve.wait_ge(rope_loaded[par], (r + 1) * 16)
                    dve.wait_ge(kv_done, n - 1)
                    rotations.base, rotations.n = r * 6 + par * 3, 0
                    rotate(dve, rotations, kr[:, par], tmp[:], ps_k[:, par], rope[:, par]).then_inc(kr_done, 1)
                    dve.wait_ge(kr_done, n + 1)

            def states(n, par, r):
                dve.wait_ge(kv_done, n + 1)
                kv = ps_kv[:].rearrange("p b (h f e) -> p (b h) f e", f=2, e=DH)
                if r is not None:
                    dve.wait_ge(rec_stored[par], r * 16)
                    dve.tensor_copy(rec[:, par, KVF].rearrange("p (h e) -> p h e", h=HEADS), kv[:, :, 0]).then_inc(kvf_done, 1)
                    dve.wait_ge(rec_stored[1 - par], (r + par) * 16)
                elif n == 0:
                    dve.tensor_copy(sf[:].rearrange("p (h e) -> p h e", h=HEADS), kv[:, :, 0]).then_inc(kvf_done, 1)
                else:
                    dve.wait_ge(c_loaded, 32)
                    dve.wait_ge(kvf_done, 1)
                    dve.tensor_tensor(tmp[:].rearrange("p (h e) -> p h e", h=HEADS), kv[:, :, 0],
                                      gc[:, :, None].broadcast_to(heads), ALU.mult).then_inc(kvf_done, 1)
                dve.wait_ge(sbd_done, n + 1)
                dve.tensor_tensor(rec[:, 1 - par, SB].rearrange("p (h e) -> p h e", h=HEADS), kv[:, :, 1],
                                  sbd[:].rearrange("p (h e) -> p h e", h=HEADS), ALU.add).then_inc(state_done, 1)
            for n in range(NC):
                to_sbuf(n, n, None)
                states(n, n, None)
            dve.wait_ge(kvf_done, 2)
            dve.tensor_tensor(sf[:], sf[:], tmp[:], ALU.add).then_inc(zeroed, 1)
            dve.wait_ge(zeroed, 2)

            def step(n, par, r):
                to_sbuf(n, par, r)
                states(n, par, r)
            loop(dve, step)

        @block.tensor
        def _(pe):
            def project_kv(n, par, r):
                pe.wait_ge(hx_loaded[par], (r + 2 if r is not None else 1) * 16)
                if r is not None:
                    pe.wait_ge(kr_done, n - 1)
                for k in range(KC):
                    last = pe.matmul(ps_k[:, par], hx[:, par, k], w[:, k, 0:HD], start=(k == 0), stop=(k == KC - 1))
                last.then_inc(k_done, 1)
                if r is not None:
                    pe.wait_ge(v_copied, n - 1)
                for k in range(KC):
                    last = pe.matmul(ps_v[:, par], hx[:, par, k], w[:, k, HD:2 * HD], start=(k == 0), stop=(k == KC - 1))
                last.then_inc(v_done, 1)

            def chunk_kv(n, par, latent):
                pe.wait_ge(kr_done, n + 1)
                if latent:
                    if not isinstance(n, int) or n > NC:
                        pe.wait_ge(kt_copied, n - NC)
                    for h in range(HEADS):
                        last = pe.transpose(ps_t[:, h * DH:(h + 1) * DH], kr[:, par, h * DH:(h + 1) * DH], ident[:])
                    last.then_inc(kt_done, 1)
                pe.wait_ge(vfb_done, (n + 1) * 2)
                if not (isinstance(n, int) and n == 0):
                    pe.wait_ge(state_done, n)
                for h in range(HEADS):
                    last = pe.matmul(ps_kv[:, h // 2, (h % 2) * 2 * DH:(h % 2 + 1) * 2 * DH],
                                     kr[:, par, h * DH:(h + 1) * DH], vfb[:, par, h], start=True, stop=True)
                last.then_inc(kv_done, 1)
            pe.wait_ge(w_loaded, 16 * KC)
            for n in range(NC):
                project_kv(n, n, None)
                chunk_kv(n, n, False)
            project_kv(NC, 0, 0)
            with pe.Fori(0, NT // 2 - 1) as r:
                project_kv(r * 2 + 3, 1, r)
                chunk_kv(r * 2 + 2, 0, True)
                project_kv(r * 2 + 4, 0, r + 1)
                chunk_kv(r * 2 + 3, 1, True)
            project_kv(NU - 1, 1, NT // 2 - 1)
            chunk_kv(NU - 2, 0, True)
            chunk_kv(NU - 1, 1, True)


def mixer_out(nc, for_dma, io, mod_d, hx_d, rec_d, yl_d, h2_d, sum_d, list_d, sf, ident, blocks_row, ends_row):
    with ExitStack() as ctx:
        def sb(name, shape, dt=F32):
            return ctx.enter_context(nc.sbuf_tensor(name, shape, dt))

        def sem(name):
            return ctx.enter_context(nc.semaphore(name))

        def dma_sem(name):
            return for_dma.enter_context(nc.semaphore(name))

        wqg = sb("w_qg_s", [P, KC, 2 * HD])
        wo = sb("w_out_s", [P, KC, D])
        wr = sb("w_router_s", [P, KC, N_EXP])
        dmat = sb("dmat_s", [P, HD])
        xi = sb("xi_s", [P, 2, HD])
        gc = sb("gc_m", [P, HEADS])
        g1 = sb("g1_row", [P, D])
        a2 = sb("a2_row", [P, D])
        b2 = sb("b2_row", [P, D])
        br = sb("b_router_s", [P, N_EXP])
        order = sb("order_s", [P, 2, P])
        iota = sb("iota_s", [P, N_EXP])
        kcol = sb("kcol_s", [P, 2])
        token = sb("token_s", [P, NT], U32)
        carry = sb("carry", [P, N_EXP])
        mhalf = sb("mhalf_m", [P, 1])
        hx = sb("hx_q", [P, 2, KC, P])
        rope = sb("rope_q", [P, 2, 2 * DH])
        rec = sb("rec_m", [P, 2, 4 * HD])
        x = sb("x_m", [P, 2, D])
        yl = sb("yl_m", [P, 2, NCT, P])
        qr = sb("qr", [P, 2, HD])
        tmp = sb("rot_q", [P, HD])
        tg = sb("tanh_g", [P, HD])
        sg = sb("silu_g", [P, 2, HD])
        q_t = sb("q_t", [P, HD])
        qf_t = sb("qf_t", [P, HD])
        qb_t = sb("qb_t", [P, HD])
        at = sb("scores_t", [P, HD])
        sfs = sb("sf_m", [P, 2, HD])
        sfd = sb("sf_decayed", [P, HD])
        sq_o = sb("sq_out_o", [P, HEADS, DH])
        ms = sb("ms", [P, HEADS])
        rh = sb("rh", [P, HEADS])
        y = sb("y_ret", [P, HD])
        y_t = sb("y_ret_t", [P, HD])
        x1 = sb("x1", [P, 2, D])
        sq_x = sb("sq_out_x", [P, D])
        gain = sq_x
        ssq = sb("ssq_m", [P, 2])
        rstd = sb("rstd_m", [P, 2])
        h2 = sb("h2", [P, 2, D])
        h2_t = sb("h2_t", [P, KC, P])
        th = sb("tanh_s", [P, N_EXP])
        s = sb("s_r", [P, N_EXP])
        sbias = sb("s_biased", [P, N_EXP])
        gt = sb("group_top", [P, N_GROUPS, 8])
        gs = sb("group_score", [P, N_GROUPS])
        m8 = sb("max8", [P, 8])
        i8 = sb("index8", [P, 8], U32)
        f8 = sb("index8_f", [P, 8])
        eq4 = sb("eq4", [P, N_GROUPS, TOP_GROUPS])
        gm = sb("group_mask", [P, N_GROUPS])
        gb = sb("group_low", [P, N_GROUPS])
        eq6 = sb("eq6", [P, 2, TOP_K, N_EXP])
        prod = sb("prod6", [P, TOP_K, N_EXP])
        chosen = sb("chosen", [P, N_EXP])
        sel = sb("sel", [P, TOP_K])
        ssum = sb("sel_sum", [P, 1])
        slot = sb("slot_f", [P, TOP_K])
        slot64 = sb("slot64", [P, N_EXP])
        slot_u = sb("slot_u", [P, 2, TOP_K], U32)
        entry = sb("entry", [P, 2, TOP_K, 2], U32)
        nt = sb("nt", [P, NE])
        nti = sb("nt_i", [P, N_EXP], I32)
        end = sb("end", [P, NE])
        ones = sb("ones65", [P, NE])
        cmp = sb("cmp", [P, 2, NE])
        cmpn = sb("cmp_nt", [P, 2, NE])
        bcol = sb("block_cols", [P, 2, 2])
        scol = sb("start_cols", [P, 2])

        ps_q = ctx.enter_context(nc.psum_tensor("ps_q", [P, 512], F32))
        ps_g = ctx.enter_context(nc.psum_tensor("ps_g", [P, 512], F32))
        ps_s = ctx.enter_context(nc.psum_tensor("ps_s", [P, 512], F32))
        ps_o = ctx.enter_context(nc.psum_tensor("ps_o", [P, 512], F32))
        ps_u = ctx.enter_context(nc.psum_tensor("ps_u", [P, 2, 512], F32))
        ps_t = ctx.enter_context(nc.psum_tensor("ps_tr", [P, 2, 512], F32))

        c_loaded, wqg_loaded, wo_loaded = dma_sem("m_c_loaded"), dma_sem("wqg_loaded"), dma_sem("wo_loaded")
        hx_loaded = [dma_sem("hxq_loaded0"), dma_sem("hxq_loaded1")]
        rec_loaded = [dma_sem("rec_loaded0"), dma_sem("rec_loaded1")]
        x_loaded = [dma_sem("xm_loaded0"), dma_sem("xm_loaded1")]
        (q_done, g_done, rot_own, qr_done, tg_done, sg_done, qt_done, qt_copied, qf_done, qb_done, s_done, at_done,
         o_done, sfd_done, sf_done, sqo_done, rh_own, rh_done, y_own, y_done, yt_done, yt_copied, u0_done, u1_done,
         x1m_done, x1_done, sqx_done, rstd_own, rstd_done, h2s_done, h2_done, ht_done, ht_copied, r_done, th_done,
         top_own, chosen_done, listed_ids, rank_done, slot_own, slot_done, entry_done, carry_done) = (
            sem(n) for n in "q_done g_done rotq_own qr_done tg_done sg_done qt_done qt_copied qf_done qb_done "
            "s_done at_done o_done sfd_done sf_done sqo_done rh_own rh_done y_own y_done yt_done yt_copied u0_done "
            "u1_done x1m_done x1_done sqx_done rstdm_own rstdm_done h2s_done h2_done ht_done ht_copied r_done "
            "th_done top_own chosen_done listed_ids rank_done slot_own slot_done entry_done carry_done".split())
        consts_set, a2_done = sem("consts_set"), sem("a2_done")
        h2_stored = [dma_sem("h2_stored0"), dma_sem("h2_stored1")]
        x1_stored = [dma_sem("x1_stored0"), dma_sem("x1_stored1")]
        listed = [dma_sem("listed0"), dma_sem("listed1")]
        tab_own, bcol_done, brow_done, rows_done = sem("tab_own"), sem("bcol_done"), sem("brow_done"), sem("rows_done")
        N_CONST = 14
        block = ctx.enter_context(nc.Block())

        def iterations(eng, step):
            for n in range(-1, 3):
                step(n, n % 2)
            with eng.Fori(0, (NT - 4) // 2) as r:
                step(r * 2 + 3, 1)
                step(r * 2 + 4, 0)
            for n in range(NT - 1, NT + 3):
                step(n, n % 2)

        def on(n, lag):
            return not isinstance(n, int) or 0 <= n - lag < NT

        def wait(eng, semaphore, value):
            if not isinstance(value, int) or value > 0:
                eng.wait_ge(semaphore, value)

        def half(n, par):
            return (n - par) // 2

        def row(t):
            return bass.ds(t, 1)

        @block.sync
        def _(sp):
            for dst, src in ((dmat[:], io["dmat"]), (xi[:].rearrange("p d n -> p (d n)"), io["xi"]), (gc[:], io["gc"]),
                             (order[:].rearrange("p d n -> p (d n)"), io["order"]), (iota[:], io["iota"]),
                             (kcol[:], io["kcol"]), (token[:], io["token"]), (carry[:], io["list_base"]),
                             (wr[:].rearrange("p k n -> p (k n)"), io["w_router"]),
                             (br[:], io["b_router"].broadcast_to([P, N_EXP])),
                             (g1[:], mod_d[0:1, 2 * D:3 * D].broadcast_to([P, D])),
                             (b2[:], mod_d[0:1, 3 * D:4 * D].broadcast_to([P, D])),
                             (a2[:], mod_d[0:1, 4 * D:5 * D].broadcast_to([P, D])),
                             (gain[:], io["gain_ffn"].broadcast_to([P, D]))):
                sp.dma_start(dst, src).then_inc(c_loaded, 16)

            def loads(n, par):
                if on(n, -2):
                    wait(sp, g_done, n + 1)
                    src = hx_d[row(n + 2 + NC)].rearrange("a p n -> (a p) n")
                    sp.dma_start(hx[:, par].rearrange("p k t -> p (k t)"), src).then_inc(hx_loaded[par], 16)
                    wait(sp, qr_done, n + 1)
                    src = io["rope"][row(n + 2)].rearrange("a p n -> (a p) n")
                    sp.dma_start(rope[:, par], src).then_inc(hx_loaded[par], 16)
                if on(n, -1):
                    wait(sp, o_done, n)
                    if not isinstance(n, int) or n >= 1:
                        sp.wait_ge(sf_done, n + 1)
                    src = rec_d[row(n + 1)].rearrange("a p n -> (a p) n")
                    sp.dma_start(rec[:, 1 - par], src).then_inc(rec_loaded[1 - par], 16)
                    wait(sp, x1_done, n)
                    wait(sp, u1_done, n)
                    src = io["xt"][row(n + 1 + NC)].rearrange("a p n -> (a p) n")
                    sp.dma_start(x[:, 1 - par], src).then_inc(x_loaded[1 - par], 16)
                    src = yl_d[row(n + 1)].rearrange("a p n -> (a p) n")
                    sp.dma_start(yl[:, 1 - par].rearrange("p c t -> p (c t)"), src).then_inc(x_loaded[1 - par], 16)
            for k in range(KC):
                sp.dma_start(wqg[:, k], io["w_qg"][:, k]).then_inc(wqg_loaded, 16)
            for n in (-2, -1):
                loads(n, n % 2)
            for k in range(KC):
                sp.dma_start(wo[:, k], io["w_out"][:, k]).then_inc(wo_loaded, 16)
            for n in range(0, 3):
                loads(n, n % 2)
            with sp.Fori(0, (NT - 6) // 2) as r:
                loads(r * 2 + 3, 1)
                loads(r * 2 + 4, 0)
            for n in (NT - 3, NT - 2):
                loads(n, n % 2)

        @block.gpsimd
        def _(pool):
            pool.memset(mhalf[:], -0.5).then_inc(consts_set, 1)
            pool.memset(ones[:], 1.0).then_inc(consts_set, 1)
            pool.wait_ge(c_loaded, 16 * N_CONST)
            pool.wait_ge(consts_set, 2)

            def step(n, par):
                if on(n, 0):
                    pool.wait_ge(qt_copied, n + 1)
                    wait(pool, o_done, n)
                    pool.tensor_tensor(qb_t[:], q_t[:], xi[:, 1], ALU.mult).then_inc(qb_done, 1)
                    wait(pool, sf_done, n + 1)
                    pool.tensor_tensor(sfd[:].rearrange("p (h e) -> p h e", h=HEADS),
                                       sfs[:, par].rearrange("p (h e) -> p h e", h=HEADS),
                                       gc[:, :, None].broadcast_to([P, HEADS, DH]), ALU.mult).then_inc(sfd_done, 1)
                if on(n, 3):
                    t = n - 3
                    pool.wait_ge(entry_done, t + 1)
                    pool.tensor_copy(entry[:, 1 - par, :, 0], token[:, row(t)].broadcast_to([P, TOP_K])).then_inc(listed_ids, 1)
                    pool.wait_ge(listed_ids, t + 1)
                    wait_apart(pool, slot_done, t + 1)
                    for j in range(TOP_K):
                        pool.indirect_dma_start(
                            list_d[:, :], bass.IndirectOffsetOnAxis(slot_u[:, 1 - par, j:j + 1], 0),
                            entry[:, 1 - par, j], None).then_inc(listed[1 - par], 16)
                if on(n, 0):
                    wait(pool, y_done, n)
                    wait_apart(pool, sqo_done, (n + 1) * HEADS)
                    pool.tensor_scalar(rh[:], ms[:], 4.0 / DH, 4.0 * EPS, ALU.mult, ALU.add).then_inc(rh_own, 1)
                    pool.wait_ge(rh_own, n + 1)
                    pool.tensor_tensor(rh[:], rh[:], mhalf[:].broadcast_to([P, HEADS]), ALU.pow).then_inc(rh_done, 1)
                if on(n, 1):
                    t, b = n - 1, 1 - par
                    pool.wait_ge(x_loaded[b], (half(t, b) + 1) * 32)
                    pool.wait_ge(x1m_done, (t + 1) * 2)
                    pool.tensor_tensor(x1[:, b], x1[:, b], x[:, b], ALU.add).then_inc(x1_done, 1)
                    pool.wait_ge(x1_done, t + 1)
                    pool.dma_start(sum_d[bass.ds(t * P, P)], x1[:, b]).then_inc(x1_stored[b], 16)
                    wait(pool, h2s_done, t - 1)
                    wait_apart(pool, sqx_done, t + 1)
                    pool.tensor_scalar(rstd[:, b:b + 1], ssq[:, b:b + 1], 1.0 / D, EPS, ALU.mult, ALU.add).then_inc(rstd_own, 1)
                    pool.wait_ge(rstd_own, t + 1)
                    pool.tensor_tensor(rstd[:, b:b + 1], rstd[:, b:b + 1], mhalf[:], ALU.pow).then_inc(rstd_done, 1)
                    pool.wait_ge(h2s_done, t + 1)
                    pool.tensor_tensor(h2[:, b], h2[:, b], b2[:], ALU.add).then_inc(h2_done, 1)
                    wait_apart(pool, h2_done, t + 1)
                    pool.dma_start(h2_d[bass.ds(t * P, P)], h2[:, b]).then_inc(h2_stored[b], 16)
            iterations(pool, step)
            for b in range(2):
                pool.wait_ge(h2_stored[b], 16 * NT // 2)
                pool.wait_ge(x1_stored[b], 16 * NT // 2)
                pool.wait_ge(listed[b], 16 * TOP_K * NT // 2)

        @block.scalar
        def _(act):
            act.wait_ge(a2_done, 1)

            def step(n, par):
                if on(n, 0):
                    act.wait_ge(qt_done, n + 1)
                    wait(act, o_done, n)
                    wait(act, qf_done, n)
                    wait(act, qb_done, n)
                    act.activation(q_t[:], ps_t[:, 0], ACT.Copy).then_inc(qt_copied, 1)
                if on(n, 1):
                    act.wait_ge(yt_done, n)
                    wait(act, u1_done, n - 1)
                    act.activation(y_t[:], ps_t[:, 1], ACT.Copy).then_inc(yt_copied, 1)
                if on(n, -1):
                    act.wait_ge(g_done, n + 2)
                    wait(act, sg_done, n + 1)
                    act.activation(tg[:], ps_g[:], ACT.Tanh, scale=0.5).then_inc(tg_done, 1)
                if on(n, 0):
                    act.wait_ge(o_done, n + 1)
                    wait(act, rh_done, n)
                    wait(act, sqo_done, n * HEADS)
                    for h in range(HEADS):
                        act.activation(sq_o[:, h], ps_o[:, h * DH:(h + 1) * DH], ACT.Square,
                                       accum_out=ms[:, h:h + 1]).then_inc(sqo_done, 1)
                if on(n, 2):
                    for b in range(2):
                        act.wait_ge(ht_done, (n - 2) * 2 + b + 1)
                        wait(act, r_done, n - 2)
                        act.activation(h2_t[:, b * 4:(b + 1) * 4].rearrange("p k t -> p (k t)"), ps_t[:, b],
                                       ACT.Copy).then_inc(ht_copied, 1)
                    act.wait_ge(r_done, n - 1)
                    wait(act, entry_done, n - 2)
                    act.activation(th[:], ps_s[:, 0:N_EXP], ACT.Tanh, scale=0.5).then_inc(th_done, 1)
                if on(n, 1):
                    act.wait_ge(x1_done, n)
                    wait(act, sqx_done, n - 1)
                    wait(act, rstd_done, n - 2)
                    act.activation(sq_x[:], x1[:, 1 - par], ACT.Square, accum_out=ssq[:, 1 - par:2 - par]).then_inc(sqx_done, 1)
            iterations(act, step)

        @block.vector
        def _(dve):
            dve.wait_ge(c_loaded, 16 * N_CONST)
            dve.scalar_tensor_tensor(a2[:], a2[:], 1.0, gain[:], ALU.add, ALU.mult).then_inc(a2_done, 1)
            dve.wait_ge(a2_done, 1)
            dve.tensor_copy(sfs[:, 0], sf[:]).then_inc(sf_done, 1)
            rotations, tops, ys, slots = Count(dve, rot_own), Count(dve, top_own), Count(dve, y_own), Count(dve, slot_own)
            N_TOP = 21

            def step(n, par):
                if on(n, 0):
                    dve.wait_ge(qt_copied, n + 1)
                    wait(dve, o_done, n)
                    dve.tensor_tensor(qf_t[:], q_t[:], xi[:, 0], ALU.mult).then_inc(qf_done, 1)
                if on(n, 3):
                    t, b = n - 3, 1 - par
                    slots.base, slots.n = t * 3, 0
                    dve.wait_ge(rank_done, t + 1)
                    slots.of(dve.tensor_tensor(slot64[:], ps_t[:, 1, 0:N_EXP], carry[:], ALU.add))
                    dve.tensor_tensor(carry[:], ps_t[:, 1, N_EXP:2 * N_EXP], carry[:], ALU.add).then_inc(carry_done, 1)
                    dve.wait_ge(carry_done, t + 1)
                    slots.of(dve.tensor_tensor(prod[:], eq6[:, b], slot64[:, None, :].broadcast_to([P, TOP_K, N_EXP]), ALU.mult))
                    slots.of(dve.tensor_reduce(slot[:], prod[:], AX.X, ALU.add))
                    wait(dve, listed[b], half(t, b) * 16 * TOP_K)
                    dve.tensor_copy(slot_u[:, b], slot[:]).then_inc(slot_done, 1)
                if on(n, -1):
                    dve.wait_ge(q_done, n + 2)
                    dve.wait_ge(hx_loaded[1 - par], (half(n + 1, 1 - par) + 1) * 32)
                    rotations.base, rotations.n = (n + 1) * 3, 0
                    wait(dve, qt_done, n)
                    rotate(dve, rotations, qr[:, 1 - par], tmp[:], ps_q[:], rope[:, 1 - par]).then_inc(qr_done, 1)
                if on(n, 0):
                    dve.wait_ge(s_done, n + 1)
                    dve.tensor_tensor(at[:], ps_s[:], dmat[:], ALU.mult).then_inc(at_done, 1)
                if on(n, -1):
                    dve.wait_ge(tg_done, n + 2)
                    wait(dve, y_done, n)
                    dve.scalar_tensor_tensor(sg[:, 1 - par], tg[:], 1.0, ps_g[:], ALU.add, ALU.mult).then_inc(sg_done, 1)
                if on(n, 0):
                    dve.wait_ge(sfd_done, n + 1)
                    dve.wait_ge(rec_loaded[par], (half(n, par) + 1) * 16)
                    wait(dve, o_done, n)
                    dve.tensor_tensor(sfs[:, 1 - par], sfd[:], rec[:, par, 2 * HD:3 * HD], ALU.add).then_inc(sf_done, 1)
                    dve.wait_ge(rh_done, n + 1)
                    wait(dve, yt_done, n)
                    for h in range(HEADS):
                        e = slice(h * DH, (h + 1) * DH)
                        last = dve.scalar_tensor_tensor(y[:, e], ps_o[:, e], rh[:, h:h + 1], sg[:, par, e], ALU.mult, ALU.mult)
                    last.then_inc(y_done, 1)
                if on(n, 1):
                    t, b = n - 1, 1 - par
                    wait(dve, x1_stored[b], half(t, b) * 16)
                    wait(dve, sqx_done, t - 1)
                    wait(dve, h2s_done, t - 1)
                    for i, u_done in enumerate((u0_done, u1_done)):
                        c = slice(i * 512, (i + 1) * 512)
                        dve.wait_ge(u_done, t + 1)
                        dve.tensor_tensor(x1[:, b, c], ps_u[:, i], g1[:, c], ALU.mult).then_inc(x1m_done, 1)
                if on(n, 2):
                    top(n - 2, par)
                if on(n, 1):
                    t, b = n - 1, 1 - par
                    dve.wait_ge(rstd_done, t + 1)
                    wait(dve, h2_stored[b], half(t, b) * 16)
                    wait(dve, ht_done, (t - 1) * 2)
                    dve.scalar_tensor_tensor(h2[:, b], x1[:, b], rstd[:, b:b + 1], a2[:], ALU.mult, ALU.mult).then_inc(h2s_done, 1)

            def top(t, b):
                tops.base, tops.n = t * N_TOP, 0
                dve.wait_ge(th_done, t + 1)
                tops.of(dve.tensor_scalar(s[:], th[:], 0.5, 0.5, ALU.mult, ALU.add))
                tops.of(dve.tensor_tensor(sbias[:], s[:], br[:], ALU.add), next_apart=True)
                for g in range(N_GROUPS):
                    last = dve.max(gt[:, g], sbias[:, g * 8:(g + 1) * 8])
                tops.of(last)
                tops.of(dve.tensor_tensor(gs[:], gt[:, :, 0], gt[:, :, 1], ALU.add), next_apart=True)
                tops.of(dve.max(m8[:], gs[:]), next_apart=True)
                tops.of(dve.max_index(i8[:], m8[:], gs[:]))
                tops.of(dve.tensor_copy(f8[:], i8[:]))
                tops.of(dve.tensor_tensor(eq4[:], iota[:, 0:N_GROUPS, None].broadcast_to([P, N_GROUPS, TOP_GROUPS]),
                                          f8[:, None, 0:TOP_GROUPS].broadcast_to([P, N_GROUPS, TOP_GROUPS]), ALU.is_equal))
                tops.of(dve.tensor_reduce(gm[:], eq4[:], AX.X, ALU.add))
                tops.of(dve.tensor_scalar(gb[:], gm[:], -1.0, 1e30, ALU.add, ALU.mult))
                by_group = sbias[:].rearrange("p (g e) -> p g e", g=N_GROUPS)
                wide = [P, N_GROUPS, N_EXP // N_GROUPS]
                tops.of(dve.tensor_tensor(by_group, by_group, gm[:, :, None].broadcast_to(wide), ALU.mult))
                tops.of(dve.tensor_tensor(by_group, by_group, gb[:, :, None].broadcast_to(wide), ALU.add), next_apart=True)
                tops.of(dve.max(m8[:], sbias[:]), next_apart=True)
                tops.of(dve.max_index(i8[:], m8[:], sbias[:]))
                tops.of(dve.tensor_copy(f8[:], i8[:]))
                each = [P, TOP_K, N_EXP]
                tops.of(dve.tensor_tensor(eq6[:, b], iota[:, None, :].broadcast_to(each),
                                          f8[:, 0:TOP_K, None].broadcast_to(each), ALU.is_equal))
                wait(dve, rank_done, t)
                dve.tensor_reduce(chosen[:], eq6[:, b].rearrange("p j e -> p e j"), AX.X, ALU.add).then_inc(chosen_done, 1)
                tops.of(dve.tensor_tensor(prod[:], eq6[:, b], s[:, None, :].broadcast_to(each), ALU.mult))
                tops.of(dve.tensor_reduce(sel[:], prod[:], AX.X, ALU.add))
                tops.of(dve.tensor_reduce(ssum[:], sel[:], AX.X, ALU.add))
                tops.of(dve.reciprocal(ssum[:], ssum[:]))
                tops.of(dve.tensor_scalar(sel[:], sel[:], ssum[:], ROUTE_SCALE, ALU.mult, ALU.mult))
                wait(dve, listed[b], half(t, b) * 16 * TOP_K)
                dve.tensor_copy(entry[:, b, :, 1].bitcast(F32), sel[:]).then_inc(entry_done, 1)
                assert tops.n == N_TOP
            iterations(dve, step)

            own = Count(dve, tab_own)
            dve.wait_ge(carry_done, NT)
            dve.wait_ge(consts_set, 2)
            own.of(dve.scalar_tensor_tensor(nt[:, 1:NE], iota[:], -float(LIST), carry[:], ALU.mult, ALU.add))
            own.of(dve.tensor_scalar(nti[:], nt[:, 1:NE], float(P - 1 - LIST), None, ALU.add))
            own.of(dve.tensor_scalar(nti[:], nti[:], 7, None, ALU.arith_shift_right))
            own.of(dve.tensor_copy(nt[:, 1:NE], nti[:]))
            own.of(dve.tensor_scalar(nt[:, 1:NE], nt[:, 1:NE], 1.0, None, ALU.max))
            own.of(dve.memset(nt[:, 0:1], float(NT)))
            own.of(dve.tensor_tensor_scan(end[:], ones[:], nt[:], 0.0, ALU.mult, ALU.add))
            for c in range(2):
                own.of(dve.tensor_scalar(cmp[:, c], end[:], kcol[:, c:c + 1], None, ALU.is_le))
                own.of(dve.tensor_tensor(cmpn[:, c], cmp[:, c], nt[:], ALU.mult))
                own.of(dve.tensor_reduce(bcol[:, c, 0:1], cmp[:, c], AX.X, ALU.add))
                own.of(dve.tensor_reduce(scol[:, c:c + 1], cmpn[:, c], AX.X, ALU.add))
                own.of(dve.tensor_tensor(scol[:, c:c + 1], kcol[:, c:c + 1], scol[:, c:c + 1], ALU.subtract))
                own.of(dve.scalar_tensor_tensor(bcol[:, c, 1:2], bcol[:, c, 0:1], float(LIST // P), scol[:, c:c + 1],
                                                ALU.mult, ALU.add))
                dve.tensor_scalar(bcol[:, c, 0:1], bcol[:, c, 0:1], float(NE - 1), None, ALU.min).then_inc(bcol_done, 1)
            dve.tensor_copy(ends_row[:, 0:NE], end[0:1, :]).then_inc(rows_done, 1)
            dve.tensor_scalar(ends_row[:, NE:NE + 1], end[0:1, NE - 1:NE], float(-NT), None, ALU.add).then_inc(rows_done, 1)
            dve.wait_ge(brow_done, 1)
            dve.tensor_copy(blocks_row[:].rearrange("p w (c k) -> p c w k", c=2),
                            ps_s[0:1, :].rearrange("p (c w k) -> p c w k", c=2, w=2)).then_inc(rows_done, 1)

        @block.tensor
        def _(pe):
            def products(out, lhs, rhs, free, done):
                for k in range(KC):
                    last = pe.matmul(out, lhs(k), rhs(k), start=(k == 0), stop=(k == KC - 1))
                last.then_inc(done, 1)

            pe.wait_ge(wqg_loaded, 16 * KC)
            pe.wait_ge(c_loaded, 16 * N_CONST)

            def step(n, par):
                q = 1 - par
                if on(n, 0):
                    pe.wait_ge(qr_done, n + 1)
                    wait(pe, ht_copied, (n - 2) * 2 - 1)
                    for h in range(HEADS):
                        last = pe.transpose(ps_t[:, 0, h * DH:(h + 1) * DH], qr[:, par, h * DH:(h + 1) * DH], ident[:])
                    last.then_inc(qt_done, 1)
                if on(n, 3):
                    pe.wait_ge(chosen_done, n - 2)
                    pe.wait_ge(ht_copied, min(n - 2, NT) * 2 if isinstance(n, int) else (n - 2) * 2)
                    for i in range(2):
                        last = pe.matmul(ps_t[:, 1, i * N_EXP:(i + 1) * N_EXP], order[:, i], chosen[:], start=True, stop=True)
                    last.then_inc(rank_done, 1)
                if on(n, -1):
                    pe.wait_ge(hx_loaded[q], (half(n + 1, q) + 1) * 32)
                    wait(pe, qr_done, n + 1)
                    products(ps_q[:], lambda k: hx[:, q, k], lambda k: wqg[:, k, 0:HD], None, q_done)
                if on(n, 0):
                    pe.wait_ge(qt_copied, n + 1)
                    pe.wait_ge(rec_loaded[par], (half(n, par) + 1) * 16)
                    wait(pe, th_done, n - 2)
                    for h in range(HEADS):
                        e = slice(h * DH, (h + 1) * DH)
                        last = pe.matmul(ps_s[:, e], rec[:, par, e], q_t[:, e], start=True, stop=True)
                    last.then_inc(s_done, 1)
                if on(n, 1):
                    pe.wait_ge(y_done, n)
                    wait(pe, carry_done, n - 2)
                    for h in range(HEADS):
                        last = pe.transpose(ps_t[:, 1, h * DH:(h + 1) * DH], y[:, h * DH:(h + 1) * DH], ident[:])
                    last.then_inc(yt_done, 1)
                if on(n, -1):
                    wait(pe, sg_done, n + 1)
                    products(ps_g[:], lambda k: hx[:, q, k], lambda k: wqg[:, k, HD:2 * HD], None, g_done)
                if on(n, 0):
                    pe.wait_ge(at_done, n + 1)
                    pe.wait_ge(qf_done, n + 1)
                    pe.wait_ge(qb_done, n + 1)
                    pe.wait_ge(sf_done, n + 1)
                    wait(pe, y_done, n)
                    for h in range(HEADS):
                        e = slice(h * DH, (h + 1) * DH)
                        pe.matmul(ps_o[:, e], at[:, e], rec[:, par, HD + h * DH:HD + (h + 1) * DH], start=True, stop=False)
                        pe.matmul(ps_o[:, e], qf_t[:, e], sfs[:, par, e], start=False, stop=False)
                        last = pe.matmul(ps_o[:, e], qb_t[:, e], rec[:, par, 3 * HD + h * DH:3 * HD + (h + 1) * DH],
                                         start=False, stop=True)
                    last.then_inc(o_done, 1)
                for i, u_done in enumerate((u0_done, u1_done)):
                    if on(n, 2):
                        pe.wait_ge(h2_done, n - 1)
                        if i == 0:
                            pe.wait_ge(qt_copied, min(n + 1, NT) if isinstance(n, int) else n + 1)
                        else:
                            pe.wait_ge(yt_copied, min(n, NT) if isinstance(n, int) else n)
                            wait(pe, carry_done, n - 2)
                        for k in range(4):
                            c = (i * 4 + k) * P
                            last = pe.transpose(ps_t[:, i, k * P:(k + 1) * P], h2[:, par, c:c + P], ident[:])
                        last.then_inc(ht_done, 1)
                    if on(n, 1):
                        if isinstance(n, int) and n == 1:
                            pe.wait_ge(wo_loaded, 16 * KC)
                        pe.wait_ge(x_loaded[q], (half(n - 1, q) + 1) * 32)
                        pe.wait_ge(yt_copied, n)
                        wait(pe, x1m_done, (n - 2) * 2 + 1 + i)
                        products(ps_u[:, i], lambda k: yl[:, q, k] if k < NCT else y_t[:, (k - NCT) * P:(k - NCT + 1) * P],
                                 lambda k: wo[:, k, i * 512:(i + 1) * 512], None, u_done)
                if on(n, 2):
                    pe.wait_ge(ht_copied, (n - 1) * 2)
                    wait(pe, th_done, n - 2)
                    pe.wait_ge(at_done, min(n + 1, NT) if isinstance(n, int) else n + 1)
                    for k in range(KC):
                        last = pe.matmul(ps_s[:, 0:N_EXP], h2_t[:, k], wr[:, k], start=(k == 0), stop=(k == KC - 1))
                    last.then_inc(r_done, 1)
            iterations(pe, step)
            pe.wait_ge(bcol_done, 2)
            pe.wait_ge(th_done, NT)
            for c in range(2):
                for w in range(2):
                    i = c * 2 + w
                    last = pe.matmul(ps_s[0:1, i * P:(i + 1) * P], bcol[:, c, w:w + 1], ident[:], start=True, stop=True)
            last.then_inc(brow_done, 1)

def layout(inputs):
    a = {k: np.asarray(v) for k, v in inputs.items()}
    w_in = a["w_in"][0]

    def cols(v):
        return np.ascontiguousarray(np.moveaxis(v.reshape(*v.shape[:-1], -1, P), -1, 0))

    def rows(w):
        return np.ascontiguousarray(w.reshape(-1, P, w.shape[1]).transpose(1, 0, 2))

    out = {}
    out["ident"] = np.eye(P, dtype=np.float32)
    out["cond"] = np.ascontiguousarray(np.stack([cols(a["c"][0]), cols(a["c_ctx"])], -1))
    wm = a["w_mod"][0].reshape(8, P, 12, 512)
    out["w_mod"] = np.ascontiguousarray(wm.transpose(2, 1, 0, 3)).reshape(12, P, 4096)
    out["b_mod"] = np.repeat(a["b_mod"], 2, 0)
    out["xt"] = np.concatenate([a["ctx"][0], a["x"][0]]).reshape(18, P, 1024)
    out["gain_mix"] = cols(a["norm_mix"][0])
    out["w_a"] = rows(w_in[:, :1024])
    dirs = np.stack([a["lru_b_rec"][0], a["lru_b_in"][0]], 1)
    chan = lambda v: v.reshape(*v.shape[:-1], 4, P)
    out["lru_small"] = np.concatenate([
        chan(a["conv_w"][0]).transpose(2, 1, 0).reshape(P, 16),
        chan(a["conv_b"][0]).T.reshape(P, 4),
        chan(dirs).transpose(3, 2, 0, 1).reshape(P, 16),
        chan(a["lru_lambda"][0]).transpose(2, 1, 0).reshape(P, 8)], 1)
    gates = np.zeros((P, 4, 2, 2, P), np.float32)
    for g, name in enumerate(("lru_w_rec", "lru_w_in")):
        for b in range(8):
            q = b % 2 * 64
            gates[q:q + 64, b // 2, :, g, q:q + 64] = a[name][0][:, b].transpose(1, 0, 2)
    out["lru_gates"] = gates.reshape(P, -1)
    out["w_kv"] = rows(w_in[:, 1536:2560])
    out["w_qg"] = rows(np.concatenate([w_in[:, 1024:1536], w_in[:, 2560:]], 1))
    out["w_out"] = rows(a["w_out"][0])
    out["w_router"] = rows(a["w_router"][0]).reshape(P, -1)
    out["b_router"] = a["b_router"]
    out["gain_ffn"] = a["norm_ffn"]
    out["gain_final"] = a["norm_final"][None]
    both = []
    for up, down in ((("w_sh_gate", "w_sh_up"), "w_sh_down"), (("w_exp_gate", "w_exp_up"), "w_exp_down")):
        gu = np.concatenate([a[n][0].reshape(-1, 8, P, 256) for n in up], 3).transpose(0, 2, 1, 3)
        dn = a[down][0].reshape(-1, 2, P, 1024).transpose(0, 2, 1, 3)
        both.append(np.concatenate([gu.reshape(-1, P, 4096), dn.reshape(-1, P, 2048)], 2))
    out["experts"] = np.concatenate(both)
    out.update(constants())
    return out


def constants():
    out = {}
    f = 10000.0 ** (-np.arange(32) / 32.0)
    t = np.arange(2048)
    ang = np.stack([(t // 64)[:, None] * f, (t % 64)[:, None] * f], 1)
    cos = np.repeat(np.cos(ang)[:, :, None], 2, 2).reshape(2048, 128)
    sin = np.stack([-np.sin(ang), np.sin(ang)], 2).reshape(2048, 128)
    out["rope"] = np.concatenate([cos, sin], 1).reshape(16, P, 256).astype(np.float32)
    g = np.log1p(-np.exp2(-(5.0 + 2.0 * np.arange(4))))
    i = np.arange(P, dtype=np.float64)
    s = 128.0 ** -0.5
    out["zeta"] = (s * np.exp(np.concatenate([(127 - i)[:, None] * g, i[:, None] * g], 1))).astype(np.float32)
    out["gc"] = np.repeat(np.exp(128 * g)[None], P, 0).astype(np.float32)
    dist = np.abs(i[:, None] - i[None])
    out["dmat"] = (s * np.exp(dist[:, None] * g[None, :, None])).reshape(P, 512).astype(np.float32)
    out["order"] = np.concatenate([i[:, None] < i[None], np.ones((P, P), bool)], 1).astype(np.float32)
    out["iota"] = np.repeat(np.arange(64, dtype=np.float32)[None], P, 0)
    out["list_base"] = (out["iota"] + 1) * 2048
    out["kcol"] = np.stack([i, i + P], 1).astype(np.float32)
    out["token"] = (np.arange(16)[None] * P + np.arange(P)[:, None]).astype(np.uint32)
    xi = np.exp(np.stack([(i + 1)[None] * g[:, None], (128 - i)[None] * g[:, None]]))
    out["xi"] = np.repeat(xi.reshape(1, -1), P, 0).astype(np.float32)
    return out


def experts(nc, for_dma, io, mod_d, h2_d, sum_d, list_d, ident, blocks_row, ends_row):
    RING = 2
    WE = KC * 2 * D_EXP
    WD = D_EXP // P * D
    W = WE + WD
    CHUNK = 1024
    N_GU, N_D = WE // CHUNK, WD // CHUNK
    with ExitStack() as ctx:
        def sb(name, shape, dt=F32):
            return ctx.enter_context(nc.sbuf_tensor(name, shape, dt))

        semaphores = []

        def sem(name, held_by=ctx):
            semaphores.append(held_by.enter_context(nc.semaphore(name)))
            return semaphores[-1]

        def dma_sem(name):
            return sem(name, for_dma)

        w_raw = sb("w_exp", [P, RING * W])
        w = [sb("w_exp_hi", [P, RING * W]), sb("w_exp_lo", [P, RING * W])]
        g2 = sb("g2_row", [P, D])
        take = sb("take", [P, 2, 2], U32)
        give = sb("give", [P, 2, 2], U32)
        xg = sb("x_gathered", [P, 2, D])
        x_t = [sb("x_exp_t_hi", [P, 2, KC * P]), sb("x_exp_t_lo", [P, 2, KC * P])]
        th = sb("tanh_e", [P, 2, D_EXP])
        hg = sb("h_gated", [P, 2, D_EXP])
        h_t = [sb("h_exp_t_hi", [P, 2, D_EXP]), sb("h_exp_t_lo", [P, 2, D_EXP])]
        y = sb("y_exp", [P, 2, D])
        ps_h = ctx.enter_context(nc.psum_tensor("ps_h", [P, 2, 512], F32))
        ps_x = ctx.enter_context(nc.psum_tensor("ps_x", [P, 2, 512], F32))
        ps_y = ctx.enter_context(nc.psum_tensor("ps_y", [P, 2, 512], F32))
        ps_t = ctx.enter_context(nc.psum_tensor("ps_ht", [P, 512], F32))
        gu_loaded = [dma_sem(f"gu_loaded{i}") for i in range(RING)]
        wd_loaded = [dma_sem(f"wd_loaded{i}") for i in range(RING)]
        take_loaded = [dma_sem("take_loaded0"), dma_sem("take_loaded1")]
        give_loaded = [dma_sem("give_loaded0"), dma_sem("give_loaded1")]
        gathered = [dma_sem("gathered0"), dma_sem("gathered1")]
        g2_loaded = dma_sem("g2_loaded")
        xt_done, xt_hi, xt_lo, h_done, th_done, hs_own, hg_done = (
            sem(n) for n in "ext_done ext_hi ext_lo eh_done eth_done ehs_own ehg_done".split())
        ht_done, ht_hi, ht_lo, d_done, y_done = (sem(n) for n in "eht_done eht_hi eht_lo ed_done ey_done".split())
        gu_hi, gu_lo, wd_hi, wd_lo = (sem(n) for n in "gu_hi gu_lo wd_hi wd_lo".split())
        added = dma_sem("added")
        clear(nc, semaphores)
        block = ctx.enter_context(nc.Block())

        def pairs(eng):
            routed = eng.value_load(ends_row[0:1, NE:NE + 1], min_val=N_EXP, max_val=MAXB - NT)
            return (routed + 1) // 2 + NT // 2

        def iterations(eng, step):
            n = pairs(eng)
            step(0, 0, 0)
            step(1, 1, 0)
            with eng.Fori(1, n) as r:
                step(r * 2, 0, r)
                step(r * 2 + 1, 1, r)
            return n

        def wait(eng, semaphore, value):
            if not isinstance(value, int) or value > 0:
                eng.wait_ge(semaphore, value)

        def expert_of(eng, k):
            return eng.value_load(blocks_row[0:1, 0, bass.ds(k, 1)], min_val=0, max_val=NE - 1)

        def change(eng, k):
            if isinstance(k, int):
                return 1, k == 0
            e = expert_of(eng, k)
            return e + 1, (e - expert_of(eng, k - 1)) * (NE - 1 - e)

        def at_change(eng, at, split, pieces):
            e, first = at
            if isinstance(first, bool):
                if first:
                    for i in pieces:
                        split(e, i)
                return
            with eng.If(first):
                for i in pieces:
                    split(e, i)

        def piece(e, i):
            return bass.ds(e % RING * W + i * CHUNK, CHUNK)

        def loaded(eng, e, loads):
            for i in range(RING):
                wait(eng, loads[i], (e + RING - i) // RING * 16)

        def slots(eng, k):
            first = eng.value_load(blocks_row[0:1, 1, bass.ds(k, 1)], min_val=0, max_val=LIST * NE // P + TAIL - 1)
            return list_d[bass.ds(first * P, P)]

        @block.sync
        def _(sp):
            sp.dma_start(g2[:], mod_d[0:1, 5 * D:6 * D].broadcast_to([P, D])).then_inc(g2_loaded, 16)

            def load(e, slot, first, size, done):
                src = io["experts"][bass.ds(e, 1)].rearrange("a p n -> (a p) n")
                to = slot * W + first
                sp.dma_start(w_raw[:, to:to + size], src[:, first:first + size]).then_inc(done[slot], 16)

            def load_free(e, slot):
                sp.wait_ge(gu_lo, (e - RING + 1) * N_GU)
                load(e, slot, 0, WE, gu_loaded)
                sp.wait_ge(wd_lo, (e - RING + 1) * N_D)
                load(e, slot, WE, WD, wd_loaded)
            for e in range(RING):
                load(e, e, 0, WE, gu_loaded)
                load(e, e, WE, WD, wd_loaded)
            with sp.Fori(1, NE // RING) as r:
                for i in range(RING):
                    load_free(r * RING + i, i)
            for e in range(NE // RING * RING, NE):
                load_free(e, e % RING)

        @block.gpsimd
        def _(pool):
            def load_take(k, par, r):
                if r is not None:
                    pool.wait_ge(gathered[par], r * 16)
                pool.dma_start(take[:, par], slots(pool, k)).then_inc(take_loaded[par], 16)

            def gather(k, par, r):
                pool.wait_ge(take_loaded[par], (r + 1) * 16)
                wait_apart(pool, xt_done, (k - 1) * 2)
                pool.indirect_dma_start(xg[:, par], None, h2_d[:, :],
                                        bass.IndirectOffsetOnAxis(take[:, par, 0:1], 0)).then_inc(gathered[par], 16)
            load_take(0, 0, None)
            load_take(1, 1, None)
            gather(0, 0, 0)
            gather(1, 1, 0)
            load_take(2, 0, 1)

            def split(e, i):
                pool.wait_ge(wd_hi, e * N_D + i - N_GU + 1)
                pool.tensor_tensor(w[1][:, piece(e, i)].bitcast(F32R), w_raw[:, piece(e, i)], w[0][:, piece(e, i)],
                                   ALU.subtract).then_inc(wd_lo, 1)

            for i in range(N_GU, N_GU + N_D):
                split(0, i)

            def step(k, par, r):
                before = change(pool, k - 1) if not isinstance(k, int) or k > 0 else None
                gather(k + 2, par, r + 1)
                load_take(k + 3, 1 - par, r + 1 + par)
                if before is not None:
                    at_change(pool, before, split, range(N_GU, N_GU + N_D))
                wait(pool, added, (k - 1) * 16)
                pool.dma_start(give[:, par], slots(pool, k)).then_inc(give_loaded[par], 16)
                if not isinstance(k, int) or k > 0:
                    scatter(k - 1, 1 - par)

            def scatter(k, par):
                wait(pool, added, k * 16)
                wait_apart(pool, y_done, (k + 1) * 2)
                pool.indirect_dma_start(sum_d[:, :], bass.IndirectOffsetOnAxis(give[:, par, 0:1], 0),
                                        y[:, par], None, compute_op=ALU.add).then_inc(added, 16)
            n = iterations(pool, step)
            scatter(n * 2 - 1, 1)
            pool.wait_ge(added, n * 32)
            pool.wait_ge(gathered[0], (n + 1) * 16)
            pool.wait_ge(gathered[1], (n + 1) * 16)
            pool.wait_ge(take_loaded[0], (n + 2) * 16)

        @block.scalar
        def _(act):
            def split_gu(e, i):
                if i == 0:
                    loaded(act, e, gu_loaded)
                act.activation(w[0][:, piece(e, i)].bitcast(F32R), w_raw[:, piece(e, i)], ACT.Copy).then_inc(gu_hi, 1)

            def split_d(e, i):
                if i == N_GU:
                    loaded(act, e, wd_loaded)
                act.activation(w[0][:, piece(e, i)].bitcast(F32R), w_raw[:, piece(e, i)], ACT.Copy).then_inc(wd_hi, 1)

            def copy_xt(k, par):
                wait(act, h_done, k - 1)
                for b in range(2):
                    act.wait_ge(xt_done, k * 2 + 1 + b)
                    act.activation(x_t[0][:, par, b * 512:(b + 1) * 512].bitcast(F32R), ps_x[:, b],
                                   ACT.Copy).then_inc(xt_hi, 1)

            def copy_ht(k, par):
                act.wait_ge(ht_done, k + 1)
                wait(act, d_done, k - 1)
                act.activation(h_t[0][:, par].bitcast(F32R), ps_t[:, 0:D_EXP], ACT.Copy).then_inc(ht_hi, 1)

            def step(k, par, r):
                here = change(act, k)
                if not isinstance(k, int) or k > 0:
                    before = change(act, k - 1)
                wait_apart(act, h_done, k)
                at_change(act, here, split_gu, range(3))
                if not isinstance(k, int) or k > 0:
                    copy_ht(k - 1, 1 - par)
                    wait_apart(act, d_done, k - 1)
                    at_change(act, before, split_d, range(N_GU, N_GU + N_D))
                act.wait_ge(h_done, k + 1)
                wait(act, hg_done, k - 1)
                act.activation(th[:, par], ps_h[:, par, 0:D_EXP], ACT.Tanh, scale=0.5).then_inc(th_done, 1)
                copy_xt(k + 1, 1 - par)
                at_change(act, here, split_gu, range(3, N_GU))
            for i in range(N_GU):
                split_gu(0, i)
            for i in range(N_GU, N_GU + N_D):
                split_d(0, i)
            copy_xt(0, 0)
            n = iterations(act, step)
            copy_ht(n * 2 - 1, 1)

        @block.vector
        def _(dve):
            own = Count(dve, hs_own)

            def split(e, i):
                dve.wait_ge(gu_hi, e * N_GU + i + 1)
                dve.tensor_tensor(w[1][:, piece(e, i)].bitcast(F32R), w_raw[:, piece(e, i)], w[0][:, piece(e, i)],
                                  ALU.subtract).then_inc(gu_lo, 1)

            def copy_xt(k, par):
                wait(dve, h_done, k - 1)
                for b in range(2):
                    c = slice(b * 512, (b + 1) * 512)
                    dve.wait_ge(xt_hi, k * 2 + 1 + b)
                    dve.tensor_tensor(x_t[1][:, par, c].bitcast(F32R), ps_x[:, b], x_t[0][:, par, c],
                                      ALU.subtract).then_inc(xt_lo, 1)

            def copy_ht(k, par):
                dve.wait_ge(ht_hi, k + 1)
                wait(dve, d_done, k - 1)
                dve.tensor_tensor(h_t[1][:, par].bitcast(F32R), ps_t[:, 0:D_EXP], h_t[0][:, par],
                                  ALU.subtract).then_inc(ht_lo, 1)

            def weigh(k, par, r):
                dve.wait_ge(give_loaded[par], (r + 1) * 16)
                wait(dve, added, (k - 1) * 16)
                dve.wait_ge(d_done, k + 1)
                for i in range(2):
                    c = slice(i * 512, (i + 1) * 512)
                    dve.scalar_tensor_tensor(y[:, par, c], ps_y[:, i], give[:, par, 1:2].bitcast(F32), g2[:, c],
                                             ALU.mult, ALU.mult).then_inc(y_done, 1)

            def step(k, par, r):
                here = change(dve, k)
                at_change(dve, here, split, range(3))
                if not isinstance(k, int) or k > 0:
                    copy_ht(k - 1, 1 - par)
                dve.wait_ge(th_done, k + 1)
                wait(dve, ht_done, k - 1)
                own.base, own.n = k, 0
                own.of(dve.scalar_tensor_tensor(hg[:, par], th[:, par], 1.0, ps_h[:, par, 0:D_EXP], ALU.add, ALU.mult))
                dve.scalar_tensor_tensor(hg[:, par], hg[:, par], 0.5, ps_h[:, par, D_EXP:2 * D_EXP],
                                         ALU.mult, ALU.mult).then_inc(hg_done, 1)
                copy_xt(k + 1, 1 - par)
                at_change(dve, here, split, range(3, N_GU))
                if not isinstance(k, int) or k > 0:
                    weigh(k - 1, 1 - par, r - (1 - par))
            for i in range(N_GU):
                split(0, i)
            dve.wait_ge(g2_loaded, 16)
            copy_xt(0, 0)
            n = iterations(dve, step)
            copy_ht(n * 2 - 1, 1)
            weigh(n * 2 - 1, 1, n - 1)

        @block.tensor
        def _(pe):
            def transposes(k, par, r):
                pe.wait_ge(gathered[par], (r + 1) * 16)
                for b in range(2):
                    wait(pe, xt_lo, k * 2 - 1 + b)
                    for j in range(4):
                        c = (b * 4 + j) * P
                        last = pe.transpose(ps_x[:, b, j * P:(j + 1) * P], xg[:, par, c:c + P], ident[:])
                    last.then_inc(xt_done, 1)

            def products(out, x, w_part, w_at, chunks, stride, start=False, stop=False):
                for j in range(chunks):
                    last = pe.matmul(out, x[:, j * P:(j + 1) * P].bitcast(F32R),
                                     w_part[:, bass.ds(w_at + j * stride, 512)].bitcast(F32R),
                                     start=(start and j == 0), stop=(stop and j == chunks - 1))
                return last

            def transposes_h(k, par):
                pe.wait_ge(hg_done, k + 1)
                wait(pe, ht_lo, k)
                for j in range(2):
                    last = pe.transpose(ps_t[:, j * P:(j + 1) * P], hg[:, par, j * P:(j + 1) * P], ident[:])
                last.then_inc(ht_done, 1)

            def down(k, par, r):
                e = expert_of(pe, k)
                at = pe.snap(e % RING * W + WE)
                pe.wait_ge(ht_lo, k + 1)
                pe.wait_ge(wd_lo, (e + 1) * N_D)
                wait(pe, y_done, k * 2)
                for i in range(2):
                    products(ps_y[:, i], h_t[0][:, par], w[0], at + i * 512, 2, D, start=True)
                    products(ps_y[:, i], h_t[0][:, par], w[1], at + i * 512, 2, D)
                    last = products(ps_y[:, i], h_t[1][:, par], w[0], at + i * 512, 2, D, stop=True)
                last.then_inc(d_done, 1)

            def step(k, par, r):
                e = expert_of(pe, k)
                at = pe.snap(e % RING * W)
                pe.wait_ge(gu_hi, (e + 1) * N_GU)
                pe.wait_ge(xt_hi, (k + 1) * 2)
                wait(pe, hg_done, k - 1)
                products(ps_h[:, par], x_t[0][:, par], w[0], at, KC, 512, start=True)
                pe.wait_ge(gu_lo, (e + 1) * N_GU)
                products(ps_h[:, par], x_t[0][:, par], w[1], at, KC, 512)
                if not isinstance(k, int) or k > 0:
                    transposes_h(k - 1, 1 - par)
                pe.wait_ge(xt_lo, (k + 1) * 2)
                products(ps_h[:, par], x_t[1][:, par], w[0], at, KC, 512, stop=True).then_inc(h_done, 1)
                transposes(k + 1, 1 - par, r + par)
                if not isinstance(k, int) or k > 0:
                    down(k - 1, 1 - par, r)
            transposes(0, 0, 0)
            n = iterations(pe, step)
            transposes_h(n * 2 - 1, 1)
            down(n * 2 - 1, 1, n)


def final(nc, for_dma, io, sum_d, out):
    RING = 4
    with ExitStack() as ctx:
        def sb(name, shape, dt=F32):
            return ctx.enter_context(nc.sbuf_tensor(name, shape, dt))

        semaphores = []

        def sem(name, held_by=ctx):
            semaphores.append(held_by.enter_context(nc.semaphore(name)))
            return semaphores[-1]

        def dma_sem(name):
            return sem(name, for_dma)

        gain = sb("gain_final_row", [P, D])
        mhalf = sb("mhalf_f", [P, 1])
        x = sb("x_f", [P, RING, D])
        sq = sb("sq_f", [P, 2, D])
        ssq = sb("ssq_f", [P, RING])
        rstd = sb("rstd_f", [P, RING])
        o = sb("out_f", [P, RING, D])
        g_loaded = dma_sem("gf_loaded")
        half_set, sq_done, r_own, r_done, o_done = (
            sem(n) for n in "halff_set sqf_done rf_own rf_done of_done".split())
        x_loaded = [dma_sem(f"xf_loaded{i}") for i in range(RING)]
        stored = [dma_sem(f"f_stored{i}") for i in range(RING)]
        clear(nc, semaphores)
        block = ctx.enter_context(nc.Block())

        @block.sync
        def _(sp):
            for t in range(RING):
                sp.dma_start(x[:, t], sum_d[t * P:(t + 1) * P]).then_inc(x_loaded[t], 16)
            sp.dma_start(gain[:], io["gain_final"].broadcast_to([P, D])).then_inc(g_loaded, 16)
            with sp.Fori(1, NT // RING) as r:
                for i in range(RING):
                    t = r * RING + i
                    sp.wait_ge(o_done, t - RING + 1)
                    sp.dma_start(x[:, i], sum_d[bass.ds(t * P, P)]).then_inc(x_loaded[i], 16)

        @block.scalar
        def _(act):
            with act.Fori(0, NT // RING) as r:
                for i in range(RING):
                    t = r * RING + i
                    act.wait_ge(x_loaded[i], (r + 1) * 16)
                    act.wait_ge(r_done, r * RING)
                    act.wait_ge(sq_done, r * RING + max(i - 1, 0))
                    act.activation(sq[:, i % 2], x[:, i], ACT.Square, accum_out=ssq[:, i:i + 1]).then_inc(sq_done, 1)

        @block.gpsimd
        def _(pool):
            pool.memset(mhalf[:], -0.5).then_inc(half_set, 1)
            pool.wait_ge(half_set, 1)
            with pool.Fori(0, NT // RING) as r:
                for i in range(RING):
                    t = r * RING + i
                    c = slice(i, i + 1)
                    pool.wait_ge(o_done, r * RING)
                    wait_apart(pool, sq_done, t + 1)
                    pool.tensor_scalar(rstd[:, c], ssq[:, c], 1.0 / D, EPS, ALU.mult, ALU.add).then_inc(r_own, 1)
                    pool.wait_ge(r_own, t + 1)
                    pool.tensor_tensor(rstd[:, c], rstd[:, c], mhalf[:], ALU.pow).then_inc(r_done, 1)
                    pool.wait_ge(o_done, t + 1)
                    pool.dma_start(out[bass.ds(t * P, P)], o[:, i]).then_inc(stored[i], 16)
            for i in range(RING):
                pool.wait_ge(stored[i], 16 * NT // RING)

        @block.vector
        def _(dve):
            dve.wait_ge(g_loaded, 16)
            with dve.Fori(0, NT // RING) as r:
                for i in range(RING):
                    t = r * RING + i
                    dve.wait_ge(r_done, t + 1)
                    dve.wait_ge(stored[i], r * 16)
                    dve.scalar_tensor_tensor(o[:, i], x[:, i], rstd[:, i:i + 1], gain[:], ALU.mult, ALU.mult).then_inc(o_done, 1)


def build(nc, io, out):
    def dram(name, shape, dt=F32):
        return nc.dram_tensor(name, shape, dt).ap()

    mod_d = dram("mod_d", (2, 6 * D))
    hx_d = dram("hx_d", (NC + NT, P, D))
    yl_d = dram("yl_d", (NT, P, D_LRU))
    rec_d = dram("rec_d", (NT, P, 4 * HD))
    h2_d = dram("h2_d", (ROWS, D))
    sum_d = dram("sum_d", (ROWS, D))
    list_d = dram("list_d", (LIST * NE + TAIL * P, 2), U32)
    with ExitStack() as for_dma, ExitStack() as ctx:
        ident = ctx.enter_context(nc.sbuf_tensor("ident", [P, P], F32))
        sf = ctx.enter_context(nc.sbuf_tensor("sf_ctx", [P, HD], F32))
        blocks_row = ctx.enter_context(nc.sbuf_tensor("blocks_row", [1, 2, 2 * P], I32))
        ends_row = ctx.enter_context(nc.sbuf_tensor("ends_row", [1, NE + 1], I32))
        i_loaded = ctx.enter_context(nc.semaphore("i_loaded"))
        with nc.Block() as block:
            @block.sync
            def _(sp):
                sp.dma_start(ident[:], io["ident"]).then_inc(i_loaded, 16)
                sp.wait_ge(i_loaded, 16)
        modulation(nc, for_dma, io, mod_d, h2_d, sum_d, list_d)
        with (nc.sbuf_tensor("xa_t", [P, NCT, UW + 3], F32) as xa_t, nc.sbuf_tensor("ga_t", [P, NCT, SEQ], F32) as ga_t):
            project(nc, for_dma, io, mod_d, hx_d, xa_t, ga_t, ident)
            lru(nc, for_dma, io, xa_t, ga_t, yl_d)
        keys(nc, for_dma, io, hx_d, rec_d, sf, ident)
        mixer_out(nc, for_dma, io, mod_d, hx_d, rec_d, yl_d, h2_d, sum_d, list_d, sf, ident, blocks_row, ends_row)
        experts(nc, for_dma, io, mod_d, h2_d, sum_d, list_d, ident, blocks_row, ends_row)
        final(nc, for_dma, io, sum_d, out)


def kernel(**inputs):
    import concourse.bacc as bacc
    from concourse.bass_utils import run_bass_kernel_spmd

    nc = bacc.Bacc("TRN2", target_bir_lowering=False, num_devices=1)
    arrays, io = {}, {}
    for name, a in layout(inputs).items():
        a = np.ascontiguousarray(a)
        arrays["in_" + name] = a
        io[name] = nc.dram_tensor("in_" + name, a.shape, mybir.dt.from_np(a.dtype), kind="ExternalInput").ap()
    out = nc.dram_tensor("out_x", (SEQ, D), F32, kind="ExternalOutput").ap()
    build(nc, io, out)
    r = run_bass_kernel_spmd(nc, [arrays], core_ids=[0])
    return r.results[0]["out_x"].reshape(1, SEQ, D)
```

```python
from contextlib import ExitStack

import numpy as np

import concourse.bass as bass
from concourse import mybir

F32 = mybir.dt.float32
F32R = mybir.dt.float32r
I32 = mybir.dt.int32
U32 = mybir.dt.uint32
ALU = mybir.AluOpType
ACT = mybir.ActivationFunctionType
AX = mybir.AxisListType

P = 128
D = 1024
KC = D // P
SEQ = 2048
CTX = 256
NT = SEQ // P
NC = CTX // P
GT = 4
NG = NT // GT
HEADS = 4
DH = 128
HD = HEADS * DH
D_LRU = 512
NCT = D_LRU // P
N_EXP = 64
TOP_K = 6
N_GROUPS = 8
TOP_GROUPS = 4
D_EXP = 256
EPS = 1e-6
ROUTE_SCALE = 2.5
NE = N_EXP + 1
LIST = SEQ
TAIL = 4
MAXB = NT + NT * TOP_K + N_EXP
ROWS = SEQ + P
PADX = CTX + 3
UW = PADX + SEQ


class Count:

    def __init__(self, eng, sem, base=0):
        self.eng, self.sem, self.base, self.n = eng, sem, base, 0

    def of(self, instruction, next_apart=False):
        self.n += 1
        instruction.then_inc(self.sem, 1)
        self.eng.wait_ge(self.sem, self.base + self.n)
        if next_apart:
            self.eng.nop(nofuse=True)


def wait_apart(eng, semaphore, value):
    if not isinstance(value, int) or value > 0:
        eng.wait_ge(semaphore, value)
        eng.nop(nofuse=True)


def clear(nc, semaphores):
    with nc.Block() as block:
        @block.gpsimd
        def _(pool):
            for s in semaphores:
                pool.sem_clear(s)


def modulation(nc, for_dma, io, mod_d, h2_d, sum_d, list_d):
    NB, RING = 12, 4
    with ExitStack() as ctx:
        def sb(name, shape, dt=F32):
            return ctx.enter_context(nc.sbuf_tensor(name, shape, dt))

        def sem(name):
            return ctx.enter_context(nc.semaphore(name))

        def dma_sem(name):
            return for_dma.enter_context(nc.semaphore(name))

        cond = sb("cond", [P, KC, 2])
        cond_t = sb("cond_t", [P, KC, 2])
        cond_s = sb("cond_s", [P, KC, 2])
        wm = sb("wm", [P, RING, KC, 512])
        bm = sb("bm", [2, NB * 512])
        mod = sb("mod", [2, NB * 512])
        fill = sb("fill", [P, LIST * N_EXP // P, 2], U32)
        fill_s = sb("fill_shared", [P, LIST // P, 2], U32)
        zero = sb("zero_rows", [P, D])
        ps = ctx.enter_context(nc.psum_tensor("ps_mod", [P, 2, 512], F32))
        c_loaded, b_loaded = dma_sem("c_loaded"), dma_sem("b_loaded")
        wm_loaded = [dma_sem(f"wm_loaded{s}") for s in range(RING)]
        tanh_done, silu_own, silu_done = sem("tanh_done"), sem("silu_own"), sem("silu_done")
        mm_done, mod_done, stored = sem("mm_done"), sem("mod_done"), dma_sem("mod_stored")
        fill_set, filled = sem("fill_set"), dma_sem("filled")
        block = ctx.enter_context(nc.Block())

        @block.sync
        def _(sp):
            sp.dma_start(cond[:], io["cond"]).then_inc(c_loaded, 16)
            sp.dma_start(bm[:], io["b_mod"]).then_inc(b_loaded, 16)
            for s in range(RING):
                sp.dma_start(wm[:, s].rearrange("p k n -> p (k n)"), io["w_mod"][s]).then_inc(wm_loaded[s], 16)
            with sp.Fori(1, NB // RING) as r:
                for s in range(RING):
                    sp.wait_ge(mm_done, (r - 1) * RING + s + 1)
                    src = io["w_mod"][bass.ds(r * RING + s, 1)].rearrange("a p n -> (a p) n")
                    sp.dma_start(wm[:, s].rearrange("p k n -> p (k n)"), src).then_inc(wm_loaded[s], 16)
            sp.wait_ge(mod_done, NB)
            sp.dma_start(mod_d, mod[:]).then_inc(stored, 16)
            sp.wait_ge(stored, 16)

        @block.gpsimd
        def _(pool):
            pool.memset(fill[:].rearrange("p r c -> p (r c)"), 0).then_inc(fill_set, 1)
            pool.memset(fill_s[:, :, 1].bitcast(F32), 1.0).then_inc(fill_set, 1)
            pool.memset(zero[:], 0.0).then_inc(fill_set, 1)
            pool.wait_ge(fill_set, 3)
            pool.iota(fill[:, :, 0].rearrange("p (a b) -> p a b", b=P), [[0, LIST * N_EXP // P // P], [1, P]], base=SEQ,
                      channel_multiplier=0).then_inc(fill_set, 1)
            pool.iota(fill_s[:, :, 0], [[1, LIST // P]], base=0, channel_multiplier=LIST // P).then_inc(fill_set, 1)
            pool.wait_ge(fill_set, 5)
            pool.dma_start(list_d[LIST:LIST * NE].rearrange("(p r) c -> p (r c)", p=P),
                           fill[:].rearrange("p r c -> p (r c)")).then_inc(filled, 16)
            pool.dma_start(list_d[0:LIST].rearrange("(p r) c -> p (r c)", p=P),
                           fill_s[:].rearrange("p r c -> p (r c)")).then_inc(filled, 16)
            pool.dma_start(list_d[LIST * NE:LIST * NE + TAIL * P].rearrange("(a r) c -> a (r c)", a=TAIL),
                           fill[0:TAIL, 0:P].rearrange("p r c -> p (r c)")).then_inc(filled, 16)
            pool.dma_start(h2_d[SEQ:ROWS], zero[:]).then_inc(filled, 16)
            pool.dma_start(sum_d[SEQ:ROWS], zero[:]).then_inc(filled, 16)
            pool.wait_ge(filled, 16 * 5)

        @block.scalar
        def _(act):
            act.wait_ge(c_loaded, 16)
            act.activation(cond_t[:], cond[:], ACT.Tanh, scale=0.5).then_inc(tanh_done, 1)

        @block.tensor
        def _(pe):
            pe.wait_ge(silu_done, 1)
            with pe.Fori(0, NB // RING) as r:
                for s in range(RING):
                    pe.wait_ge(wm_loaded[s], (r + 1) * 16)
                    pe.wait_ge(mod_done, r * RING + max(s - 1, 0))
                    for k in range(KC):
                        last = pe.matmul(ps[0:2, s % 2], cond_s[:, k], wm[:, s, k],
                                         start=(k == 0), stop=(k == KC - 1))
                    last.then_inc(mm_done, 1)

        @block.vector
        def _(dve):
            own = Count(dve, silu_own)
            dve.wait_ge(tanh_done, 1)
            own.of(dve.scalar_tensor_tensor(cond_s[:], cond_t[:], 1.0, cond[:], ALU.add, ALU.mult))
            dve.tensor_scalar(cond_s[:], cond_s[:], 0.5, None, ALU.mult).then_inc(silu_done, 1)
            dve.wait_ge(b_loaded, 16)
            with dve.Fori(0, NB // 2) as r:
                for s in range(2):
                    dve.wait_ge(mm_done, r * 2 + s + 1)
                    cols = bass.ds((r * 2 + s) * 512, 512)
                    dve.tensor_tensor(mod[:, cols], ps[0:2, s], bm[:, cols], ALU.add).then_inc(mod_done, 1)


def project(nc, for_dma, io, mod_d, hx_d, xa_t, ga_t, ident):
    with ExitStack() as ctx:
        def sb(name, shape, dt=F32):
            return ctx.enter_context(nc.sbuf_tensor(name, shape, dt))

        semaphores = []

        def sem(name, held_by=ctx):
            semaphores.append(held_by.enter_context(nc.semaphore(name)))
            return semaphores[-1]

        def dma_sem(name):
            return sem(name, for_dma)

        wa = sb("wa", [P, KC, 2 * D_LRU])
        xt = sb("xt", [P, 2, GT, D])
        junk = sb("sq_out", [P, 2, D])
        hx = sb("hx", [P, 2, KC, GT * P])
        ssq = sb("ssq", [P, NC + NT])
        rstd = sb("rstd", [P, NC + NT])
        mhalf = sb("mhalf", [P, 1])
        shift = sb("shift", [P, 2, KC])
        scale = sb("scale", [P, 2, KC])
        gain = sb("gain", [P, KC])
        ps_t = ctx.enter_context(nc.psum_tensor("ps_t", [P, 4, 512], F32))
        ps_p = ctx.enter_context(nc.psum_tensor("ps_p", [P, 4, 512], F32))
        w_loaded, m_loaded = dma_sem("wa_loaded"), dma_sem("m_loaded")
        x_loaded = [[dma_sem(f"x_loaded{p}{j}") for j in range(GT)] for p in range(2)]
        sq_done, half_set, rstd_own, rstd_done = sem("sq_done"), sem("half_set"), sem("rstd_own"), sem("rstd_done")
        z_done, t_done = sem("z_done"), sem("t_done")
        ev_act, ev_dve = sem("ev_act"), sem("ev_dve")
        p_done, xa_done, ga_done = sem("p_done"), sem("xa_done"), sem("ga_done")
        hx_stored = [dma_sem("hx_stored0"), dma_sem("hx_stored1")]
        scale_own, pads_set = sem("scale_own"), sem("pads_set")
        clear(nc, semaphores)
        block = ctx.enter_context(nc.Block())

        first_tile = [0] + [NC + i * GT for i in range(NG)]
        tiles = [NC] + [GT] * NG
        n_groups = NG + 1
        p_before = [0] + [NCT + i * 2 * NCT for i in range(NG)]

        def loads(i, j):
            return sum(1 for h in range(i % 2, i + 1, 2) if j < tiles[h])

        def stores(i):
            return sum(tiles[h] for h in range(i % 2, i, 2))

        @block.sync
        def _(sp):
            sp.dma_start(gain[:], io["gain_mix"]).then_inc(m_loaded, 16)
            for s in range(2):
                for n, t in ((0, shift), (1, scale)):
                    src = mod_d[s, n * D:(n + 1) * D].rearrange("(k p) -> p k", p=P)
                    sp.dma_start(t[:, s], src, allow_slow_non_contiguous=True).then_inc(m_loaded, 16)
            for k in range(KC):
                sp.dma_start(wa[:, k], io["w_a"][:, k]).then_inc(w_loaded, 16)

            for i in range(n_groups):
                sp.wait_ge(ev_act, (i + 1) * (KC // 2))
                sp.wait_ge(ev_dve, (i + 1) * (KC // 2))
                for j in range(tiles[i]):
                    dst = hx_d[first_tile[i] + j].rearrange("p (k t) -> p k t", k=KC)
                    sp.dma_start(dst, hx[:, i % 2, :, j * P:(j + 1) * P]).then_inc(hx_stored[i % 2], 16)
            for b in range(2):
                sp.wait_ge(hx_stored[b], 16 * sum(tiles[b::2]))

        @block.gpsimd
        def _(pool):
            pool.memset(mhalf[:], -0.5).then_inc(half_set, 1)
            for c in range(NCT):
                for a, b in ((0, 2), (2 + CTX, 2 + PADX), (2 + UW, 3 + UW)):
                    pool.memset(xa_t[:, c, a:b], 0.0).then_inc(pads_set, 1)
            pool.wait_ge(half_set, 1)

            def load(i):
                if i >= 2:
                    pool.wait_ge(t_done, (i - 1) * KC)
                for j in range(tiles[i]):
                    pool.dma_start(xt[:, i % 2, j], io["xt"][first_tile[i] + j]).then_inc(x_loaded[i % 2][j], 16)

            load(0)
            load(1)
            for i in range(n_groups):
                for t in range(first_tile[i], first_tile[i] + tiles[i]):
                    col = slice(t, t + 1)
                    pool.wait_ge(sq_done, t + 1)
                    pool.tensor_scalar(rstd[:, col], ssq[:, col], 1.0 / D, EPS, ALU.mult, ALU.add).then_inc(rstd_own, 1)
                    pool.wait_ge(rstd_own, t + 1)
                    pool.tensor_tensor(rstd[:, col], rstd[:, col], mhalf[:], ALU.pow).then_inc(rstd_done, 1)
                if i + 2 < n_groups:
                    load(i + 2)

        @block.scalar
        def _(act):
            act.wait_ge(scale_own, 2)

            def squares(i):
                for j in range(tiles[i]):
                    t = first_tile[i] + j
                    act.wait_ge(x_loaded[i % 2][j], loads(i, j) * 16)
                    if t >= 2:
                        act.wait_ge(sq_done, t - 1)
                    act.activation(junk[:, t % 2], xt[:, i % 2, j], ACT.Square, accum_out=ssq[:, t:t + 1]).then_inc(sq_done, 1)

            squares(0)
            for i in range(n_groups):
                w = tiles[i] * P
                s = 1 if i == 0 else 0
                if i >= 2:
                    act.wait_ge(hx_stored[i % 2], stores(i) * 16)
                for k in range(0, KC, 2):
                    act.wait_ge(t_done, i * KC + k + 1)
                    act.activation(hx[:, i % 2, k, 0:w], ps_t[:, k % 4, 0:w], ACT.Identity,
                                   bias=shift[:, s, k:k + 1], scale=scale[:, s, k:k + 1]).then_inc(ev_act, 1)
                if i + 1 < n_groups:
                    squares(i + 1)
                if i >= 1:
                    for c in range(NCT):
                        act.wait_ge(p_done, p_before[i] + NCT + c + 1)
                        act.activation(ga_t[:, c, (i - 1) * GT * P:i * GT * P], ps_p[:, c],
                                       ACT.Gelu_apprx_tanh).then_inc(ga_done, 1)

        @block.vector
        def _(dve):
            dve.wait_ge(m_loaded, 5 * 16)
            for s in range(2):
                dve.scalar_tensor_tensor(scale[:, s], scale[:, s], 1.0, gain[:], ALU.add, ALU.mult).then_inc(scale_own, 1)
            dve.wait_ge(scale_own, 2)

            def normed(i):
                for j in range(tiles[i]):
                    t = first_tile[i] + j
                    dve.wait_ge(rstd_done, t + 1)
                    dve.tensor_scalar(xt[:, i % 2, j], xt[:, i % 2, j], rstd[:, t:t + 1], None, ALU.mult).then_inc(z_done, 1)

            normed(0)
            for i in range(n_groups):
                w = tiles[i] * P
                s = 1 if i == 0 else 0
                if i >= 2:
                    dve.wait_ge(hx_stored[i % 2], stores(i) * 16)
                for k in range(1, KC, 2):
                    dve.wait_ge(t_done, i * KC + k + 1)
                    dve.tensor_scalar(hx[:, i % 2, k, 0:w], ps_t[:, k % 4, 0:w], scale[:, s, k:k + 1],
                                      shift[:, s, k:k + 1], ALU.mult, ALU.add).then_inc(ev_dve, 1)
                if i + 1 < n_groups:
                    normed(i + 1)
                to = 2 if i == 0 else 2 + PADX + (i - 1) * GT * P
                for c in range(NCT):
                    dve.wait_ge(p_done, p_before[i] + c + 1)
                    dve.tensor_copy(xa_t[:, c, to:to + w], ps_p[:, c, 0:w]).then_inc(xa_done, 1)

        @block.tensor
        def _(pe):
            for i in range(n_groups):
                w = tiles[i] * P
                pe.wait_ge(z_done, first_tile[i] + tiles[i])
                for k in range(KC):
                    if i >= 1 or k >= 4:
                        pe.wait_ge(ev_act if k % 2 == 0 else ev_dve, i * (KC // 2) + (k - 4) // 2 + 1)
                    for j in range(tiles[i]):
                        last = pe.transpose(ps_t[:, k % 4, j * P:(j + 1) * P], xt[:, i % 2, j, k * P:(k + 1) * P], ident[:])
                    last.then_inc(t_done, 1)
                if i == 0:
                    pe.wait_ge(w_loaded, 16 * KC)
                pe.wait_ge(ev_act, (i + 1) * (KC // 2))
                pe.wait_ge(ev_dve, (i + 1) * (KC // 2))
                for c in range(NCT if i == 0 else 2 * NCT):
                    if c >= NCT:
                        pe.wait_ge(xa_done, i * NCT + c - NCT + 1)
                    elif i == 1:
                        pe.wait_ge(xa_done, c + 1)
                    elif i >= 2:
                        pe.wait_ge(ga_done, (i - 2) * NCT + c + 1)
                    for k in range(KC):
                        last = pe.matmul(ps_p[:, c % 4, 0:w], wa[:, k, c * P:(c + 1) * P], hx[:, i % 2, k, 0:w],
                                         start=(k == 0), stop=(k == KC - 1))
                    last.then_inc(p_done, 1)
def lru(nc, for_dma, io, xa_t, ga_t, yl_d):
    SEG = [(a, min(a + 512, UW)) for a in range(0, UW, 512)]
    NS = len(SEG)
    LOG_TERMS = 9
    with ExitStack() as ctx:
        def sb(name, shape, dt=F32):
            return ctx.enter_context(nc.sbuf_tensor(name, shape, dt))

        def sem(name):
            return ctx.enter_context(nc.semaphore(name))

        def dma_sem(name):
            return for_dma.enter_context(nc.semaphore(name))

        wg = sb("w_gates", [P, NCT, 2, 2, P])
        small = sb("lru_small", [P, NCT * 15])
        taps = small[:, 0:NCT * 4].rearrange("p (c j) -> p c j", j=4)
        cbias = small[:, NCT * 4:NCT * 5]
        gbias = small[:, NCT * 5:NCT * 9].rearrange("p (c d g) -> p c d g", d=2, g=2)
        lam = small[:, NCT * 9:NCT * 11]
        hbias = sb("half_bias", [P, NCT, 2, 2])
        lw = sb("lam_work", [P, 5, NCT * 2])
        ch = sb("decay_half", [P, NCT * 2])
        u = sb("u", [P, 2, UW])
        tr = sb("tanh_r", [P, 2, UW])
        ti = sb("tanh_i", [P, 3, UW])
        a = sb("decay", [P, 2, UW])
        tl = sb("tanh_l", [P, 2, UW])
        h = sb("states", [P, 2, UW])
        ps = ctx.enter_context(nc.psum_tensor("ps_gate", [P, 8, 512], F32))
        g_loaded, s_loaded = dma_sem("g_loaded"), dma_sem("s_loaded")
        exp_lam, ch_own, ch_done, hb_done = sem("exp_lam"), sem("ch_own"), sem("ch_done"), sem("hb_done")
        u_done, u_own, gates_done, tanh_done = sem("u_done"), sem("u_own"), sem("gates_done"), sem("gate_tanh_done")
        a_done, tl_done, sq_done, s2_done, beta_done = sem("a_done"), sem("tl_done"), sem("a2_done"), sem("s2_done"), sem("beta_done")
        ib_done, b_done, scan_own, scan_done = sem("ib_done"), sem("b_done"), sem("scan_own"), sem("scan_done")
        sum_done, y_done, y_stored = sem("sum_done"), sem("y_done"), dma_sem("y_stored")
        block = ctx.enter_context(nc.Block())

        @block.sync
        def _(sp):
            sp.dma_start(small[:, 0:NCT * 11], io["lru_small"]).then_inc(s_loaded, 16)
            sp.dma_start(wg[:].rearrange("p c d g n -> p (c d g n)"), io["lru_gates"]).then_inc(g_loaded, 16)
            for c in range(NCT):
                sp.wait_ge(y_done, c + 1)
                dst = yl_d.rearrange("m p (c t) -> c p m t", c=NCT)[c]
                sp.dma_start(dst, ga_t[:, c].rearrange("p (m t) -> p m t", t=P)).then_inc(y_stored, 16)
            sp.wait_ge(y_stored, 16 * NCT)

        @block.tensor
        def _(pe):
            pe.wait_ge(g_loaded, 16)
            for c in range(NCT):
                for d in range(2):
                    if d == 0:
                        pe.wait_ge(u_done, c + 1)
                    for s, (lo, hi) in enumerate(SEG):
                        for g in range(2):
                            n = ((c * 2 + d) * NS + s) * 2 + g
                            if n >= 8:
                                pe.wait_ge(tanh_done, n - 7)
                            pe.matmul(ps[:, n % 8, 0:hi - lo], wg[:, c, d, g], u[:, c % 2, lo:hi],
                                      start=True, stop=True).then_inc(gates_done, 1)

        @block.scalar
        def _(act):
            act.wait_ge(s_loaded, 16)
            act.activation(lw[:, 0], lam, ACT.Abs).then_inc(exp_lam, 1)
            act.wait_ge(exp_lam, 1)
            act.activation(lw[:, 1], lw[:, 0], ACT.Exp, scale=-1.0).then_inc(exp_lam, 1)
            act.wait_ge(hb_done, 1)
            for c in range(NCT):
                for d in range(2):
                    i = c * 2 + d
                    for s, (lo, hi) in enumerate(SEG):
                        for g, dst in enumerate((tr[:, d], ti[:, i % 3])):
                            n = (i * NS + s) * 2 + g
                            if s == 0 and g == 0 and i >= 2:
                                act.wait_ge(s2_done, i - 1)
                            if s == 0 and g == 1 and i >= 3:
                                act.wait_ge(scan_done, i - 2)
                            act.wait_ge(gates_done, n + 1)
                            act.activation(dst[:, lo:hi], ps[:, n % 8, 0:hi - lo], ACT.Tanh,
                                           bias=hbias[:, c, d, g:g + 1], scale=0.5).then_inc(tanh_done, 1)
                    act.wait_ge(tanh_done, (i + 1) * NS * 2)
                    if i >= 2:
                        act.wait_ge(scan_done, (i - 1))
                        act.wait_ge(b_done, i - 1)
                    if i == 0:
                        act.wait_ge(ch_done, 1)
                    k = ch[:, i:i + 1]
                    act.activation(a[:, d], tr[:, d], ACT.Exp, bias=k, scale=k).then_inc(a_done, 1)
                    act.activation(tl[:, d], tr[:, d], ACT.Tanh, bias=k, scale=k).then_inc(tl_done, 1)
                    act.wait_ge(a_done, i + 1)
                    act.wait_ge(tl_done, i + 1)
                    act.activation(tr[:, d], a[:, d], ACT.Square).then_inc(sq_done, 1)
                for d in range(2):
                    i = c * 2 + d
                    act.wait_ge(s2_done, i + 1)
                    act.activation(tl[:, d], tl[:, d], ACT.Sqrt, scale=-0.25).then_inc(beta_done, 1)

        @block.gpsimd
        def _(pool):
            for c in range(NCT):
                for d in range(2):
                    i = c * 2 + d
                    pool.wait_ge(beta_done, i + 1)
                    pool.wait_ge(ib_done, i + 1)
                    pool.tensor_tensor(ti[:, i % 3], ti[:, i % 3], tl[:, d], ALU.mult).then_inc(b_done, 1)

        @block.vector
        def _(dve):
            dve.wait_ge(s_loaded, 16)
            dve.tensor_scalar(hbias[:].rearrange("p c d g -> p (c d g)"), gbias.rearrange("p c d g -> p (c d g)"),
                              0.5, None, ALU.mult).then_inc(hb_done, 1)
            conv = Count(dve, u_own)

            def convolve(c):
                b = c % 2
                if c >= 2:
                    dve.wait_ge(gates_done, (c - 1) * 4 * NS)
                    dve.wait_ge(ib_done, (c - 1) * 2)
                conv.of(dve.tensor_scalar(u[:, b], xa_t[:, c, 0:UW], taps[:, c, 0:1], cbias[:, c:c + 1],
                                          ALU.mult, ALU.add))
                for j in range(1, 4):
                    step = dve.scalar_tensor_tensor(u[:, b], xa_t[:, c, j:j + UW], taps[:, c, j:j + 1], u[:, b],
                                                    ALU.mult, ALU.add)
                    if j < 3:
                        conv.of(step)
                    else:
                        step.then_inc(u_done, 1)
                dve.wait_ge(u_done, c + 1)

            convolve(0)
            own = Count(dve, ch_own)
            dve.wait_ge(exp_lam, 2)
            z, s, s2, t = lw[:, 1], lw[:, 2], lw[:, 3], lw[:, 4]
            own.of(dve.tensor_scalar(s, z, 2.0, None, ALU.add))
            own.of(dve.reciprocal(s, s))
            own.of(dve.tensor_tensor(s, s, z, ALU.mult))
            own.of(dve.tensor_tensor(s2, s, s, ALU.mult))
            own.of(dve.memset(t, 1.0 / (2 * LOG_TERMS - 1)))
            for k in range(LOG_TERMS - 2, -1, -1):
                own.of(dve.tensor_tensor(t, t, s2, ALU.mult))
                own.of(dve.tensor_scalar(t, t, 1.0 / (2 * k + 1), None, ALU.add))
            own.of(dve.scalar_tensor_tensor(t, t, 2.0, s, ALU.mult, ALU.mult))
            own.of(dve.tensor_scalar(s, lam, -1.0, 0.0, ALU.mult, ALU.max))
            own.of(dve.tensor_tensor(t, t, s, ALU.add))
            dve.tensor_scalar(ch[:], t, -4.0, None, ALU.mult).then_inc(ch_done, 1)
            convolve(1)
            scans = Count(dve, scan_own)
            for c in range(NCT):
                for d in range(2):
                    i = c * 2 + d
                    dve.wait_ge(sq_done, i + 1)
                    dve.scalar_tensor_tensor(tl[:, d], tr[:, d], 1.0, tl[:, d], ALU.add, ALU.mult).then_inc(s2_done, 1)
                    dve.scalar_tensor_tensor(ti[:, i % 3], ti[:, i % 3], 1.0, u[:, c % 2], ALU.add, ALU.mult).then_inc(ib_done, 1)
                lat, con = slice(PADX, UW), slice(0, CTX)
                b0, b1 = ti[:, c * 2 % 3], ti[:, (c * 2 + 1) % 3]
                dve.wait_ge(b_done, c * 2 + 1)
                if c >= 1:
                    dve.wait_ge(y_done, c)
                scans.of(dve.tensor_tensor_scan(h[:, 0, con], a[:, 0, con], b0[:, con], 0.0, ALU.mult, ALU.add))
                dve.tensor_tensor_scan(h[:, 0, lat], a[:, 0, lat], b0[:, lat], h[:, 0, CTX - 1:CTX],
                                       ALU.mult, ALU.add).then_inc(scan_done, 1)
                if c + 2 < NCT:
                    convolve(c + 2)
                dve.wait_ge(b_done, c * 2 + 2)
                scans.of(dve.tensor_tensor_scan(h[:, 1, 0:CTX][:, ::-1], a[:, 1, 0:CTX][:, ::-1], b1[:, 0:CTX][:, ::-1],
                                                0.0, ALU.mult, ALU.add))
                dve.tensor_tensor_scan(h[:, 1, lat][:, ::-1], a[:, 1, lat][:, ::-1], b1[:, lat][:, ::-1], h[:, 1, 0:1],
                                       ALU.mult, ALU.add).then_inc(scan_done, 1)
                dve.wait_ge(scan_done, c * 2 + 2)
                dve.tensor_tensor(h[:, 0, lat], h[:, 0, lat], h[:, 1, lat], ALU.add).then_inc(sum_done, 1)
                dve.wait_ge(sum_done, c + 1)
                dve.tensor_tensor(ga_t[:, c], h[:, 0, lat], ga_t[:, c], ALU.mult).then_inc(y_done, 1)


def rotate(dve, own, out, tmp, src, table):
    heads = [P, HEADS, DH]
    src4 = src.rearrange("p (h a s i) -> p h a s i", h=HEADS, a=2, s=2)
    tmp4 = tmp.rearrange("p (h a s i) -> p h a s i", h=HEADS, a=2, s=2)
    own.of(dve.tensor_tensor(out.rearrange("p (h e) -> p h e", h=HEADS), src.rearrange("p (h e) -> p h e", h=HEADS),
                             table[:, None, 0:DH].broadcast_to(heads), ALU.mult))
    sines = table[:, DH:2 * DH].rearrange("p (a s i) -> p a s i", a=2, s=2)
    for s in range(2):
        own.of(dve.tensor_tensor(tmp4[:, :, :, s], src4[:, :, :, 1 - s],
                                 sines[:, None, :, s].broadcast_to([P, HEADS, 2, DH // 4]), ALU.mult))
    return dve.tensor_tensor(out, out, tmp, ALU.add)


def keys(nc, for_dma, io, hx_d, rec_d, sf, ident):
    NU = NC + NT
    KT, V, KVF, SB, Q, SG = (slice(i * HD, (i + 1) * HD) for i in range(6))
    with ExitStack() as ctx:
        def sb(name, shape, dt=F32):
            return ctx.enter_context(nc.sbuf_tensor(name, shape, dt))

        semaphores = []

        def sem(name, held_by=ctx):
            semaphores.append(held_by.enter_context(nc.semaphore(name)))
            return semaphores[-1]

        def dma_sem(name):
            return sem(name, for_dma)

        w = [sb("w_in_hi", [P, 2, KC, 2 * HD]), sb("w_in_lo", [P, 2, KC, 2 * HD])]
        hx_raw = sb("hx_raw", [P, KC * P])
        hx = [sb("hx_hi", [P, 2, KC * P]), sb("hx_lo", [P, 2, KC * P])]
        stage = sb("w_stage", [P, 2, 2 * HD])
        rope = sb("rope_kv", [P, 2, 2 * DH])
        kr = sb("kr", [P, 2, HD])
        tmp = sb("rot_kv", [P, HD])
        tg = sb("tanh_g", [P, HD])
        rec = sb("rec", [P, 2, 6 * HD])
        vfb = sb("vfb", [P, 2, HEADS, 2, DH])
        sbd = sb("sb_decayed", [P, HD])
        zeta = sb("zeta_s", [P, 2 * HEADS])
        gc = sb("gc_s", [P, HEADS])
        ps_p = ctx.enter_context(nc.psum_tensor("ps_kvqg", [P, 4, 512], F32))
        ps_k, ps_v, ps_q, ps_g = (ps_p[:, i] for i in range(4))
        ps_t = ctx.enter_context(nc.psum_tensor("ps_kt", [P, 512], F32))
        ps_kv = ctx.enter_context(nc.psum_tensor("ps_kv", [P, 2, 512], F32))
        c_loaded = dma_sem("kv_c_loaded")
        w_loaded = [dma_sem(f"w_loaded{k}") for k in range(KC)]
        hx_loaded = dma_sem("hxk_loaded")
        rope_loaded = [dma_sem("rok_loaded0"), dma_sem("rok_loaded1")]
        w_hi, w_lo, hx_hi, hx_lo = sem("w_hi_k"), sem("w_lo_k"), sem("hx_hi_k"), sem("hx_lo_k")
        q_done, g_done, qr_done, tg_done, sg_done = (sem(n) for n in "q_done g_done qr_done tg_done sg_done".split())
        k_done, v_done, rot_own, kr_done = sem("k_done"), sem("v_done"), sem("rotk_own"), sem("kr_done")
        v_copied, vfb_done, kt_done, kt_copied = sem("v_copied"), sem("vfb_done"), sem("kt_done"), sem("kt_copied")
        kv_done, kvf_done, sbd_done, state_done = sem("kv_done"), sem("kvf_done"), sem("sbd_done"), sem("state_done")
        zeroed = sem("sb_zeroed")
        rec_stored = [dma_sem("rec_stored0"), dma_sem("rec_stored1")]
        clear(nc, semaphores)
        block = ctx.enter_context(nc.Block())

        def wait(eng, semaphore, value):
            if not isinstance(value, int) or value > 0:
                eng.wait_ge(semaphore, value)

        def raw(i, k):
            if i == 0 and k < KC - 2:
                return rec[:, k // 3, k % 3 * 2 * HD:(k % 3 + 1) * 2 * HD]
            return stage[:, k % 2]

        def raw_loaded(eng, i, k):
            if i == 0:
                eng.wait_ge(w_loaded[k], 16)
            else:
                eng.wait_ge(w_loaded[KC - 2 + k % 2], (k // 2 + 2) * 16)

        def used(eng, n):
            if isinstance(n, int) and n < NC:
                wait(eng, v_done, n + 1)
            else:
                eng.wait_ge(g_done, n - NC + 1)

        def loop(eng, step):
            step(2, 0, 0)
            step(3, 1, 0)
            with eng.Fori(1, NT // 2 - 1) as r:
                step(r * 2 + 2, 0, r)
                step(r * 2 + 3, 1, r)
            step(NU - 2, 0, NT // 2 - 1)
            step(NU - 1, 1, NT // 2 - 1)

        @block.sync
        def _(sp):
            sp.dma_start(hx_raw[:], hx_d[1]).then_inc(hx_loaded, 16)
            for k in range(KC):
                sp.dma_start(raw(0, k), io["w_kv"][:, k]).then_inc(w_loaded[k], 16)
            sp.dma_start(zeta[:], io["zeta"]).then_inc(c_loaded, 16)
            sp.dma_start(gc[:], io["gc"]).then_inc(c_loaded, 16)
            sp.wait_ge(hx_lo, 1)
            sp.dma_start(hx_raw[:], hx_d[0]).then_inc(hx_loaded, 16)
            for k in range(KC):
                sp.wait_ge(w_lo, KC - 1 + k)
                sp.dma_start(raw(1, k), io["w_qg"][:, k]).then_inc(w_loaded[KC - 2 + k % 2], 16)
                if k == 3:
                    sp.wait_ge(hx_lo, 2)
                    src = hx_d[bass.ds(NC + NT - 1, 1)].rearrange("a p n -> (a p) n")
                    sp.dma_start(hx_raw[:], src).then_inc(hx_loaded, 16)

            def step(n, par, r):
                tile = r * -2 + (NT - 1 - par)
                wait(sp, qr_done, n - 3)
                src = io["rope"][bass.ds(tile, 1)].rearrange("a p n -> (a p) n")
                sp.dma_start(rope[:, par], src).then_inc(rope_loaded[par], 16)
                if not isinstance(n, int) or n + 1 < NU:
                    sp.wait_ge(hx_lo, n + 1)
                    src = hx_d[bass.ds(tile + (NC - 1), 1)].rearrange("a p n -> (a p) n")
                    sp.dma_start(hx_raw[:], src).then_inc(hx_loaded, 16)
            loop(sp, step)

        @block.gpsimd
        def _(pool):
            pool.wait_ge(w_lo, KC)
            pool.memset(rec[:, 0, SB], 0.0).then_inc(zeroed, 1)
            pool.wait_ge(c_loaded, 32)
            pool.wait_ge(zeroed, 1)
            heads = [P, HEADS, DH]

            def scaled(n, par):
                wait(pool, kv_done, n - 1)
                pool.wait_ge(v_copied, n + 1)
                v = rec[:, par, V].rearrange("p (h e) -> p h e", h=HEADS)
                for f in range(2):
                    z = zeta[:, f * HEADS:(f + 1) * HEADS]
                    pool.tensor_tensor(vfb[:, par, :, f], v, z[:, :, None].broadcast_to(heads), ALU.mult).then_inc(vfb_done, 1)
                wait(pool, state_done, n)
                pool.tensor_tensor(sbd[:].rearrange("p (h e) -> p h e", h=HEADS),
                                   rec[:, par, SB].rearrange("p (h e) -> p h e", h=HEADS),
                                   gc[:, :, None].broadcast_to(heads), ALU.mult).then_inc(sbd_done, 1)

            def store(n, par, r):
                pool.wait_ge(v_copied, n + 1)
                pool.wait_ge(kt_copied, n - 1)
                pool.wait_ge(kvf_done, n + 1)
                pool.wait_ge(qr_done, n - 1)
                wait_apart(pool, sg_done, n - 1)
                tile = r * -2 + (NT - 1 - par)
                dst = rec_d[bass.ds(tile, 1)].rearrange("a p n -> (a p) n")
                pool.dma_start(dst, rec[:, par]).then_inc(rec_stored[par], 16)
            scaled(0, 0)
            scaled(1, 1)

            def step(n, par, r):
                scaled(n, par)
                store(n, par, r)
            loop(pool, step)
            for b in range(2):
                pool.wait_ge(rec_stored[b], 16 * (NT // 2))

        @block.scalar
        def _(act):
            def split_w(i, chunks=range(KC)):
                for k in chunks:
                    raw_loaded(act, i, k)
                    act.activation(w[0][:, i, k].bitcast(F32R), raw(i, k), ACT.Copy).then_inc(w_hi, 1)

            def split_hx(n, par):
                act.wait_ge(hx_loaded, (n + 1) * 16)
                used(act, n - 2)
                act.activation(hx[0][:, par].bitcast(F32R), hx_raw[:], ACT.Copy).then_inc(hx_hi, 1)

            def copy_v(n, par, r):
                if r is not None:
                    wait(act, rec_stored[par], r * 16)
                act.wait_ge(v_done, n + 1)
                act.activation(rec[:, par, V], ps_v, ACT.Copy).then_inc(v_copied, 1)

            split_hx(0, 0)
            split_w(0)
            split_hx(1, 1)
            split_w(1, range(KC // 2))
            copy_v(0, 0, None)
            split_w(1, range(KC // 2, KC))
            split_hx(2, 0)
            copy_v(1, 1, None)
            split_hx(3, 1)

            def copy_kt(n, par):
                act.wait_ge(kt_done, n - 1)
                act.activation(rec[:, par, KT], ps_t[:], ACT.Copy).then_inc(kt_copied, 1)

            def step(n, par, r):
                copy_v(n, par, r)
                if not isinstance(n, int) or n > NC:
                    copy_kt(n - 1, 1 - par)
                act.wait_ge(g_done, n - 1)
                wait(act, sg_done, n - 2)
                act.activation(tg[:], ps_g, ACT.Tanh, scale=0.5).then_inc(tg_done, 1)
                if not isinstance(n, int) or n + 2 < NU:
                    split_hx(n + 2, par)
            loop(act, step)
            copy_kt(NU - 1, 1)

        @block.vector
        def _(dve):
            heads = [P, HEADS, DH]
            rotations = Count(dve, rot_own)

            def split_w(i, chunks=range(KC)):
                for k in chunks:
                    dve.wait_ge(w_hi, i * KC + k + 1)
                    dve.tensor_tensor(w[1][:, i, k].bitcast(F32R), raw(i, k), w[0][:, i, k],
                                      ALU.subtract).then_inc(w_lo, 1)

            def split_hx(n, par):
                dve.wait_ge(hx_hi, n + 1)
                dve.tensor_tensor(hx[1][:, par].bitcast(F32R), hx_raw[:], hx[0][:, par],
                                  ALU.subtract).then_inc(hx_lo, 1)

            def context_k(n):
                dve.wait_ge(k_done, n + 1)
                dve.tensor_copy(kr[:, n], ps_k).then_inc(kr_done, 1)

            def rotate_k(n, par, r):
                dve.wait_ge(k_done, n + 1)
                dve.wait_ge(rope_loaded[par], (r + 1) * 16)
                dve.wait_ge(kv_done, n - 1)
                rotations.base, rotations.n = r * 12 + par * 6, 0
                rotate(dve, rotations, kr[:, par], tmp[:], ps_k, rope[:, par]).then_inc(kr_done, 1)
                dve.wait_ge(kr_done, n + 1)

            def rotate_q(n, par, r):
                dve.wait_ge(q_done, n - 1)
                wait(dve, rec_stored[par], r * 16)
                rotate(dve, rotations, rec[:, par, Q], tmp[:], ps_q, rope[:, par]).then_inc(qr_done, 1)
                dve.wait_ge(tg_done, n - 1)
                dve.scalar_tensor_tensor(rec[:, par, SG], tg[:], 1.0, ps_g, ALU.add, ALU.mult).then_inc(sg_done, 1)
                dve.wait_ge(qr_done, n - 1)

            def states(n, par, r):
                dve.wait_ge(kv_done, n + 1)
                kv = ps_kv[:].rearrange("p b (h f e) -> p (b h) f e", f=2, e=DH)
                if r is not None:
                    dve.tensor_copy(rec[:, par, KVF].rearrange("p (h e) -> p h e", h=HEADS), kv[:, :, 0]).then_inc(kvf_done, 1)
                    wait(dve, rec_stored[1 - par], (r + par) * 16)
                elif n == 0:
                    dve.tensor_copy(sf[:].rearrange("p (h e) -> p h e", h=HEADS), kv[:, :, 0]).then_inc(kvf_done, 1)
                else:
                    dve.wait_ge(c_loaded, 32)
                    dve.wait_ge(kvf_done, 1)
                    dve.tensor_tensor(tmp[:].rearrange("p (h e) -> p h e", h=HEADS), kv[:, :, 0],
                                      gc[:, :, None].broadcast_to(heads), ALU.mult).then_inc(kvf_done, 1)
                dve.wait_ge(sbd_done, n + 1)
                dve.tensor_tensor(rec[:, 1 - par, SB].rearrange("p (h e) -> p h e", h=HEADS), kv[:, :, 1],
                                  sbd[:].rearrange("p (h e) -> p h e", h=HEADS), ALU.add).then_inc(state_done, 1)
            split_hx(0, 0)
            split_w(0)
            split_hx(1, 1)
            split_w(1, range(KC // 2))
            context_k(0)
            split_w(1, range(KC // 2, KC))
            split_hx(2, 0)
            context_k(1)
            states(0, 0, None)
            split_hx(3, 1)

            def step(n, par, r):
                rotate_k(n, par, r)
                if isinstance(n, int) and n == NC:
                    states(1, 1, None)
                    dve.wait_ge(kvf_done, 2)
                    dve.tensor_tensor(sf[:], sf[:], tmp[:], ALU.add).then_inc(zeroed, 1)
                    dve.wait_ge(zeroed, 2)
                else:
                    states(n - 1, 1 - par, r - (1 - par))
                rotate_q(n, par, r)
                if not isinstance(n, int) or n + 2 < NU:
                    split_hx(n + 2, par)
            loop(dve, step)
            states(NU - 1, 1, NT // 2 - 1)

        @block.tensor
        def _(pe):
            def products(out, par, i, half, done):
                for p, (a, b) in enumerate(((0, 0), (0, 1), (1, 0))):
                    for k in range(KC):
                        last = pe.matmul(out, hx[a][:, par, k * P:(k + 1) * P].bitcast(F32R),
                                         w[b][:, i, k, half * HD:(half + 1) * HD].bitcast(F32R),
                                         start=(p + k == 0), stop=(p == 2 and k == KC - 1))
                last.then_inc(done, 1)

            def step(n, par):
                pe.wait_ge(hx_lo, n + 1)
                wait(pe, kr_done, n)
                products(ps_k, par, 0, 0, k_done)
                wait(pe, v_copied, n)
                products(ps_v, par, 0, 1, v_done)
                if not isinstance(n, int) or n > 0:
                    chunk_kv(n - 1, 1 - par, not isinstance(n, int) or n > NC)
                if not isinstance(n, int) or n >= NC:
                    if isinstance(n, int) and n == NC:
                        pe.wait_ge(w_lo, 2 * KC)
                    wait(pe, qr_done, n - 2)
                    products(ps_q, par, 1, 0, q_done)
                    wait(pe, sg_done, n - 2)
                    products(ps_g, par, 1, 1, g_done)

            def chunk_kv(n, par, latent):
                pe.wait_ge(kr_done, n + 1)
                if latent:
                    wait(pe, kt_copied, n - NC)
                    for h in range(HEADS):
                        last = pe.transpose(ps_t[:, h * DH:(h + 1) * DH], kr[:, par, h * DH:(h + 1) * DH], ident[:])
                    last.then_inc(kt_done, 1)
                pe.wait_ge(vfb_done, (n + 1) * 2)
                wait(pe, state_done, n)
                for h in range(HEADS):
                    last = pe.matmul(ps_kv[:, h // 2, (h % 2) * 2 * DH:(h % 2 + 1) * 2 * DH],
                                     kr[:, par, h * DH:(h + 1) * DH], vfb[:, par, h], start=True, stop=True)
                last.then_inc(kv_done, 1)
            pe.wait_ge(w_lo, KC)
            for n in range(NC + 1):
                step(n, n % 2)
            step(3, 1)
            with pe.Fori(1, NT // 2 - 1) as r:
                step(r * 2 + 2, 0)
                step(r * 2 + 3, 1)
            step(NU - 2, 0)
            step(NU - 1, 1)
            chunk_kv(NU - 1, 1, True)


def mixer_out(nc, for_dma, io, mod_d, hx_d, rec_d, yl_d, h2_d, sum_d, list_d, sf, ident, blocks_row, ends_row):
    with ExitStack() as ctx:
        def sb(name, shape, dt=F32):
            return ctx.enter_context(nc.sbuf_tensor(name, shape, dt))

        semaphores = []

        def sem(name, held_by=ctx):
            semaphores.append(held_by.enter_context(nc.semaphore(name)))
            return semaphores[-1]

        def dma_sem(name):
            return sem(name, for_dma)

        wo = [sb("w_out_hi", [P, KC, D]), sb("w_out_lo", [P, KC, D])]
        wr = sb("w_router_s", [P, KC, N_EXP])
        dmat = sb("dmat_s", [P, HD])
        xi = sb("xi_s", [P, 2, HD])
        gc = sb("gc_m", [P, HEADS])
        g1 = sb("g1_row", [P, D])
        a2 = sb("a2_row", [P, D])
        b2 = sb("b2_row", [P, D])
        br = sb("b_router_s", [P, N_EXP])
        order = sb("order_s", [P, 2, P])
        iota = sb("iota_s", [P, N_EXP])
        kcol = sb("kcol_s", [P, 2])
        token = sb("token_s", [P, NT], U32)
        carry = sb("carry", [P, N_EXP])
        mhalf = sb("mhalf_m", [P, 1])
        rec = sb("rec_m", [P, 2, 6 * HD])
        x = sb("x_m", [P, 2, D])
        yl_raw = sb("yl_m", [P, 2, NCT * P])
        yl = [sb("yl_hi", [P, 2, NCT * P]), sb("yl_lo", [P, 2, NCT * P])]
        q_t = sb("q_t", [P, HD])
        qf_t = sb("qf_t", [P, HD])
        qb_t = sb("qb_t", [P, HD])
        at = sb("scores_t", [P, HD])
        sfs = sb("sf_m", [P, 2, HD])
        sfd = sb("sf_decayed", [P, HD])
        sq_o = sb("sq_out_o", [P, HEADS, DH])
        ms = sb("ms", [P, HEADS])
        rh = sb("rh", [P, HEADS])
        y = sb("y_ret", [P, HD])
        y_t = [sb("y_ret_t_hi", [P, HD]), sb("y_ret_t_lo", [P, HD])]
        x1 = sb("x1", [P, 2, D])
        sq_x = sb("sq_out_x", [P, D])
        gain = sq_x
        ssq = sb("ssq_m", [P, 2])
        rstd = sb("rstd_m", [P, 2])
        h2 = sb("h2", [P, 2, D])
        h2_t = sb("h2_t", [P, KC, P])
        th = sb("tanh_s", [P, N_EXP])
        s = sb("s_r", [P, N_EXP])
        sbias = sb("s_biased", [P, N_EXP])
        gt = sb("group_top", [P, N_GROUPS, 8])
        gs = sb("group_score", [P, N_GROUPS])
        m8 = sb("max8", [P, 8])
        i8 = sb("index8", [P, 8], U32)
        f8 = sb("index8_f", [P, 8])
        eq4 = sb("eq4", [P, N_GROUPS, TOP_GROUPS])
        gm = sb("group_mask", [P, N_GROUPS])
        gb = sb("group_low", [P, N_GROUPS])
        eq6 = sb("eq6", [P, 2, TOP_K, N_EXP])
        prod = sb("prod6", [P, TOP_K, N_EXP])
        chosen = sb("chosen", [P, N_EXP])
        sel = sb("sel", [P, TOP_K])
        ssum = sb("sel_sum", [P, 1])
        slot = sb("slot_f", [P, TOP_K])
        slot64 = sb("slot64", [P, N_EXP])
        slot_u = sb("slot_u", [P, 2, TOP_K], U32)
        entry = sb("entry", [P, 2, TOP_K, 2], U32)
        nt = sb("nt", [P, NE])
        nti = sb("nt_i", [P, N_EXP], I32)
        end = sb("end", [P, NE])
        ones = sb("ones65", [P, NE])
        cmp = sb("cmp", [P, 2, NE])
        cmpn = sb("cmp_nt", [P, 2, NE])
        bcol = sb("block_cols", [P, 2, 2])
        scol = sb("start_cols", [P, 2])

        ps_s = ctx.enter_context(nc.psum_tensor("ps_s", [P, 512], F32))
        ps_o = ctx.enter_context(nc.psum_tensor("ps_o", [P, 512], F32))
        ps_u = ctx.enter_context(nc.psum_tensor("ps_u", [P, 2, 512], F32))
        ps_t = ctx.enter_context(nc.psum_tensor("ps_tr", [P, 2, 512], F32))
        ps_q = ctx.enter_context(nc.psum_tensor("ps_qt", [P, 512], F32))
        ps_y = ctx.enter_context(nc.psum_tensor("ps_yt", [P, 512], F32))

        c_loaded = dma_sem("m_c_loaded")
        wo_loaded = [dma_sem(f"wo_loaded{k}") for k in range(4)]
        rec_loaded = [dma_sem("rec_loaded0"), dma_sem("rec_loaded1")]
        x_loaded = [dma_sem("xm_loaded0"), dma_sem("xm_loaded1")]
        (wo_hi, wo_lo, yl_hi, yl_lo, yt_lo, qt_done, qt_copied, qf_done, qb_done, s_done, at_done,
         o_done, sfd_done, sf_done, sqo_done, rh_own, rh_done, y_own, y_done, yt_done, yt_copied, u0_done, u1_done,
         x1m_done, x1_done, sqx_done, rstd_own, rstd_done, h2s_done, h2_done, ht_done, ht_copied, r_done, th_done,
         top_own, chosen_done, listed_ids, rank_done, slot_own, slot_done, entry_done, carry_done) = (
            sem(n) for n in "wo_hi wo_lo yl_hi yl_lo yt_lo qt_done qt_copied qf_done qb_done "
            "s_done at_done o_done sfd_done sf_done sqo_done rh_own rh_done y_own y_done yt_done yt_copied u0_done "
            "u1_done x1m_done x1_done sqx_done rstdm_own rstdm_done h2s_done h2_done ht_done ht_copied r_done "
            "th_done top_own chosen_done listed_ids rank_done slot_own slot_done entry_done carry_done".split())
        consts_set, a2_done = sem("consts_set"), sem("a2_done")
        h2_stored = [dma_sem("h2_stored0"), dma_sem("h2_stored1")]
        x1_stored = [dma_sem("x1_stored0"), dma_sem("x1_stored1")]
        listed = [dma_sem("listed0"), dma_sem("listed1")]
        tab_own, bcol_done, brow_done, rows_done = sem("tab_own"), sem("bcol_done"), sem("brow_done"), sem("rows_done")
        rows_loaded = dma_sem("m_rows_loaded")
        N_CONST, N_ROWS = 10, 4
        clear(nc, semaphores)
        block = ctx.enter_context(nc.Block())

        def iterations(eng, step):
            for n in range(-1, 5):
                step(n, n % 2)
            with eng.Fori(0, (NT - 6) // 2) as r:
                step(r * 2 + 5, 1)
                step(r * 2 + 6, 0)
            for n in range(NT - 1, NT + 4):
                step(n, n % 2)

        def wo_raw(k):
            return (x1, h2)[k % 4 // 2][:, k % 2]

        def on(n, lag):
            return not isinstance(n, int) or 0 <= n - lag < NT

        def wait(eng, semaphore, value):
            if not isinstance(value, int) or value > 0:
                eng.wait_ge(semaphore, value)

        def half(n, par):
            return (n - par) // 2

        def row(t):
            return bass.ds(t, 1)

        @block.sync
        def _(sp):
            def step(n, par):
                if on(n, -1):
                    wait_apart(sp, o_done, n)
                    wait_apart(sp, y_done, n)
                    if not isinstance(n, int) or n >= 1:
                        wait_apart(sp, sf_done, n + 1)
                    src = rec_d[row(n + 1)].rearrange("a p n -> (a p) n")
                    sp.dma_start(rec[:, 1 - par], src).then_inc(rec_loaded[1 - par], 16)
                    wait(sp, x1_done, n)
                    wait(sp, u1_done, n)
                    src = io["xt"][row(n + 1 + NC)].rearrange("a p n -> (a p) n")
                    sp.dma_start(x[:, 1 - par], src).then_inc(x_loaded[1 - par], 16)
                    src = yl_d[row(n + 1)].rearrange("a p n -> (a p) n")
                    sp.dma_start(yl_raw[:, 1 - par], src).then_inc(x_loaded[1 - par], 16)
                if on(n, 1):
                    wait_apart(sp, x1_done, n)
                    sp.dma_start(sum_d[bass.ds((n - 1) * P, P)], x1[:, 1 - par]).then_inc(x1_stored[1 - par], 16)
                    sp.wait_ge(h2_done, n)
                    sp.dma_start(h2_d[bass.ds((n - 1) * P, P)], h2[:, 1 - par]).then_inc(h2_stored[1 - par], 16)
            step(-1, 1)
            for dst, src in ((dmat[:], io["dmat"]), (xi[:].rearrange("p d n -> p (d n)"), io["xi"]), (gc[:], io["gc"]),
                             (order[:].rearrange("p d n -> p (d n)"), io["order"]), (iota[:], io["iota"]),
                             (kcol[:], io["kcol"]), (token[:], io["token"]), (carry[:], io["list_base"]),
                             (wr[:].rearrange("p k n -> p (k n)"), io["w_router"]),
                             (br[:], io["b_router"].broadcast_to([P, N_EXP]))):
                sp.dma_start(dst, src).then_inc(c_loaded, 16)
            for k in range(4):
                sp.dma_start(wo_raw(k), io["w_out"][:, k]).then_inc(wo_loaded[k], 16)
            for dst, src in ((g1[:], mod_d[0:1, 2 * D:3 * D].broadcast_to([P, D])),
                             (b2[:], mod_d[0:1, 3 * D:4 * D].broadcast_to([P, D])),
                             (a2[:], mod_d[0:1, 4 * D:5 * D].broadcast_to([P, D])),
                             (gain[:], io["gain_ffn"].broadcast_to([P, D]))):
                sp.dma_start(dst, src).then_inc(rows_loaded, 16)
            step(0, 0)
            for k in range(4, KC):
                sp.wait_ge(wo_lo, k - 3)
                sp.dma_start(wo_raw(k), io["w_out"][:, k]).then_inc(wo_loaded[k - 4], 16)
            for n in range(1, 3):
                step(n, n % 2)
            with sp.Fori(0, (NT - 6) // 2) as r:
                step(r * 2 + 3, 1)
                step(r * 2 + 4, 0)
            for n in range(NT - 3, NT + 1):
                step(n, n % 2)
            for b in range(2):
                sp.wait_ge(h2_stored[b], 16 * NT // 2)
                sp.wait_ge(x1_stored[b], 16 * NT // 2)

        @block.gpsimd
        def _(pool):
            pool.memset(mhalf[:], -0.5).then_inc(consts_set, 1)
            pool.memset(ones[:], 1.0).then_inc(consts_set, 1)
            pool.wait_ge(c_loaded, 16 * N_CONST)
            pool.wait_ge(consts_set, 2)

            def step(n, par):
                if on(n, 0):
                    pool.wait_ge(qt_copied, n + 1)
                    wait(pool, o_done, n)
                    pool.tensor_tensor(qb_t[:], q_t[:], xi[:, 1], ALU.mult).then_inc(qb_done, 1)
                    wait(pool, sf_done, n + 1)
                    pool.tensor_tensor(sfd[:].rearrange("p (h e) -> p h e", h=HEADS),
                                       sfs[:, par].rearrange("p (h e) -> p h e", h=HEADS),
                                       gc[:, :, None].broadcast_to([P, HEADS, DH]), ALU.mult).then_inc(sfd_done, 1)
                if on(n, 4):
                    t = n - 4
                    pool.wait_ge(entry_done, t + 1)
                    pool.tensor_copy(entry[:, par, :, 0], token[:, row(t)].broadcast_to([P, TOP_K])).then_inc(listed_ids, 1)
                    pool.wait_ge(listed_ids, t + 1)
                    wait_apart(pool, slot_done, t + 1)
                    for j in range(TOP_K):
                        pool.indirect_dma_start(
                            list_d[:, :], bass.IndirectOffsetOnAxis(slot_u[:, par, j:j + 1], 0),
                            entry[:, par, j], None).then_inc(listed[par], 16)
                if isinstance(n, int) and n == 1:
                    pool.wait_ge(rows_loaded, 16 * N_ROWS)
                if on(n, 1):
                    t, b = n - 1, 1 - par
                    pool.wait_ge(x_loaded[b], (half(t, b) + 1) * 32)
                    pool.wait_ge(x1m_done, (t + 1) * 2)
                    pool.tensor_tensor(x1[:, b], x1[:, b], x[:, b], ALU.add).then_inc(x1_done, 1)
                if on(n, 0):
                    wait(pool, y_done, n)
                    wait_apart(pool, sqo_done, (n + 1) * HEADS)
                    pool.tensor_scalar(rh[:], ms[:], 4.0 / DH, 4.0 * EPS, ALU.mult, ALU.add).then_inc(rh_own, 1)
                    pool.wait_ge(rh_own, n + 1)
                    pool.tensor_tensor(rh[:], rh[:], mhalf[:].broadcast_to([P, HEADS]), ALU.pow).then_inc(rh_done, 1)
                if on(n, 1):
                    wait(pool, h2s_done, t - 1)
                    wait_apart(pool, sqx_done, t + 1)
                    pool.tensor_scalar(rstd[:, b:b + 1], ssq[:, b:b + 1], 1.0 / D, EPS, ALU.mult, ALU.add).then_inc(rstd_own, 1)
                    pool.wait_ge(rstd_own, t + 1)
                    pool.tensor_tensor(rstd[:, b:b + 1], rstd[:, b:b + 1], mhalf[:], ALU.pow).then_inc(rstd_done, 1)
                    pool.wait_ge(h2s_done, t + 1)
                    pool.tensor_tensor(h2[:, b], h2[:, b], b2[:], ALU.add).then_inc(h2_done, 1)
            iterations(pool, step)
            for b in range(2):
                pool.wait_ge(listed[b], 16 * TOP_K * NT // 2)

        @block.scalar
        def _(act):
            def step(n, par):
                if on(n, 0):
                    act.wait_ge(qt_done, n + 1)
                    wait(act, o_done, n)
                    wait(act, qf_done, n)
                    wait(act, qb_done, n)
                    act.activation(q_t[:], ps_q[:], ACT.Copy).then_inc(qt_copied, 1)
                if on(n, 1):
                    act.wait_ge(yt_done, n)
                    wait(act, u1_done, n - 1)
                    act.activation(y_t[0][:].bitcast(F32R), ps_y[:], ACT.Copy).then_inc(yt_copied, 1)
                if on(n, 0):
                    act.wait_ge(x_loaded[par], (half(n, par) + 1) * 32)
                    wait(act, u1_done, n - 1)
                    act.activation(yl[0][:, par].bitcast(F32R), yl_raw[:, par], ACT.Copy).then_inc(yl_hi, 1)
                if on(n, 2):
                    for b in range(2):
                        act.wait_ge(ht_done, (n - 2) * 2 + b + 1)
                        wait(act, r_done, n - 2)
                        act.activation(h2_t[:, b * 4:(b + 1) * 4].rearrange("p k t -> p (k t)"), ps_t[:, b],
                                       ACT.Copy).then_inc(ht_copied, 1)
                if on(n, 0):
                    act.wait_ge(o_done, n + 1)
                    wait(act, rh_done, n)
                    wait(act, sqo_done, n * HEADS)
                    for h in range(HEADS):
                        act.activation(sq_o[:, h], ps_o[:, h * DH:(h + 1) * DH], ACT.Square,
                                       accum_out=ms[:, h:h + 1]).then_inc(sqo_done, 1)
                if on(n, 1):
                    act.wait_ge(x1_done, n)
                    if isinstance(n, int) and n == 1:
                        act.wait_ge(a2_done, 1)
                    wait(act, sqx_done, n - 1)
                    wait(act, rstd_done, n - 2)
                    act.activation(sq_x[:], x1[:, 1 - par], ACT.Square, accum_out=ssq[:, 1 - par:2 - par]).then_inc(sqx_done, 1)
                if on(n, 2):
                    act.wait_ge(r_done, n - 1)
                    wait(act, entry_done, n - 2)
                    act.activation(th[:], ps_s[:, 0:N_EXP], ACT.Tanh, scale=0.5).then_inc(th_done, 1)
                if isinstance(n, int) and n == 0:
                    for k in range(KC):
                        act.wait_ge(wo_loaded[k % 4], (k // 4 + 1) * 16)
                        act.activation(wo[0][:, k].bitcast(F32R), wo_raw(k), ACT.Copy).then_inc(wo_hi, 1)
            iterations(act, step)

        @block.vector
        def _(dve):
            dve.wait_ge(c_loaded, 16 * N_CONST)
            dve.tensor_copy(sfs[:, 0], sf[:]).then_inc(sf_done, 1)
            tops, slots = Count(dve, top_own), Count(dve, slot_own)
            N_TOP = 21

            def step(n, par):
                if on(n, 1):
                    dve.wait_ge(yt_copied, n)
                    wait(dve, u1_done, n - 1)
                    dve.tensor_tensor(y_t[1][:].bitcast(F32R), ps_y[:], y_t[0][:], ALU.subtract).then_inc(yt_lo, 1)
                if on(n, 0):
                    dve.wait_ge(qt_copied, n + 1)
                    wait(dve, o_done, n)
                    dve.tensor_tensor(qf_t[:], q_t[:], xi[:, 0], ALU.mult).then_inc(qf_done, 1)
                    dve.wait_ge(s_done, n + 1)
                    dve.tensor_tensor(at[:], ps_s[:], dmat[:], ALU.mult).then_inc(at_done, 1)
                    dve.wait_ge(sfd_done, n + 1)
                    dve.wait_ge(rec_loaded[par], (half(n, par) + 1) * 16)
                    wait(dve, o_done, n)
                    dve.tensor_tensor(sfs[:, 1 - par], sfd[:], rec[:, par, 2 * HD:3 * HD], ALU.add).then_inc(sf_done, 1)
                    dve.wait_ge(yl_hi, n + 1)
                    dve.tensor_tensor(yl[1][:, par].bitcast(F32R), yl_raw[:, par], yl[0][:, par], ALU.subtract).then_inc(yl_lo, 1)
                if on(n, 3):
                    top(n - 3, 1 - par)
                if on(n, 1):
                    t, b = n - 1, 1 - par
                    wait(dve, x1_stored[b], half(t, b) * 16)
                    wait(dve, sqx_done, t - 1)
                    wait(dve, h2s_done, t - 1)
                    for i, u_done in enumerate((u0_done, u1_done)):
                        c = slice(i * 512, (i + 1) * 512)
                        dve.wait_ge(u_done, t + 1)
                        dve.tensor_tensor(x1[:, b, c], ps_u[:, i], g1[:, c], ALU.mult).then_inc(x1m_done, 1)
                if on(n, 0):
                    dve.wait_ge(rh_done, n + 1)
                    wait(dve, yt_done, n)
                    for h in range(HEADS):
                        e = slice(h * DH, (h + 1) * DH)
                        last = dve.scalar_tensor_tensor(y[:, e], ps_o[:, e], rh[:, h:h + 1],
                                                        rec[:, par, 5 * HD + h * DH:5 * HD + (h + 1) * DH], ALU.mult, ALU.mult)
                    last.then_inc(y_done, 1)
                if on(n, 3):
                    t, b = n - 3, 1 - par
                    slots.base, slots.n = t * 3, 0
                    dve.wait_ge(rank_done, t + 1)
                    slots.of(dve.tensor_tensor(slot64[:], ps_y[:, 0:N_EXP], carry[:], ALU.add))
                    dve.tensor_tensor(carry[:], ps_y[:, N_EXP:2 * N_EXP], carry[:], ALU.add).then_inc(carry_done, 1)
                    dve.wait_ge(carry_done, t + 1)
                    slots.of(dve.tensor_tensor(prod[:], eq6[:, b], slot64[:, None, :].broadcast_to([P, TOP_K, N_EXP]), ALU.mult))
                    slots.of(dve.tensor_reduce(slot[:], prod[:], AX.X, ALU.add))
                    wait(dve, listed[b], half(t, b) * 16 * TOP_K)
                    dve.tensor_copy(slot_u[:, b], slot[:]).then_inc(slot_done, 1)
                if on(n, 1):
                    t, b = n - 1, 1 - par
                    dve.wait_ge(rstd_done, t + 1)
                    wait(dve, h2_stored[b], half(t, b) * 16)
                    wait(dve, ht_done, (t - 1) * 2)
                    dve.scalar_tensor_tensor(h2[:, b], x1[:, b], rstd[:, b:b + 1], a2[:], ALU.mult, ALU.mult).then_inc(h2s_done, 1)
                if isinstance(n, int) and n == 0:
                    for k in range(KC):
                        dve.wait_ge(wo_hi, k + 1)
                        dve.tensor_tensor(wo[1][:, k].bitcast(F32R), wo_raw(k), wo[0][:, k], ALU.subtract).then_inc(wo_lo, 1)
                    dve.wait_ge(rows_loaded, 16 * N_ROWS)
                    dve.scalar_tensor_tensor(a2[:], a2[:], 1.0, gain[:], ALU.add, ALU.mult).then_inc(a2_done, 1)
                    dve.wait_ge(a2_done, 1)

            def top(t, b):
                tops.base, tops.n = t * N_TOP, 0
                dve.wait_ge(th_done, t + 1)
                tops.of(dve.tensor_scalar(s[:], th[:], 0.5, 0.5, ALU.mult, ALU.add))
                tops.of(dve.tensor_tensor(sbias[:], s[:], br[:], ALU.add), next_apart=True)
                for g in range(N_GROUPS):
                    last = dve.max(gt[:, g], sbias[:, g * 8:(g + 1) * 8])
                tops.of(last)
                tops.of(dve.tensor_tensor(gs[:], gt[:, :, 0], gt[:, :, 1], ALU.add), next_apart=True)
                tops.of(dve.max(m8[:], gs[:]), next_apart=True)
                tops.of(dve.max_index(i8[:], m8[:], gs[:]))
                tops.of(dve.tensor_copy(f8[:], i8[:]))
                tops.of(dve.tensor_tensor(eq4[:], iota[:, 0:N_GROUPS, None].broadcast_to([P, N_GROUPS, TOP_GROUPS]),
                                          f8[:, None, 0:TOP_GROUPS].broadcast_to([P, N_GROUPS, TOP_GROUPS]), ALU.is_equal))
                tops.of(dve.tensor_reduce(gm[:], eq4[:], AX.X, ALU.add))
                tops.of(dve.tensor_scalar(gb[:], gm[:], -1.0, 1e30, ALU.add, ALU.mult))
                by_group = sbias[:].rearrange("p (g e) -> p g e", g=N_GROUPS)
                wide = [P, N_GROUPS, N_EXP // N_GROUPS]
                tops.of(dve.tensor_tensor(by_group, by_group, gm[:, :, None].broadcast_to(wide), ALU.mult))
                tops.of(dve.tensor_tensor(by_group, by_group, gb[:, :, None].broadcast_to(wide), ALU.add), next_apart=True)
                tops.of(dve.max(m8[:], sbias[:]), next_apart=True)
                tops.of(dve.max_index(i8[:], m8[:], sbias[:]))
                tops.of(dve.tensor_copy(f8[:], i8[:]))
                each = [P, TOP_K, N_EXP]
                tops.of(dve.tensor_tensor(eq6[:, b], iota[:, None, :].broadcast_to(each),
                                          f8[:, 0:TOP_K, None].broadcast_to(each), ALU.is_equal))
                wait(dve, rank_done, t)
                dve.tensor_reduce(chosen[:], eq6[:, b].rearrange("p j e -> p e j"), AX.X, ALU.add).then_inc(chosen_done, 1)
                tops.of(dve.tensor_tensor(prod[:], eq6[:, b], s[:, None, :].broadcast_to(each), ALU.mult))
                tops.of(dve.tensor_reduce(sel[:], prod[:], AX.X, ALU.add))
                tops.of(dve.tensor_reduce(ssum[:], sel[:], AX.X, ALU.add))
                tops.of(dve.reciprocal(ssum[:], ssum[:]))
                tops.of(dve.tensor_scalar(sel[:], sel[:], ssum[:], ROUTE_SCALE, ALU.mult, ALU.mult))
                wait(dve, listed[b], half(t, b) * 16 * TOP_K)
                dve.tensor_copy(entry[:, b, :, 1].bitcast(F32), sel[:]).then_inc(entry_done, 1)
                assert tops.n == N_TOP
            iterations(dve, step)

            own = Count(dve, tab_own)
            dve.wait_ge(carry_done, NT)
            dve.wait_ge(consts_set, 2)
            own.of(dve.scalar_tensor_tensor(nt[:, 1:NE], iota[:], -float(LIST), carry[:], ALU.mult, ALU.add))
            own.of(dve.tensor_scalar(nti[:], nt[:, 1:NE], float(P - 1 - LIST), None, ALU.add))
            own.of(dve.tensor_scalar(nti[:], nti[:], 7, None, ALU.arith_shift_right))
            own.of(dve.tensor_copy(nt[:, 1:NE], nti[:]))
            own.of(dve.tensor_scalar(nt[:, 1:NE], nt[:, 1:NE], 1.0, None, ALU.max))
            own.of(dve.memset(nt[:, 0:1], float(NT)))
            own.of(dve.tensor_tensor_scan(end[:], ones[:], nt[:], 0.0, ALU.mult, ALU.add))
            for c in range(2):
                own.of(dve.tensor_scalar(cmp[:, c], end[:], kcol[:, c:c + 1], None, ALU.is_le))
                own.of(dve.tensor_tensor(cmpn[:, c], cmp[:, c], nt[:], ALU.mult))
                own.of(dve.tensor_reduce(bcol[:, c, 0:1], cmp[:, c], AX.X, ALU.add))
                own.of(dve.tensor_reduce(scol[:, c:c + 1], cmpn[:, c], AX.X, ALU.add))
                own.of(dve.tensor_tensor(scol[:, c:c + 1], kcol[:, c:c + 1], scol[:, c:c + 1], ALU.subtract))
                own.of(dve.scalar_tensor_tensor(bcol[:, c, 1:2], bcol[:, c, 0:1], float(LIST // P), scol[:, c:c + 1],
                                                ALU.mult, ALU.add))
                dve.tensor_scalar(bcol[:, c, 0:1], bcol[:, c, 0:1], float(NE - 1), None, ALU.min).then_inc(bcol_done, 1)
            dve.tensor_copy(ends_row[:, 0:NE], end[0:1, :]).then_inc(rows_done, 1)
            dve.tensor_scalar(ends_row[:, NE:NE + 1], end[0:1, NE - 1:NE], float(-NT), None, ALU.add).then_inc(rows_done, 1)
            dve.wait_ge(brow_done, 1)
            dve.tensor_copy(blocks_row[:].rearrange("p w (c k) -> p c w k", c=2),
                            ps_s[0:1, :].rearrange("p (c w k) -> p c w k", c=2, w=2)).then_inc(rows_done, 1)

        @block.tensor
        def _(pe):
            def out_products(i, x, first, start, stop):
                for p, (a, b) in enumerate(((0, 0), (0, 1), (1, 0))):
                    for k in range(NCT):
                        last = pe.matmul(ps_u[:, i], x[a][:, k * P:(k + 1) * P].bitcast(F32R),
                                         wo[b][:, first + k, i * 512:(i + 1) * 512].bitcast(F32R),
                                         start=(start and p + k == 0), stop=(stop and p == 2 and k == NCT - 1))
                return last

            pe.wait_ge(c_loaded, 16 * N_CONST)

            def step(n, par):
                q = 1 - par
                if on(n, 0):
                    pe.wait_ge(rec_loaded[par], (half(n, par) + 1) * 16)
                    wait(pe, qt_copied, n)
                    for h in range(HEADS):
                        last = pe.transpose(ps_q[:, h * DH:(h + 1) * DH], rec[:, par, 4 * HD + h * DH:4 * HD + (h + 1) * DH],
                                            ident[:])
                    last.then_inc(qt_done, 1)
                if on(n, 1):
                    if isinstance(n, int) and n == 1:
                        pe.wait_ge(wo_lo, KC)
                    pe.wait_ge(yl_lo, n)
                    for i in range(2):
                        wait(pe, x1m_done, (n - 2) * 2 + 1 + i)
                        out_products(i, [t[:, q] for t in yl], 0, True, False)
                    pe.wait_ge(y_done, n)
                    wait(pe, carry_done, n - 3)
                    wait(pe, yt_lo, n - 1)
                    for h in range(HEADS):
                        last = pe.transpose(ps_y[:, h * DH:(h + 1) * DH], y[:, h * DH:(h + 1) * DH], ident[:])
                    last.then_inc(yt_done, 1)
                if on(n, 0):
                    pe.wait_ge(qt_copied, n + 1)
                    wait(pe, th_done, n - 2)
                    for h in range(HEADS):
                        e = slice(h * DH, (h + 1) * DH)
                        last = pe.matmul(ps_s[:, e], rec[:, par, e], q_t[:, e], start=True, stop=True)
                    last.then_inc(s_done, 1)
                if on(n, 1):
                    pe.wait_ge(yt_lo, n)
                    for i, u_done in enumerate((u0_done, u1_done)):
                        out_products(i, y_t, NCT, False, True).then_inc(u_done, 1)
                if on(n, 2):
                    pe.wait_ge(h2_done, n - 1)
                    for i in range(2):
                        wait(pe, ht_copied, (n - 3) * 2 + i + 1)
                        for k in range(4):
                            c = (i * 4 + k) * P
                            last = pe.transpose(ps_t[:, i, k * P:(k + 1) * P], h2[:, par, c:c + P], ident[:])
                        last.then_inc(ht_done, 1)
                if on(n, 0):
                    pe.wait_ge(at_done, n + 1)
                    pe.wait_ge(qf_done, n + 1)
                    pe.wait_ge(qb_done, n + 1)
                    pe.wait_ge(sf_done, n + 1)
                    wait(pe, y_done, n)
                    for h in range(HEADS):
                        e = slice(h * DH, (h + 1) * DH)
                        pe.matmul(ps_o[:, e], at[:, e], rec[:, par, HD + h * DH:HD + (h + 1) * DH], start=True, stop=False)
                        pe.matmul(ps_o[:, e], qf_t[:, e], sfs[:, par, e], start=False, stop=False)
                        last = pe.matmul(ps_o[:, e], qb_t[:, e], rec[:, par, 3 * HD + h * DH:3 * HD + (h + 1) * DH],
                                         start=False, stop=True)
                    last.then_inc(o_done, 1)
                if on(n, 3):
                    pe.wait_ge(chosen_done, n - 2)
                    pe.wait_ge(yt_lo, min(n, NT) if isinstance(n, int) else n)
                    for i in range(2):
                        last = pe.matmul(ps_y[:, i * N_EXP:(i + 1) * N_EXP], order[:, i], chosen[:], start=True, stop=True)
                    last.then_inc(rank_done, 1)
                if on(n, 2):
                    pe.wait_ge(ht_copied, (n - 1) * 2)
                    wait(pe, th_done, n - 2)
                    pe.wait_ge(at_done, min(n + 1, NT) if isinstance(n, int) else n + 1)
                    for k in range(KC):
                        last = pe.matmul(ps_s[:, 0:N_EXP], h2_t[:, k], wr[:, k], start=(k == 0), stop=(k == KC - 1))
                    last.then_inc(r_done, 1)
            iterations(pe, step)
            pe.wait_ge(bcol_done, 2)
            pe.wait_ge(th_done, NT)
            for c in range(2):
                for w in range(2):
                    i = c * 2 + w
                    last = pe.matmul(ps_s[0:1, i * P:(i + 1) * P], bcol[:, c, w:w + 1], ident[:], start=True, stop=True)
            last.then_inc(brow_done, 1)

def layout(inputs):
    a = {k: np.asarray(v) for k, v in inputs.items()}
    w_in = a["w_in"][0]

    def cols(v):
        return np.ascontiguousarray(np.moveaxis(v.reshape(*v.shape[:-1], -1, P), -1, 0))

    def rows(w):
        return np.ascontiguousarray(w.reshape(-1, P, w.shape[1]).transpose(1, 0, 2))

    out = {}
    out["ident"] = np.eye(P, dtype=np.float32)
    out["cond"] = np.ascontiguousarray(np.stack([cols(a["c"][0]), cols(a["c_ctx"])], -1))
    wm = a["w_mod"][0].reshape(8, P, 12, 512)
    out["w_mod"] = np.ascontiguousarray(wm.transpose(2, 1, 0, 3)).reshape(12, P, 4096)
    out["b_mod"] = np.repeat(a["b_mod"], 2, 0)
    out["xt"] = np.concatenate([a["ctx"][0], a["x"][0]]).reshape(18, P, 1024)
    out["gain_mix"] = cols(a["norm_mix"][0])
    out["w_a"] = rows(w_in[:, :1024])
    dirs = np.stack([a["lru_b_rec"][0], a["lru_b_in"][0]], 1)
    chan = lambda v: v.reshape(*v.shape[:-1], 4, P)
    out["lru_small"] = np.concatenate([
        chan(a["conv_w"][0]).transpose(2, 1, 0).reshape(P, 16),
        chan(a["conv_b"][0]).T.reshape(P, 4),
        chan(dirs).transpose(3, 2, 0, 1).reshape(P, 16),
        chan(a["lru_lambda"][0]).transpose(2, 1, 0).reshape(P, 8)], 1)
    gates = np.zeros((P, 4, 2, 2, P), np.float32)
    for g, name in enumerate(("lru_w_rec", "lru_w_in")):
        for b in range(8):
            q = b % 2 * 64
            gates[q:q + 64, b // 2, :, g, q:q + 64] = a[name][0][:, b].transpose(1, 0, 2)
    out["lru_gates"] = gates.reshape(P, -1)
    out["w_kv"] = rows(w_in[:, 1536:2560])
    out["w_qg"] = rows(np.concatenate([w_in[:, 1024:1536], w_in[:, 2560:]], 1))
    out["w_out"] = rows(a["w_out"][0])
    out["w_router"] = rows(a["w_router"][0]).reshape(P, -1)
    out["b_router"] = a["b_router"]
    out["gain_ffn"] = a["norm_ffn"]
    out["gain_final"] = a["norm_final"][None]
    both = []
    for up, down in ((("w_sh_gate", "w_sh_up"), "w_sh_down"), (("w_exp_gate", "w_exp_up"), "w_exp_down")):
        gu = np.concatenate([a[n][0].reshape(-1, 8, P, 256) for n in up], 3).transpose(0, 2, 1, 3)
        dn = a[down][0].reshape(-1, 2, P, 1024).transpose(0, 2, 1, 3)
        both.append(np.concatenate([gu.reshape(-1, P, 4096), dn.reshape(-1, P, 2048)], 2))
    out["experts"] = np.concatenate(both)
    out.update(constants())
    return out


def constants():
    out = {}
    f = 10000.0 ** (-np.arange(32) / 32.0)
    t = np.arange(2048)
    ang = np.stack([(t // 64)[:, None] * f, (t % 64)[:, None] * f], 1)
    cos = np.repeat(np.cos(ang)[:, :, None], 2, 2).reshape(2048, 128)
    sin = np.stack([-np.sin(ang), np.sin(ang)], 2).reshape(2048, 128)
    out["rope"] = np.concatenate([cos, sin], 1).reshape(16, P, 256).astype(np.float32)
    g = np.log1p(-np.exp2(-(5.0 + 2.0 * np.arange(4))))
    i = np.arange(P, dtype=np.float64)
    s = 128.0 ** -0.5
    out["zeta"] = (s * np.exp(np.concatenate([(127 - i)[:, None] * g, i[:, None] * g], 1))).astype(np.float32)
    out["gc"] = np.repeat(np.exp(128 * g)[None], P, 0).astype(np.float32)
    dist = np.abs(i[:, None] - i[None])
    out["dmat"] = (s * np.exp(dist[:, None] * g[None, :, None])).reshape(P, 512).astype(np.float32)
    out["order"] = np.concatenate([i[:, None] < i[None], np.ones((P, P), bool)], 1).astype(np.float32)
    out["iota"] = np.repeat(np.arange(64, dtype=np.float32)[None], P, 0)
    out["list_base"] = (out["iota"] + 1) * 2048
    out["kcol"] = np.stack([i, i + P], 1).astype(np.float32)
    out["token"] = (np.arange(16)[None] * P + np.arange(P)[:, None]).astype(np.uint32)
    xi = np.exp(np.stack([(i + 1)[None] * g[:, None], (128 - i)[None] * g[:, None]]))
    out["xi"] = np.repeat(xi.reshape(1, -1), P, 0).astype(np.float32)
    return out


def experts(nc, for_dma, io, mod_d, h2_d, sum_d, list_d, ident, blocks_row, ends_row):
    RING = 2
    WE = KC * 2 * D_EXP
    WD = D_EXP // P * D
    W = WE + WD
    CHUNK = 1024
    N_GU, N_D = WE // CHUNK, WD // CHUNK
    with ExitStack() as ctx:
        def sb(name, shape, dt=F32):
            return ctx.enter_context(nc.sbuf_tensor(name, shape, dt))

        semaphores = []

        def sem(name, held_by=ctx):
            semaphores.append(held_by.enter_context(nc.semaphore(name)))
            return semaphores[-1]

        def dma_sem(name):
            return sem(name, for_dma)

        w_raw = sb("w_exp", [P, RING * W])
        w = [sb("w_exp_hi", [P, RING * W]), sb("w_exp_lo", [P, RING * W])]
        g2 = sb("g2_row", [P, D])
        take = sb("take", [P, 2, 2], U32)
        give = sb("give", [P, 2, 2], U32)
        xg = sb("x_gathered", [P, 2, D])
        x_t = [sb("x_exp_t_hi", [P, 2, KC * P]), sb("x_exp_t_lo", [P, 2, KC * P])]
        th = sb("tanh_e", [P, 2, D_EXP])
        hg = sb("h_gated", [P, 2, D_EXP])
        h_t = [sb("h_exp_t_hi", [P, 2, D_EXP]), sb("h_exp_t_lo", [P, 2, D_EXP])]
        y = sb("y_exp", [P, 2, D])
        ps_h = ctx.enter_context(nc.psum_tensor("ps_h", [P, 2, 512], F32))
        ps_x = ctx.enter_context(nc.psum_tensor("ps_x", [P, 2, 512], F32))
        ps_y = ctx.enter_context(nc.psum_tensor("ps_y", [P, 2, 512], F32))
        ps_t = ctx.enter_context(nc.psum_tensor("ps_ht", [P, 512], F32))
        gu_loaded = [dma_sem(f"gu_loaded{i}") for i in range(RING)]
        wd_loaded = [dma_sem(f"wd_loaded{i}") for i in range(RING)]
        take_loaded = [dma_sem("take_loaded0"), dma_sem("take_loaded1")]
        give_loaded = [dma_sem("give_loaded0"), dma_sem("give_loaded1")]
        gathered = [dma_sem("gathered0"), dma_sem("gathered1")]
        g2_loaded = dma_sem("g2_loaded")
        xt_done, xt_hi, xt_lo, h_done, th_done, hs_own, hg_done = (
            sem(n) for n in "ext_done ext_hi ext_lo eh_done eth_done ehs_own ehg_done".split())
        ht_done, ht_hi, ht_lo, d_done, y_done = (sem(n) for n in "eht_done eht_hi eht_lo ed_done ey_done".split())
        gu_hi, gu_lo, wd_hi, wd_lo = (sem(n) for n in "gu_hi gu_lo wd_hi wd_lo".split())
        added = dma_sem("added")
        clear(nc, semaphores)
        block = ctx.enter_context(nc.Block())

        def pairs(eng):
            routed = eng.value_load(ends_row[0:1, NE:NE + 1], min_val=N_EXP, max_val=MAXB - NT)
            return (routed + 1) // 2 + NT // 2

        def iterations(eng, step):
            n = pairs(eng)
            step(0, 0, 0)
            step(1, 1, 0)
            with eng.Fori(1, n) as r:
                step(r * 2, 0, r)
                step(r * 2 + 1, 1, r)
            return n

        def wait(eng, semaphore, value):
            if not isinstance(value, int) or value > 0:
                eng.wait_ge(semaphore, value)

        def expert_of(eng, k):
            return eng.value_load(blocks_row[0:1, 0, bass.ds(k, 1)], min_val=0, max_val=NE - 1)

        def change(eng, k):
            if isinstance(k, int):
                return 1, k == 0
            e = expert_of(eng, k)
            return e + 1, (e - expert_of(eng, k - 1)) * (NE - 1 - e)

        def at_change(eng, at, split, pieces):
            e, first = at
            if isinstance(first, bool):
                if first:
                    for i in pieces:
                        split(e, i)
                return
            with eng.If(first):
                for i in pieces:
                    split(e, i)

        def piece(e, i):
            return bass.ds(e % RING * W + i * CHUNK, CHUNK)

        def loaded(eng, e, loads):
            for i in range(RING):
                wait(eng, loads[i], (e + RING - i) // RING * 16)

        def slots(eng, k):
            first = eng.value_load(blocks_row[0:1, 1, bass.ds(k, 1)], min_val=0, max_val=LIST * NE // P + TAIL - 1)
            return list_d[bass.ds(first * P, P)]

        @block.sync
        def _(sp):
            sp.dma_start(g2[:], mod_d[0:1, 5 * D:6 * D].broadcast_to([P, D])).then_inc(g2_loaded, 16)

            def load(e, slot, first, size, done):
                src = io["experts"][bass.ds(e, 1)].rearrange("a p n -> (a p) n")
                to = slot * W + first
                sp.dma_start(w_raw[:, to:to + size], src[:, first:first + size]).then_inc(done[slot], 16)

            def load_free(e, slot):
                sp.wait_ge(gu_lo, (e - RING + 1) * N_GU)
                load(e, slot, 0, WE, gu_loaded)
                sp.wait_ge(wd_lo, (e - RING + 1) * N_D)
                load(e, slot, WE, WD, wd_loaded)
            for e in range(RING):
                load(e, e, 0, WE, gu_loaded)
                load(e, e, WE, WD, wd_loaded)
            with sp.Fori(1, NE // RING) as r:
                for i in range(RING):
                    load_free(r * RING + i, i)
            for e in range(NE // RING * RING, NE):
                load_free(e, e % RING)

        @block.gpsimd
        def _(pool):
            def load_take(k, par, r):
                if r is not None:
                    pool.wait_ge(gathered[par], r * 16)
                pool.dma_start(take[:, par], slots(pool, k)).then_inc(take_loaded[par], 16)

            def gather(k, par, r):
                pool.wait_ge(take_loaded[par], (r + 1) * 16)
                wait_apart(pool, xt_done, (k - 1) * 2)
                pool.indirect_dma_start(xg[:, par], None, h2_d[:, :],
                                        bass.IndirectOffsetOnAxis(take[:, par, 0:1], 0)).then_inc(gathered[par], 16)
            load_take(0, 0, None)
            load_take(1, 1, None)
            gather(0, 0, 0)
            gather(1, 1, 0)
            load_take(2, 0, 1)

            def split(e, i):
                pool.wait_ge(wd_hi, e * N_D + i - N_GU + 1)
                pool.tensor_tensor(w[1][:, piece(e, i)].bitcast(F32R), w_raw[:, piece(e, i)], w[0][:, piece(e, i)],
                                   ALU.subtract).then_inc(wd_lo, 1)

            for i in range(N_GU, N_GU + N_D):
                split(0, i)

            def step(k, par, r):
                before = change(pool, k - 1) if not isinstance(k, int) or k > 0 else None
                gather(k + 2, par, r + 1)
                load_take(k + 3, 1 - par, r + 1 + par)
                if before is not None:
                    at_change(pool, before, split, range(N_GU, N_GU + N_D))
                wait(pool, added, (k - 1) * 16)
                pool.dma_start(give[:, par], slots(pool, k)).then_inc(give_loaded[par], 16)
                if not isinstance(k, int) or k > 0:
                    scatter(k - 1, 1 - par)

            def scatter(k, par):
                wait(pool, added, k * 16)
                wait_apart(pool, y_done, (k + 1) * 2)
                pool.indirect_dma_start(sum_d[:, :], bass.IndirectOffsetOnAxis(give[:, par, 0:1], 0),
                                        y[:, par], None, compute_op=ALU.add).then_inc(added, 16)
            n = iterations(pool, step)
            scatter(n * 2 - 1, 1)
            pool.wait_ge(added, n * 32)
            pool.wait_ge(gathered[0], (n + 1) * 16)
            pool.wait_ge(gathered[1], (n + 1) * 16)
            pool.wait_ge(take_loaded[0], (n + 2) * 16)

        @block.scalar
        def _(act):
            def split_gu(e, i):
                if i == 0:
                    loaded(act, e, gu_loaded)
                act.activation(w[0][:, piece(e, i)].bitcast(F32R), w_raw[:, piece(e, i)], ACT.Copy).then_inc(gu_hi, 1)

            def split_d(e, i):
                if i == N_GU:
                    loaded(act, e, wd_loaded)
                act.activation(w[0][:, piece(e, i)].bitcast(F32R), w_raw[:, piece(e, i)], ACT.Copy).then_inc(wd_hi, 1)

            def copy_xt(k, par):
                wait(act, h_done, k - 1)
                for b in range(2):
                    act.wait_ge(xt_done, k * 2 + 1 + b)
                    act.activation(x_t[0][:, par, b * 512:(b + 1) * 512].bitcast(F32R), ps_x[:, b],
                                   ACT.Copy).then_inc(xt_hi, 1)

            def copy_ht(k, par):
                act.wait_ge(ht_done, k + 1)
                wait(act, d_done, k - 1)
                act.activation(h_t[0][:, par].bitcast(F32R), ps_t[:, 0:D_EXP], ACT.Copy).then_inc(ht_hi, 1)

            def step(k, par, r):
                here = change(act, k)
                if not isinstance(k, int) or k > 0:
                    before = change(act, k - 1)
                wait_apart(act, h_done, k)
                at_change(act, here, split_gu, range(3))
                if not isinstance(k, int) or k > 0:
                    copy_ht(k - 1, 1 - par)
                    wait_apart(act, d_done, k - 1)
                    at_change(act, before, split_d, range(N_GU, N_GU + N_D))
                act.wait_ge(h_done, k + 1)
                wait(act, hg_done, k - 1)
                act.activation(th[:, par], ps_h[:, par, 0:D_EXP], ACT.Tanh, scale=0.5).then_inc(th_done, 1)
                copy_xt(k + 1, 1 - par)
                at_change(act, here, split_gu, range(3, N_GU))
            for i in range(N_GU):
                split_gu(0, i)
            for i in range(N_GU, N_GU + N_D):
                split_d(0, i)
            copy_xt(0, 0)
            n = iterations(act, step)
            copy_ht(n * 2 - 1, 1)

        @block.vector
        def _(dve):
            own = Count(dve, hs_own)

            def split(e, i):
                dve.wait_ge(gu_hi, e * N_GU + i + 1)
                dve.tensor_tensor(w[1][:, piece(e, i)].bitcast(F32R), w_raw[:, piece(e, i)], w[0][:, piece(e, i)],
                                  ALU.subtract).then_inc(gu_lo, 1)

            def copy_xt(k, par):
                wait(dve, h_done, k - 1)
                for b in range(2):
                    c = slice(b * 512, (b + 1) * 512)
                    dve.wait_ge(xt_hi, k * 2 + 1 + b)
                    dve.tensor_tensor(x_t[1][:, par, c].bitcast(F32R), ps_x[:, b], x_t[0][:, par, c],
                                      ALU.subtract).then_inc(xt_lo, 1)

            def copy_ht(k, par):
                dve.wait_ge(ht_hi, k + 1)
                wait(dve, d_done, k - 1)
                dve.tensor_tensor(h_t[1][:, par].bitcast(F32R), ps_t[:, 0:D_EXP], h_t[0][:, par],
                                  ALU.subtract).then_inc(ht_lo, 1)

            def weigh(k, par, r):
                dve.wait_ge(give_loaded[par], (r + 1) * 16)
                wait(dve, added, (k - 1) * 16)
                dve.wait_ge(d_done, k + 1)
                for i in range(2):
                    c = slice(i * 512, (i + 1) * 512)
                    dve.scalar_tensor_tensor(y[:, par, c], ps_y[:, i], give[:, par, 1:2].bitcast(F32), g2[:, c],
                                             ALU.mult, ALU.mult).then_inc(y_done, 1)

            def step(k, par, r):
                here = change(dve, k)
                at_change(dve, here, split, range(3))
                if not isinstance(k, int) or k > 0:
                    copy_ht(k - 1, 1 - par)
                dve.wait_ge(th_done, k + 1)
                wait(dve, ht_done, k - 1)
                own.base, own.n = k, 0
                own.of(dve.scalar_tensor_tensor(hg[:, par], th[:, par], 1.0, ps_h[:, par, 0:D_EXP], ALU.add, ALU.mult))
                dve.scalar_tensor_tensor(hg[:, par], hg[:, par], 0.5, ps_h[:, par, D_EXP:2 * D_EXP],
                                         ALU.mult, ALU.mult).then_inc(hg_done, 1)
                copy_xt(k + 1, 1 - par)
                at_change(dve, here, split, range(3, N_GU))
                if not isinstance(k, int) or k > 0:
                    weigh(k - 1, 1 - par, r - (1 - par))
            for i in range(N_GU):
                split(0, i)
            dve.wait_ge(g2_loaded, 16)
            copy_xt(0, 0)
            n = iterations(dve, step)
            copy_ht(n * 2 - 1, 1)
            weigh(n * 2 - 1, 1, n - 1)

        @block.tensor
        def _(pe):
            def transposes(k, par, r):
                pe.wait_ge(gathered[par], (r + 1) * 16)
                for b in range(2):
                    wait(pe, xt_lo, k * 2 - 1 + b)
                    for j in range(4):
                        c = (b * 4 + j) * P
                        last = pe.transpose(ps_x[:, b, j * P:(j + 1) * P], xg[:, par, c:c + P], ident[:])
                    last.then_inc(xt_done, 1)

            def products(out, x, w_part, w_at, chunks, stride, start=False, stop=False):
                for j in range(chunks):
                    last = pe.matmul(out, x[:, j * P:(j + 1) * P].bitcast(F32R),
                                     w_part[:, bass.ds(w_at + j * stride, 512)].bitcast(F32R),
                                     start=(start and j == 0), stop=(stop and j == chunks - 1))
                return last

            def transposes_h(k, par):
                pe.wait_ge(hg_done, k + 1)
                wait(pe, ht_lo, k)
                for j in range(2):
                    last = pe.transpose(ps_t[:, j * P:(j + 1) * P], hg[:, par, j * P:(j + 1) * P], ident[:])
                last.then_inc(ht_done, 1)

            def down(k, par, r):
                e = expert_of(pe, k)
                at = pe.snap(e % RING * W + WE)
                pe.wait_ge(ht_lo, k + 1)
                pe.wait_ge(wd_lo, (e + 1) * N_D)
                wait(pe, y_done, k * 2)
                for i in range(2):
                    products(ps_y[:, i], h_t[0][:, par], w[0], at + i * 512, 2, D, start=True)
                    products(ps_y[:, i], h_t[0][:, par], w[1], at + i * 512, 2, D)
                    last = products(ps_y[:, i], h_t[1][:, par], w[0], at + i * 512, 2, D, stop=True)
                last.then_inc(d_done, 1)

            def step(k, par, r):
                e = expert_of(pe, k)
                at = pe.snap(e % RING * W)
                pe.wait_ge(gu_hi, (e + 1) * N_GU)
                pe.wait_ge(xt_hi, (k + 1) * 2)
                wait(pe, hg_done, k - 1)
                products(ps_h[:, par], x_t[0][:, par], w[0], at, KC, 512, start=True)
                pe.wait_ge(gu_lo, (e + 1) * N_GU)
                products(ps_h[:, par], x_t[0][:, par], w[1], at, KC, 512)
                if not isinstance(k, int) or k > 0:
                    transposes_h(k - 1, 1 - par)
                pe.wait_ge(xt_lo, (k + 1) * 2)
                products(ps_h[:, par], x_t[1][:, par], w[0], at, KC, 512, stop=True).then_inc(h_done, 1)
                transposes(k + 1, 1 - par, r + par)
                if not isinstance(k, int) or k > 0:
                    down(k - 1, 1 - par, r)
            transposes(0, 0, 0)
            n = iterations(pe, step)
            transposes_h(n * 2 - 1, 1)
            down(n * 2 - 1, 1, n)


def final(nc, for_dma, io, sum_d, out):
    RING = 4
    with ExitStack() as ctx:
        def sb(name, shape, dt=F32):
            return ctx.enter_context(nc.sbuf_tensor(name, shape, dt))

        semaphores = []

        def sem(name, held_by=ctx):
            semaphores.append(held_by.enter_context(nc.semaphore(name)))
            return semaphores[-1]

        def dma_sem(name):
            return sem(name, for_dma)

        gain = sb("gain_final_row", [P, D])
        mhalf = sb("mhalf_f", [P, 1])
        x = sb("x_f", [P, RING, D])
        sq = sb("sq_f", [P, 2, D])
        ssq = sb("ssq_f", [P, RING])
        rstd = sb("rstd_f", [P, RING])
        o = sb("out_f", [P, RING, D])
        g_loaded = dma_sem("gf_loaded")
        half_set, sq_done, r_own, r_done, o_done = (
            sem(n) for n in "halff_set sqf_done rf_own rf_done of_done".split())
        x_loaded = [dma_sem(f"xf_loaded{i}") for i in range(RING)]
        stored = [dma_sem(f"f_stored{i}") for i in range(RING)]
        clear(nc, semaphores)
        block = ctx.enter_context(nc.Block())

        @block.sync
        def _(sp):
            for t in range(RING):
                sp.dma_start(x[:, t], sum_d[t * P:(t + 1) * P]).then_inc(x_loaded[t], 16)
            sp.dma_start(gain[:], io["gain_final"].broadcast_to([P, D])).then_inc(g_loaded, 16)
            with sp.Fori(1, NT // RING) as r:
                for i in range(RING):
                    t = r * RING + i
                    sp.wait_ge(o_done, t - RING + 1)
                    sp.dma_start(x[:, i], sum_d[bass.ds(t * P, P)]).then_inc(x_loaded[i], 16)

        @block.scalar
        def _(act):
            with act.Fori(0, NT // RING) as r:
                for i in range(RING):
                    t = r * RING + i
                    act.wait_ge(x_loaded[i], (r + 1) * 16)
                    act.wait_ge(r_done, r * RING)
                    act.wait_ge(sq_done, r * RING + max(i - 1, 0))
                    act.activation(sq[:, i % 2], x[:, i], ACT.Square, accum_out=ssq[:, i:i + 1]).then_inc(sq_done, 1)

        @block.gpsimd
        def _(pool):
            pool.memset(mhalf[:], -0.5).then_inc(half_set, 1)
            pool.wait_ge(half_set, 1)
            with pool.Fori(0, NT // RING) as r:
                for i in range(RING):
                    t = r * RING + i
                    c = slice(i, i + 1)
                    pool.wait_ge(o_done, r * RING)
                    wait_apart(pool, sq_done, t + 1)
                    pool.tensor_scalar(rstd[:, c], ssq[:, c], 1.0 / D, EPS, ALU.mult, ALU.add).then_inc(r_own, 1)
                    pool.wait_ge(r_own, t + 1)
                    pool.tensor_tensor(rstd[:, c], rstd[:, c], mhalf[:], ALU.pow).then_inc(r_done, 1)
                    pool.wait_ge(o_done, t + 1)
                    pool.dma_start(out[bass.ds(t * P, P)], o[:, i]).then_inc(stored[i], 16)
            for i in range(RING):
                pool.wait_ge(stored[i], 16 * NT // RING)

        @block.vector
        def _(dve):
            dve.wait_ge(g_loaded, 16)
            with dve.Fori(0, NT // RING) as r:
                for i in range(RING):
                    t = r * RING + i
                    dve.wait_ge(r_done, t + 1)
                    dve.wait_ge(stored[i], r * 16)
                    dve.scalar_tensor_tensor(o[:, i], x[:, i], rstd[:, i:i + 1], gain[:], ALU.mult, ALU.mult).then_inc(o_done, 1)


def build(nc, io, out):
    def dram(name, shape, dt=F32):
        return nc.dram_tensor(name, shape, dt).ap()

    mod_d = dram("mod_d", (2, 6 * D))
    hx_d = dram("hx_d", (NC + NT, P, D))
    yl_d = dram("yl_d", (NT, P, D_LRU))
    rec_d = dram("rec_d", (NT, P, 6 * HD))
    h2_d = dram("h2_d", (ROWS, D))
    sum_d = dram("sum_d", (ROWS, D))
    list_d = dram("list_d", (LIST * NE + TAIL * P, 2), U32)
    with ExitStack() as for_dma, ExitStack() as ctx:
        ident = ctx.enter_context(nc.sbuf_tensor("ident", [P, P], F32))
        sf = ctx.enter_context(nc.sbuf_tensor("sf_ctx", [P, HD], F32))
        blocks_row = ctx.enter_context(nc.sbuf_tensor("blocks_row", [1, 2, 2 * P], I32))
        ends_row = ctx.enter_context(nc.sbuf_tensor("ends_row", [1, NE + 1], I32))
        i_loaded = ctx.enter_context(nc.semaphore("i_loaded"))
        with nc.Block() as block:
            @block.sync
            def _(sp):
                sp.dma_start(ident[:], io["ident"]).then_inc(i_loaded, 16)
                sp.wait_ge(i_loaded, 16)
        modulation(nc, for_dma, io, mod_d, h2_d, sum_d, list_d)
        with (nc.sbuf_tensor("xa_t", [P, NCT, UW + 3], F32) as xa_t, nc.sbuf_tensor("ga_t", [P, NCT, SEQ], F32) as ga_t):
            project(nc, for_dma, io, mod_d, hx_d, xa_t, ga_t, ident)
            lru(nc, for_dma, io, xa_t, ga_t, yl_d)
        keys(nc, for_dma, io, hx_d, rec_d, sf, ident)
        mixer_out(nc, for_dma, io, mod_d, hx_d, rec_d, yl_d, h2_d, sum_d, list_d, sf, ident, blocks_row, ends_row)
        experts(nc, for_dma, io, mod_d, h2_d, sum_d, list_d, ident, blocks_row, ends_row)
        final(nc, for_dma, io, sum_d, out)


def kernel(**inputs):
    import concourse.bacc as bacc
    from concourse.bass_utils import run_bass_kernel_spmd

    nc = bacc.Bacc("TRN2", target_bir_lowering=False, num_devices=1)
    arrays, io = {}, {}
    for name, a in layout(inputs).items():
        a = np.ascontiguousarray(a)
        arrays["in_" + name] = a
        io[name] = nc.dram_tensor("in_" + name, a.shape, mybir.dt.from_np(a.dtype), kind="ExternalInput").ap()
    out = nc.dram_tensor("out_x", (SEQ, D), F32, kind="ExternalOutput").ap()
    build(nc, io, out)
    r = run_bass_kernel_spmd(nc, [arrays], core_ids=[0])
    return r.results[0]["out_x"].reshape(1, SEQ, D)
```
